# Optimizing a Trainium2 kernel written in Bass

```python
import math
import jax, jax.numpy as jnp
from jax import lax
import numpy as np

D_MODEL = 1024
BATCH = 1
SEQ = 512
DEPTH = 1

CHUNK = 64
N_META = 16
BLOCK = math.gcd(N_META, CHUNK)
N_MIXERS = 2
N_LAYERS_A = (DEPTH + N_MIXERS - 1) // N_MIXERS
N_LAYERS_B = DEPTH // N_MIXERS
EPS = 1e-6

D_FF = 2816

A_HEADS = 8
A_DK = D_MODEL // 2 // A_HEADS
A_DV = D_MODEL // A_HEADS
A_CONV = 4
A_QK = A_HEADS * A_DK
A_V = A_HEADS * A_DV
A_COLS = 2 * A_QK + 2 * A_V + 2 * A_HEADS

B_HEADS = 8
B_DK = 128
B_DV = D_MODEL // B_HEADS
B_F = B_HEADS * B_DK
B_I = B_HEADS * B_DV
B_COLS = 2 * B_F + 2 * B_I


def rmsnorm(x, g):
    xf = x.astype(jnp.float32)
    y = xf * lax.rsqrt(jnp.mean(xf * xf, axis=-1, keepdims=True) + EPS)
    return (y * g.astype(jnp.float32)).astype(x.dtype)

def swiglu(x, w_in, w_out):
    gu = x @ w_in
    return (jax.nn.silu(gu[..., :D_FF]) * gu[..., D_FF:]) @ w_out

def causal_conv(x, w, b):
    kw, c = w.shape
    y = lax.conv_general_dilated(x, w[:, None, :].astype(x.dtype), window_strides=(1,),
                                 padding=[(kw - 1, 0)], dimension_numbers=('NWC', 'WIO', 'NWC'),
                                 feature_group_count=c)
    return y + b.astype(y.dtype)

def to_blocks(x):
    bsz, t = x.shape[0], x.shape[1]
    x = x.reshape((bsz, t // BLOCK, BLOCK) + x.shape[2:])
    return jnp.swapaxes(jnp.moveaxis(x, 1, 0), 2, 3)

def from_blocks(x):
    nb, bsz, h, l, d = x.shape
    x = jnp.moveaxis(jnp.swapaxes(x, 2, 3), 0, 1)
    return x.reshape(bsz, nb * l, h * d)

def mlstm_scan(q, k, v, ig, lf):
    _, bsz, nh, l, dk = q.shape
    dv = v.shape[-1]
    causal = jnp.tril(jnp.ones((l, l), dtype=bool))

    def step(carry, xs):
        c_prev, n_prev, m_prev = carry
        qb, kb, vb, ib, fb = xs
        bcum = jnp.cumsum(fb, axis=-1)
        dmat = jnp.where(causal, bcum[..., :, None] - bcum[..., None, :] + ib[..., None, :], -jnp.inf)
        g_inter = bcum + m_prev[..., None]
        m = jnp.maximum(g_inter, jnp.max(dmat, axis=-1))
        w_intra = jnp.exp(dmat - m[..., None])
        w_inter = jnp.exp(g_inter - m)
        s = jnp.einsum('bhld,bhsd->bhls', qb, kb) * w_intra
        num = jnp.einsum('bhls,bhsv->bhlv', s, vb) + w_inter[..., None] * jnp.einsum('bhvd,bhld->bhlv', c_prev, qb)
        den = jnp.sum(s, axis=-1) + w_inter * jnp.einsum('bhd,bhld->bhl', n_prev, qb)
        hb = num / jnp.maximum(jnp.abs(den), jnp.exp(-m))[..., None]
        b_last = bcum[..., -1]
        g_state = b_last[..., None] - bcum + ib
        m_new = jnp.maximum(b_last + m_prev, jnp.max(g_state, axis=-1))
        w_s = jnp.exp(g_state - m_new[..., None])
        decay = jnp.exp(b_last + m_prev - m_new)
        c_new = decay[..., None, None] * c_prev + jnp.einsum('bhsv,bhsd->bhvd', vb * w_s[..., None], kb)
        n_new = decay[..., None] * n_prev + jnp.einsum('bhs,bhsd->bhd', w_s, kb)
        return (c_new, n_new, m_new), hb

    init = (jnp.zeros((bsz, nh, dv, dk), jnp.float32), jnp.zeros((bsz, nh, dk), jnp.float32),
            jnp.zeros((bsz, nh), jnp.float32))
    _, hs = lax.scan(step, init, (q, k, v, ig, lf))
    return hs

def hgrn2_scan(q, k, v, lf):
    _, bsz, nh, l, dk = q.shape
    dv = v.shape[-1]
    causal = jnp.tril(jnp.ones((l, l), dtype=bool))

    def step(s_prev, xs):
        qb, kb, vb, fb = xs
        bcum = jnp.cumsum(fb, axis=-2)
        rel = jnp.where(causal[:, :, None], bcum[..., :, None, :] - bcum[..., None, :, :], -jnp.inf)
        a = jnp.sum(qb[..., :, None, :] * jnp.exp(rel) * kb[..., None, :, :], axis=-1)
        o = jnp.einsum('bhls,bhsv->bhlv', a, vb) + jnp.einsum('bhld,bhdv->bhlv', qb * jnp.exp(bcum), s_prev)
        b_last = bcum[..., -1, :]
        s_new = jnp.exp(b_last)[..., None] * s_prev + jnp.einsum(
            'bhsd,bhsv->bhdv', kb * jnp.exp(b_last[..., None, :] - bcum), vb)
        return s_new, o

    _, os_ = lax.scan(step, jnp.zeros((bsz, nh, dk, dv), jnp.float32), (q, k, v, lf))
    return os_

def mlstm_mixer(u, w_in, conv_w, conv_b, gate_b, w_out):
    bsz, t, _ = u.shape
    z = u @ w_in
    qk = jax.nn.silu(causal_conv(z[..., :2 * A_QK], conv_w, conv_b))
    v = z[..., 2 * A_QK:2 * A_QK + A_V]
    og = z[..., 2 * A_QK + A_V:2 * A_QK + 2 * A_V]
    gates = z[..., 2 * A_QK + 2 * A_V:].astype(jnp.float32) + gate_b.astype(jnp.float32)
    q = qk[..., :A_QK].reshape(bsz, t, A_HEADS, A_DK).astype(jnp.float32) * (A_DK ** -0.5)
    k = qk[..., A_QK:].reshape(bsz, t, A_HEADS, A_DK).astype(jnp.float32)
    v = v.reshape(bsz, t, A_HEADS, A_DV).astype(jnp.float32)
    ig = gates[..., :A_HEADS]
    lf = jax.nn.log_sigmoid(gates[..., A_HEADS:])
    hs = mlstm_scan(to_blocks(q), to_blocks(k), to_blocks(v), to_blocks(ig), to_blocks(lf))
    y = from_blocks(hs).astype(u.dtype) * jax.nn.sigmoid(og)
    return y @ w_out

def hgrn2_mixer(u, w_in, f_bias, lower_bound, g_norm, w_out):
    bsz, t, _ = u.shape
    z = u @ w_in
    q = jax.nn.silu(z[..., :B_F])
    fpre = z[..., B_F:2 * B_F].astype(jnp.float32) + f_bias.astype(jnp.float32)
    i_in = z[..., 2 * B_F:2 * B_F + B_I]
    g = z[..., 2 * B_F + B_I:]
    lf = jnp.logaddexp(jnp.log(lower_bound), jnp.log1p(-lower_bound) + jax.nn.log_sigmoid(fpre))
    k = (1.0 - lower_bound) * jax.nn.sigmoid(-fpre)
    q = q.reshape(bsz, t, B_HEADS, B_DK).astype(jnp.float32)
    k = k.reshape(bsz, t, B_HEADS, B_DK)
    lf = lf.reshape(bsz, t, B_HEADS, B_DK)
    v = i_in.reshape(bsz, t, B_HEADS, B_DV).astype(jnp.float32)
    o = hgrn2_scan(to_blocks(q), to_blocks(k), to_blocks(v), to_blocks(lf))
    y = from_blocks(o).astype(u.dtype) * jax.nn.sigmoid(g)
    return rmsnorm(y, g_norm) @ w_out

def first_inputs(seed: int = 0) -> dict:
    key = jax.random.key(seed)
    ks = jax.random.split(key, 16)
    f32 = jnp.float32
    x = jax.random.normal(ks[0], (BATCH, SEQ, D_MODEL), f32)
    meta_tokens = jax.random.normal(ks[1], (N_META, D_MODEL), f32)
    norm_gains = 1.0 + 0.1 * jax.random.normal(ks[2], (DEPTH, 6, D_MODEL), f32)
    ffn_w_in = jax.random.normal(ks[3], (DEPTH, 2, D_MODEL, 2 * D_FF), f32) * D_MODEL ** -0.5
    ffn_w_out = jax.random.normal(ks[4], (DEPTH, 2, D_FF, D_MODEL), f32) * D_FF ** -0.5
    a_w_in = jax.random.normal(ks[5], (N_LAYERS_A, D_MODEL, A_COLS), f32) * D_MODEL ** -0.5
    a_conv_w = jax.random.normal(ks[6], (N_LAYERS_A, A_CONV, 2 * A_QK), f32) * A_CONV ** -0.5
    a_conv_b = 0.01 * jax.random.normal(ks[7], (N_LAYERS_A, 2 * A_QK), f32)
    i_bias = 0.1 * jax.random.normal(ks[8], (N_LAYERS_A, A_HEADS), f32)
    f_bias_a = jnp.linspace(3.0, 6.0, A_HEADS, dtype=f32)[None, :] + 0.1 * jax.random.normal(ks[9], (N_LAYERS_A, A_HEADS), f32)
    a_gate_b = jnp.concatenate([i_bias, f_bias_a], axis=-1)
    a_w_out = jax.random.normal(ks[10], (N_LAYERS_A, A_V, D_MODEL), f32) * A_V ** -0.5
    b_w_in = jax.random.normal(ks[11], (N_LAYERS_B, D_MODEL, B_COLS), f32) * D_MODEL ** -0.5
    b_f_bias = 0.1 * jax.random.normal(ks[12], (N_LAYERS_B, B_F), f32)
    b_lb_raw = 0.5 * jax.random.normal(ks[13], (DEPTH, B_F), f32)
    b_g_norm = 1.0 + 0.1 * jax.random.normal(ks[14], (N_LAYERS_B, B_I), f32)
    b_w_out = jax.random.normal(ks[15], (N_LAYERS_B, B_I, D_MODEL), f32) * B_I ** -0.5
    return {'x': x, 'meta_tokens': meta_tokens, 'norm_gains': norm_gains, 'ffn_w_in': ffn_w_in,
            'ffn_w_out': ffn_w_out, 'a_w_in': a_w_in, 'a_conv_w': a_conv_w, 'a_conv_b': a_conv_b,
            'a_gate_b': a_gate_b, 'a_w_out': a_w_out, 'b_w_in': b_w_in, 'b_f_bias': b_f_bias,
            'b_lb_raw': b_lb_raw, 'b_g_norm': b_g_norm, 'b_w_out': b_w_out}

def first_block(x, meta_tokens, norm_gains, ffn_w_in, ffn_w_out, a_w_in, a_conv_w, a_conv_b, a_gate_b,
              a_w_out, b_w_in, b_f_bias, b_lb_raw, b_g_norm, b_w_out):
    bsz = x.shape[0]
    meta = jnp.broadcast_to(meta_tokens[None].astype(x.dtype), (bsz, N_META, D_MODEL))
    h = jnp.concatenate([meta, x], axis=1)
    sm = jax.nn.softmax(b_lb_raw.astype(jnp.float32), axis=0)
    lb_all = jnp.cumsum(sm, axis=0) - sm[0]
    for i in range(DEPTH):
        gn = norm_gains[i]
        h = h + 0.5 * rmsnorm(swiglu(rmsnorm(h, gn[0]), ffn_w_in[i, 0], ffn_w_out[i, 0]), gn[1])
        u = rmsnorm(h, gn[2])
        j = i // N_MIXERS
        if i % N_MIXERS == 0:
            y = mlstm_mixer(u, a_w_in[j], a_conv_w[j], a_conv_b[j], a_gate_b[j], a_w_out[j])
        else:
            y = hgrn2_mixer(u, b_w_in[j], b_f_bias[j], lb_all[i], b_g_norm[j], b_w_out[j])
        h = h + rmsnorm(y, gn[3])
        h = h + 0.5 * rmsnorm(swiglu(rmsnorm(h, gn[4]), ffn_w_in[i, 1], ffn_w_out[i, 1]), gn[5])
    return h[:, N_META:]


MLA_HEADS = 8
Q_LORA_RANK = 256
KV_LORA_RANK = 128
QK_NOPE_DIM = 64
QK_ROPE_DIM = 32
V_HEAD_DIM = 64
MLA_SCALE = (QK_NOPE_DIM + QK_ROPE_DIM) ** -0.5
Q_BLOCK = 128

RET_HEADS = 8
RET_HEAD_DIM = 64
RET_CHUNK = 128

D_MIX = MLA_HEADS * V_HEAD_DIM + RET_HEADS * RET_HEAD_DIM
ROPE_THETA = 10000.0

IN_SIZES = (Q_LORA_RANK, KV_LORA_RANK, QK_ROPE_DIM,
            RET_HEADS * RET_HEAD_DIM, RET_HEADS * RET_HEAD_DIM,
            RET_HEADS * RET_HEAD_DIM, RET_HEADS * RET_HEAD_DIM)
D_IN = sum(IN_SIZES)
SPLIT_POINTS = tuple(int(s) for s in np.cumsum(IN_SIZES)[:-1])


def rms_norm(x, g):
    xf = x.astype(jnp.float32)
    y = xf * lax.rsqrt(jnp.mean(xf * xf, axis=-1, keepdims=True) + EPS)
    return (y * g.astype(jnp.float32)).astype(x.dtype)

def swiglu_2(x, w_gate, w_up, w_down):
    return (jax.nn.silu(x @ w_gate) * (x @ w_up)) @ w_down

def rope(x, pos_f):
    half = x.shape[-1] // 2
    inv = ROPE_THETA ** (-jnp.arange(half, dtype=jnp.float32) / half)
    ang = pos_f[..., None] * inv
    cos = jnp.cos(ang)[:, :, None, :]
    sin = jnp.sin(ang)[:, :, None, :]
    x1 = x[..., :half].astype(jnp.float32)
    x2 = x[..., half:].astype(jnp.float32)
    return jnp.concatenate([x1 * cos - x2 * sin, x1 * sin + x2 * cos], axis=-1).astype(x.dtype)

def mla_group(c_q, c_kv, k_pe_raw, pos_f, q_norm, w_uq, kv_norm, w_ukv):
    B, S, _ = c_q.shape
    H = MLA_HEADS
    q = (rms_norm(c_q, q_norm) @ w_uq).reshape(B, S, H, QK_NOPE_DIM + QK_ROPE_DIM)
    q_nope = q[..., :QK_NOPE_DIM]
    q_pe = rope(q[..., QK_NOPE_DIM:], pos_f)
    kv = (rms_norm(c_kv, kv_norm) @ w_ukv).reshape(B, S, H, QK_NOPE_DIM + V_HEAD_DIM)
    k_nope = kv[..., :QK_NOPE_DIM]
    v = kv[..., QK_NOPE_DIM:]
    k_pe = rope(k_pe_raw[:, :, None, :], pos_f)[:, :, 0]
    nb = S // Q_BLOCK

    def block(args):
        qn, qp = args
        s = (jnp.einsum('bqhd,bkhd->bhqk', qn, k_nope).astype(jnp.float32)
             + jnp.einsum('bqhr,bkr->bhqk', qp, k_pe).astype(jnp.float32))
        p = jax.nn.softmax(s * MLA_SCALE, axis=-1)
        return jnp.einsum('bhqk,bkhd->bqhd', p.astype(v.dtype), v)

    qn_b = q_nope.reshape(B, nb, Q_BLOCK, H, QK_NOPE_DIM).swapaxes(0, 1)
    qp_b = q_pe.reshape(B, nb, Q_BLOCK, H, QK_ROPE_DIM).swapaxes(0, 1)
    out = lax.map(block, (qn_b, qp_b))
    return out.swapaxes(0, 1).reshape(B, S, H * V_HEAD_DIM)

def retention_scan(q, k, v, log_gamma, inclusive):
    B, S, H, d = q.shape
    C = RET_CHUNK
    nc = S // C
    idx = jnp.arange(C, dtype=jnp.float32)
    rel = idx[:, None] - idx[None, :]
    mask = (rel >= 0) if inclusive else (rel > 0)
    d_inner = jnp.where(mask[None], jnp.exp(log_gamma[:, None, None] * jnp.maximum(rel, 0.0)[None]), 0.0)
    q_dec = jnp.exp(log_gamma[None, :] * (idx[:, None] + 1.0))
    k_dec = jnp.exp(log_gamma[None, :] * (C - 1.0 - idx)[:, None])
    c_dec = jnp.exp(log_gamma * C)

    def to_chunks(t):
        return t.reshape(B, nc, C, H, d).swapaxes(0, 1)

    def step(state, inp):
        qc, kc, vc = inp
        s = jnp.einsum('bihd,bjhd->bhij', qc, kc) * d_inner
        inner = jnp.einsum('bhij,bjhe->bihe', s, vc)
        cross = jnp.einsum('bihd,bhde->bihe', qc * q_dec[None, :, :, None], state)
        state = (state * c_dec[None, :, None, None]
                 + jnp.einsum('bjhd,bjhe->bhde', kc * k_dec[None, :, :, None], vc))
        return state, inner + cross

    state0 = jnp.zeros((B, H, d, d), jnp.float32)
    _, out = lax.scan(step, state0, (to_chunks(q), to_chunks(k), to_chunks(v)))
    return out.swapaxes(0, 1).reshape(B, S, H, d)

def retention_group(r_q, r_k, r_v, r_g, pos_f, decay_fwd, decay_bwd):
    B, S, _ = r_q.shape
    shp = (B, S, RET_HEADS, RET_HEAD_DIM)
    q = rope(r_q.reshape(shp), pos_f).astype(jnp.float32)
    k = rope(r_k.reshape(shp), pos_f).astype(jnp.float32) * (RET_HEAD_DIM ** -0.5)
    v = r_v.reshape(shp).astype(jnp.float32)
    lg_f = jax.nn.log_sigmoid(decay_fwd.astype(jnp.float32))
    lg_b = jax.nn.log_sigmoid(decay_bwd.astype(jnp.float32))
    fwd = retention_scan(q, k, v, lg_f, True)
    bwd = jnp.flip(retention_scan(jnp.flip(q, 1), jnp.flip(k, 1), jnp.flip(v, 1), lg_b, False), 1)
    o = fwd + bwd
    mu = jnp.mean(o, axis=-1, keepdims=True)
    var = jnp.mean(jnp.square(o - mu), axis=-1, keepdims=True)
    o = ((o - mu) * lax.rsqrt(var + EPS)).reshape(B, S, RET_HEADS * RET_HEAD_DIM)
    return (jax.nn.silu(r_g.astype(jnp.float32)) * o).astype(r_q.dtype)

def second_inputs(seed: int = 0) -> dict:
    key = jax.random.key(seed)
    ks = jax.random.split(key, 24)
    f32 = jnp.float32

    def w(k, shape, fan_in):
        return jax.random.normal(k, shape, f32) * (fan_in ** -0.5)

    def gain(k, shape):
        return 1.0 + 0.02 * jax.random.normal(k, shape, f32)

    L = DEPTH
    offset = jax.random.randint(ks[1], (BATCH, 1), 0, 4096, dtype=jnp.int32)
    positions = offset + jnp.arange(SEQ, dtype=jnp.int32)[None, :]
    decay_init = jnp.asarray(np.log(2.0 ** (5.0 + np.arange(RET_HEADS)) - 1.0), f32)
    return {
        "x": jax.random.normal(ks[0], (BATCH, SEQ, D_MODEL), f32),
        "positions": positions,
        "ffn1_norm": gain(ks[2], (L, D_MODEL)),
        "ffn1_w_gate": w(ks[3], (L, D_MODEL, D_FF), D_MODEL),
        "ffn1_w_up": w(ks[4], (L, D_MODEL, D_FF), D_MODEL),
        "ffn1_w_down": w(ks[5], (L, D_FF, D_MODEL), D_FF),
        "mix_norm": gain(ks[6], (L, D_MODEL)),
        "w_in": w(ks[7], (L, D_MODEL, D_IN), D_MODEL),
        "q_norm": gain(ks[8], (L, Q_LORA_RANK)),
        "w_uq": w(ks[9], (L, Q_LORA_RANK, MLA_HEADS * (QK_NOPE_DIM + QK_ROPE_DIM)), Q_LORA_RANK),
        "kv_norm": gain(ks[10], (L, KV_LORA_RANK)),
        "w_ukv": w(ks[11], (L, KV_LORA_RANK, MLA_HEADS * (QK_NOPE_DIM + V_HEAD_DIM)), KV_LORA_RANK),
        "ret_decay_fwd": decay_init[None, :] + 0.05 * jax.random.normal(ks[12], (L, RET_HEADS), f32),
        "ret_decay_bwd": decay_init[None, :] + 0.05 * jax.random.normal(ks[13], (L, RET_HEADS), f32),
        "w_o": w(ks[14], (L, D_MIX, D_MODEL), D_MIX),
        "ffn2_norm": gain(ks[15], (L, D_MODEL)),
        "ffn2_w_gate": w(ks[16], (L, D_MODEL, D_FF), D_MODEL),
        "ffn2_w_up": w(ks[17], (L, D_MODEL, D_FF), D_MODEL),
        "ffn2_w_down": w(ks[18], (L, D_FF, D_MODEL), D_FF),
        "final_norm": gain(ks[19], (D_MODEL,)),
    }

def second_block(x, positions, ffn1_norm, ffn1_w_gate, ffn1_w_up, ffn1_w_down, mix_norm, w_in,
              q_norm, w_uq, kv_norm, w_ukv, ret_decay_fwd, ret_decay_bwd, w_o,
              ffn2_norm, ffn2_w_gate, ffn2_w_up, ffn2_w_down, final_norm):
    pos_f = positions.astype(jnp.float32)
    h = x
    for l in range(DEPTH):
        h = h + 0.5 * swiglu_2(rms_norm(h, ffn1_norm[l]), ffn1_w_gate[l], ffn1_w_up[l], ffn1_w_down[l])
        n = rms_norm(h, mix_norm[l])
        proj = n @ w_in[l]
        c_q, c_kv, k_pe, r_q, r_k, r_v, r_g = jnp.split(proj, SPLIT_POINTS, axis=-1)
        a = mla_group(c_q, c_kv, k_pe, pos_f, q_norm[l], w_uq[l], kv_norm[l], w_ukv[l])
        r = retention_group(r_q, r_k, r_v, r_g, pos_f, ret_decay_fwd[l], ret_decay_bwd[l])
        h = h + jnp.concatenate([a, r], axis=-1) @ w_o[l]
        h = h + 0.5 * swiglu_2(rms_norm(h, ffn2_norm[l]), ffn2_w_gate[l], ffn2_w_up[l], ffn2_w_down[l])
    return rms_norm(h, final_norm)


def setup_inputs(seed=0):
    out = dict(first_inputs(seed))
    for name, value in second_inputs(seed + 1).items():
        if name != "x":
            out[name + "_2"] = value
    return out


def reference(
    x, meta_tokens, norm_gains, ffn_w_in, ffn_w_out, a_w_in, a_conv_w, a_conv_b, a_gate_b,
    a_w_out, b_w_in, b_f_bias, b_lb_raw, b_g_norm, b_w_out, positions_2, ffn1_norm_2,
    ffn1_w_gate_2, ffn1_w_up_2, ffn1_w_down_2, mix_norm_2, w_in_2, q_norm_2, w_uq_2, kv_norm_2,
    w_ukv_2, ret_decay_fwd_2, ret_decay_bwd_2, w_o_2, ffn2_norm_2, ffn2_w_gate_2, ffn2_w_up_2,
    ffn2_w_down_2, final_norm_2,
):
    x = first_block(
        x, meta_tokens, norm_gains, ffn_w_in, ffn_w_out, a_w_in, a_conv_w, a_conv_b, a_gate_b,
        a_w_out, b_w_in, b_f_bias, b_lb_raw, b_g_norm, b_w_out,
    )
    return second_block(
        x, positions_2, ffn1_norm_2, ffn1_w_gate_2, ffn1_w_up_2, ffn1_w_down_2, mix_norm_2,
        w_in_2, q_norm_2, w_uq_2, kv_norm_2, w_ukv_2, ret_decay_fwd_2, ret_decay_bwd_2, w_o_2,
        ffn2_norm_2, ffn2_w_gate_2, ffn2_w_up_2, ffn2_w_down_2, final_norm_2,
    )


_drawn_inputs = setup_inputs


def setup_inputs(seed=0):
    import zlib

    import numpy as np

    out = dict(_drawn_inputs(seed))
    spreads = {}
    factors = {'a_conv_b': 3.867,
     'ffn1_norm_2': 8.0,
     'mix_norm_2': 5.395,
     'q_norm_2': 8.0,
     'kv_norm_2': 8.0,
     'ffn2_norm_2': 23.261}
    for name, (base, spread) in spreads.items():
        noise = np.random.default_rng([zlib.crc32(name.encode()), seed]).standard_normal(out[name].shape)
        drawn = base * np.exp(spread * noise) if base else spread * noise
        out[name] = __import__('jax').numpy.asarray(drawn.astype(out[name].dtype))
    for name, factor in factors.items():
        out[name] = (out[name] * factor).astype(out[name].dtype)
    return out
```

```python
from contextlib import ExitStack

import numpy as np

import concourse.bass as bass
from concourse import mybir

F32 = mybir.dt.float32
F32R = mybir.dt.float32r
I32 = mybir.dt.int32
ACT = mybir.ActivationFunctionType
ALU = mybir.AluOpType
AX_X = mybir.AxisListType.X

P = 128
D = 1024
KD = D // P
META = 16
SEQ = 512
TOK = META + SEQ
HALF = TOK // 2
DFF = 2816
KF = DFF // P
EPS = 1e-6
CH = SEQ // P

HEADS = 8
A_DK = 64
A_QK = HEADS * A_DK
A_V = D
CONV = 4

Q_RANK, KV_RANK, ROPE_DIM, NOPE, V_DIM = 256, 128, 32, 64, 64
QK_DIM = NOPE + ROPE_DIM
MLA_SCALE = QK_DIM ** -0.5
RET_DIM = 64
RET = HEADS * RET_DIM
ROPE_THETA = 10000.0
WIN = SEQ + SEQ - P

SLOTS = 4
UNIT = 1024
STARTED = 1
AHEAD = SLOTS - 1

VEC_ROWS = [("norm_gains", 48), ("ffn1_norm_2", 8), ("mix_norm_2", 8), ("ffn2_norm_2", 8), ("final_norm_2", 8),
            ("q_norm_2", 2), ("kv_norm_2", 1), ("a_conv_b", 8), ("a_conv_w", 32)]
VEC = {}
_n = 0
for _name, _rows in VEC_ROWS:
    VEC[_name] = _n
    _n += _rows
NVEC = _n

CONST = {}
_n = 0
for _name, _cols in [("ident", P), ("ones", P), ("tri", P), ("selrow", HEADS * P), ("selcol", HEADS * HEADS),
                     ("perm", P), ("permpe", QK_DIM), ("block", P), ("invf", 2), ("relpos", WIN), ("relneg", WIN)]:
    CONST[_name] = slice(_n, _n + _cols)
    _n += _cols
NCONST = _n


def constants():
    c = np.zeros((P, NCONST), np.float32)
    p = np.arange(P)
    c[:, CONST["ident"]] = np.eye(P)
    c[:, CONST["ones"]] = 1.0
    c[:, CONST["tri"]] = p[None, :] >= p[:, None]
    for h in range(HEADS):
        c[h, CONST["selrow"].start + h * P:CONST["selrow"].start + (h + 1) * P] = 1.0
        c[:, CONST["selcol"].start + h * HEADS + h] = 1.0

    def swap(name, rows, half):
        for m in rows:
            first = (m % (2 * half)) < half
            c[m + half if first else m - half, CONST[name].start + m] = -1.0 if first else 1.0

    swap("perm", range(P), RET_DIM // 2)
    swap("permpe", range(NOPE, QK_DIM), ROPE_DIM // 2)
    for b in range(P // RET_DIM):
        rows = slice(b * RET_DIM, (b + 1) * RET_DIM)
        c[rows, CONST["block"].start + b * RET_DIM:CONST["block"].start + (b + 1) * RET_DIM] = 1.0 / RET_DIM

    def inv(half):
        return (np.float32(ROPE_THETA) ** (-np.arange(half, dtype=np.float32) / np.float32(half))).astype(np.float32)

    c[NOPE:QK_DIM, CONST["invf"].start] = np.tile(inv(ROPE_DIM // 2), 2)
    c[:, CONST["invf"].start + 1] = np.tile(inv(RET_DIM // 2), P // (RET_DIM // 2))
    rel = np.arange(WIN)[None, :] - (SEQ - P) - p[:, None]
    c[:, CONST["relpos"]] = np.maximum(rel, 0)
    c[:, CONST["relneg"]] = np.maximum(-rel, 0)
    return c


def program(nc, dram, out, stop=99):
    ctx = ExitStack()

    def sb(name, shape, dt=F32):
        return ctx.enter_context(nc.sbuf_tensor(name, shape, dt))

    def region(tensors):
        with ExitStack() as r:
            return {n: r.enter_context(nc.sbuf_tensor(n, s, dt)) for n, s, dt in tensors}

    def region_parts(first, parts):
        with ExitStack() as r:
            common = {n: r.enter_context(nc.sbuf_tensor(n, s, dt)) for n, s, dt in first}
            return [{**common, **region(part)} for part in parts]

    def sems(stage, names):
        return {n: ctx.enter_context(nc.semaphore(f"{stage}_{n}")) for n in names}

    hT = sb("hT", [P, KD * TOK])
    raw = sb("raw", [P, SLOTS, UNIT])
    whi = sb("whi", [P, SLOTS, UNIT], F32R)
    wlo = sb("wlo", [P, SLOTS, UNIT], F32R)
    wa = sb("wa", [P, 2 * TOK])
    wb = sb("wb", [P, 2 * TOK])
    sq = sb("sq", [P, 2 * TOK])
    acc = sb("acc", [P, TOK])
    rbc = sb("rbc", [P, TOK])
    vec = sb("vec", [P, NVEC])
    ident = sb("ident", [P, P])
    ones = sb("ones", [P, P])
    eps = sb("eps", [P, 1])
    halfpi = sb("halfpi", [P, 1])
    cell = sb("cell", [P, 1])
    small = sb("small", [P, 32])
    gateb = sb("gateb", [HEADS, 2])
    with ExitStack() as r:
        ybuf = r.enter_context(nc.sbuf_tensor("ybuf", [P, KD * TOK], F32))
    xhi = sb("xhi", [P, KD * TOK], F32R)
    xlo = sb("xlo", [P, KD * TOK], F32R)
    t = region([("x_tok", [P, CH, D], F32), ("meta_tok", [META, D], F32), ("vrows", [NVEC, P], F32)])
    x_tok, meta_tok, vrows = t["x_tok"], t["meta_tok"], t["vrows"]
    t = region([("hid_hi", [P, KF * TOK], F32R), ("hid_lo", [P, KF * TOK], F32R)])
    hid_hi, hid_lo = t["hid_hi"], t["hid_lo"]
    EW = [SEQ] + [SEQ - P * c for c in range(CH)]
    EO = [sum(EW[:j]) for j in range(len(EW))]
    m1 = region([("qkT", [P, KD * TOK], F32), ("v_real", [P, CH, D], F32), ("v_meta", [META, D], F32),
                 ("og", [P, KD, SEQ], F32), ("num", [P, KD * TOK], F32), ("E", [P, 2 * sum(EW)], F32),
                 ("tri", [P, P], F32), ("selrow", [HEADS, HEADS * P], F32),
                 ("selcol", [P, HEADS * HEADS], F32), ("acol", [P, (CH + 1) * HEADS], F32)])
    shared = [("cq", [P, 2, SEQ], F32), ("cq_hi", [P, 2, SEQ], F32R), ("cq_lo", [P, 2, SEQ], F32R),
              ("ckv", [P, SEQ], F32), ("ckv_hi", [P, SEQ], F32R), ("ckv_lo", [P, SEQ], F32R),
              ("cosm", [P, SEQ], F32), ("sinm", [P, SEQ], F32), ("kpe", [P, SEQ], F32),
              ("permpe", [P, QK_DIM], F32)]
    m2, m3 = region_parts(shared, [[("cosr", [P, SEQ], F32), ("sinr", [P, SEQ], F32), ("perm", [P, P], F32),
                          ("block", [P, P], F32), ("invf", [P, 2], F32), ("lg", [P, 2 * HEADS], F32),
                          ("lgt", [P, 2 * HEADS], F32),
                          ("rq", [P, 4, SEQ], F32), ("rk", [P, 4, SEQ], F32), ("rv", [P, CH, RET], F32),
                          ("rg", [P, 4, SEQ], F32), ("relpos", [P, WIN], F32), ("relneg", [P, WIN], F32),
                          ("dec", [P, WIN], F32), ("RS", [P, CH, SEQ], F32)], [("qT", [QK_DIM, HEADS, SEQ], F32), ("kT", [QK_DIM, HEADS, SEQ], F32),
                          ("vm", [P, CH, RET], F32), ("PR", [P, CH * SEQ], F32), ("PT", [P, CH * SEQ], F32)]])
    fin = region([("fin", [P, KD, SEQ], F32), ("otok", [P, CH, D], F32)])
    ps = ctx.enter_context(nc.psum_tensor("ps", [P, 8, 512], F32))

    def cols(n):
        return (0, TOK) if n == TOK else (META, SEQ)

    def tile(buf, k, n, start=0):
        o, w = cols(n)
        ap = buf[:, bass.ds(k * TOK + o, w)]
        return ap.rearrange("p (a n) -> p a n", a=2) if n == TOK else ap

    def bank(b, n, rows=P):
        return ps[0:rows, b:b + 2, 0:HALF] if n == TOK else ps[0:rows, b, :]

    def pieces(b, n):
        if n == TOK:
            return [(ps[:, b + c, 0:HALF], HALF * c, HALF) for c in range(2)]
        return [(ps[:, b, :], META, SEQ)]

    def gain(name, k):
        return vec[:, VEC[name] + k:VEC[name] + k + 1]

    def kcols(w, c0, n, k0=0, kn=KD):
        return w[k0 * P:(k0 + kn) * P, c0:c0 + n].rearrange("(k p) n -> p k n", p=P)

    FFN_PIECES = [(0, 8), (8, 8), (16, KF - 16)]
    NU_UP, NU_DOWN = 2 * KF, KD * len(FFN_PIECES)
    NU_FFN = NU_UP + NU_DOWN
    w1, w2 = dram["a_w_in"][0], dram["w_in_2"][0]
    VCOL = 2 * A_QK
    OCOL = VCOL + A_V
    GCOL = OCOL + A_V
    units1 = [kcols(w1, m * P, P) for m in range(8)] + [kcols(w1, GCOL, 2 * HEADS)]
    units1 += [kcols(w1, VCOL + 512 * n, 512, 2 * j, 2) for n in range(2) for j in range(4)]
    units1 += [kcols(w1, OCOL + m * P, P) for m in range(8)]
    units1 += [kcols(dram["a_w_out"][0], m * P, P) for m in range(8)]
    c_kv, c_kpe = Q_RANK, Q_RANK + KV_RANK
    c_rq = c_kpe + ROPE_DIM
    c_rk, c_rv, c_rg = c_rq + RET, c_rq + 2 * RET, c_rq + 3 * RET
    units2 = [kcols(w2, m * P, P) for m in range(2)] + [kcols(w2, c_kv, P), kcols(w2, c_kpe, ROPE_DIM)]
    units2 += [kcols(w2, c + m * P, P) for c in (c_rq, c_rk) for m in range(4)]
    units2 += [kcols(w2, c_rv, 512, 2 * j, 2) for j in range(4)]
    units2 += [kcols(w2, c_rg + m * P, P) for m in range(4)]
    units2 += [kcols(dram["w_uq_2"][0], 384 * j, 384, 0, 2) for j in range(2)]
    units2 += [kcols(dram["w_ukv_2"][0], 0, 1024, 0, 1)]
    units2 += [kcols(dram["w_o_2"][0], m * P, P) for m in range(8)]
    f_in, f_out = dram["ffn_w_in"][0], dram["ffn_w_out"][0]
    FFNS = [
        dict(gate=f_in[0], gc=0, up=f_in[0], uc=DFF, down=f_out[0], n=TOK, norm=("norm_gains", 0), post=8),
        dict(gate=f_in[1], gc=0, up=f_in[1], uc=DFF, down=f_out[1], n=SEQ, norm=("norm_gains", 32), post=40),
        dict(gate=dram["ffn1_w_gate_2"][0], gc=0, up=dram["ffn1_w_up_2"][0], uc=0, down=dram["ffn1_w_down_2"][0],
             n=SEQ, norm=("ffn1_norm_2", 0), post=None),
        dict(gate=dram["ffn2_w_gate_2"][0], gc=0, up=dram["ffn2_w_up_2"][0], uc=0, down=dram["ffn2_w_down_2"][0],
             n=SEQ, norm=("ffn2_norm_2", 0), post=None),
    ]
    U_M1 = NU_FFN
    FFNS[0]["u0"] = 0
    FFNS[1]["u0"] = U_M1 + len(units1)
    FFNS[2]["u0"] = FFNS[1]["u0"] + NU_FFN
    U_M2 = FFNS[2]["u0"] + NU_FFN
    FFNS[3]["u0"] = U_M2 + len(units2)
    UNITS = FFNS[3]["u0"] + NU_FFN
    assert UNITS % SLOTS == 0

    raw_loaded = [ctx.enter_context(nc.semaphore(f"raw_loaded{s}")) for s in range(SLOTS)]
    hi_done, lo_done, unit_done, unused = (ctx.enter_context(nc.semaphore(n))
                                           for n in ("hi_done", "lo_done", "unit_done", "unused"))

    def slot_view(buf, u, a, n):
        return buf[:, u % SLOTS, 0:a * n].rearrange("p (a n) -> p a n", a=a)

    init = sems("init", ["x0", "x1", "x2", "x3", "meta", "vecs", "const", "turned", "h_ready", "eps"])
    NORM = ["sq_ready", "sq_used", "root_ready", "recip", "t_ready", "hi_ready", "x_ready"]
    OUTP = ["v_ready", "sq_ready", "acc_done"]
    norm_s, out_s = sems("norm", NORM), sems("out", OUTP)
    res_s = sems("res", ["stat", "root_ready", "recip", "t_ready", "h_ready"])
    ffn_s = sems("ffn", ["silu_done", "banks_free", "hi_ready", "hid_ready"])
    norm_at = [dict(sq_ready=KD * min(i, 4), sq_used=KD * min(i, 4) + max(i - 4, 0), root_ready=i, recip=i,
                    t_ready=KD * i, hi_ready=KD * i, x_ready=KD * i) for i in range(7)]
    out_at = [dict(v_ready=(KD + 2) * i, sq_ready=KD * i, acc_done=(KD + 2) * i) for i in range(6)]
    res_at = [dict(stat=i, root_ready=i, recip=i, t_ready=KD * i, h_ready=KD * i) for i in range(3)]
    ffn_at = [dict(silu_done=KF * i, banks_free=(KF + 2) * i, hi_ready=KF * i, hid_ready=(KF + 2) * i)
              for i in range(4)]
    a1 = sems("mlstm", ["const", "z_ready", "conv_done", "qk_ready", "pad", "gates_read", "neg_abs", "softplus",
                        "nm_ready", "em_ready", "v_ready", "og_ready", "a_turned", "acol_ready", "bc_done",
                        "E_ready", "dots", "S_ready", "num_done", "num_kept", "rden", "rb_done", "y_ready",
                        "y_hi", "y_split"])
    a2 = sems("mix2", ["const", "pos", "decay", "raw_ready", "swapped", "swap_used", "roped", "angle", "trig",
                       "csq", "cstat", "croot", "cnorm", "chi", "csplit", "rv_ready", "lg1", "lg2", "lg_ready",
                       "arg", "dec_ready", "dots", "RS_ready", "o_done", "ob_ready", "mean", "cent", "csq2",
                       "var", "rroot", "r_ready", "r_hi", "r_split", "dec_used"])
    a3 = sems("mla", ["q_part", "q_raw", "swapped", "q_ready", "k_part", "k_ready", "kpe_ready", "v_part",
                      "v_ready", "dots", "max_ready", "P_exp", "P_ready", "turned", "PT_act", "PT_dve",
                      "o_done", "o_hi", "o_split"])
    fin_s = sems("fin", ["t_ready", "turned", "kept_act", "stored"])
    steps = {e: ctx.enter_context(nc.semaphore(f"{e}_step")) for e in ("dve", "act")}
    step_count = {"dve": 0, "act": 0}

    def link(e, name, ins):
        step_count[name] += 1
        ins.then_inc(steps[name], 1)
        e.wait_ge(steps[name], step_count[name])

    def load_ffn(sp, f):
        u0 = f["u0"]
        first = 0
        if u0 == 0:
            for j in range(SLOTS):
                src = kcols(f["gate"] if j % 2 == 0 else f["up"], (f["gc"] if j % 2 == 0 else f["uc"]) + (j // 2) * P, P)
                sp.dma_start(slot_view(raw, j, KD, P), src).then_inc(raw_loaded[j], 16)
            first = 1
        with sp.Fori(first, KF // 2) as i:
            for j in range(4):
                u = u0 + j
                sp.wait_ge(lo_done, 4 * i + (u - SLOTS + 1))
                w, c = (f["gate"], f["gc"]) if j % 2 == 0 else (f["up"], f["uc"])
                src = w.rearrange("(k p) n -> p k n", p=P)[:, :, bass.ds(i * (2 * P) + (c + (j // 2) * P), P)]
                sp.dma_start(slot_view(raw, u, KD, P), src).then_inc(raw_loaded[u % SLOTS], 16)
        u0 += NU_UP
        with sp.Fori(0, 2) as i:
            for j in range(4):
                for q, (k0, kn) in enumerate(FFN_PIECES):
                    u = u0 + 3 * j + q
                    sp.wait_ge(lo_done, 12 * i + (u - SLOTS + 1))
                    src = f["down"][k0 * P:(k0 + kn) * P, :].rearrange("(k p) n -> p k n", p=P)
                    sp.dma_start(slot_view(raw, u, kn, P), src[:, :, bass.ds(i * (4 * P) + j * P, P)]) \
                      .then_inc(raw_loaded[u % SLOTS], 16)

    def load_units(sp, u0, units):
        for j, src in enumerate(units):
            u = u0 + j
            sp.wait_ge(lo_done, u - SLOTS + 1)
            sp.dma_start(slot_view(raw, u, src.shape[1], src.shape[2]), src).then_inc(raw_loaded[u % SLOTS], 16)

    def prog_sync(sp):
        for c in range(CH):
            sp.dma_start(x_tok[:, c, :], dram["x"][0, c * P:(c + 1) * P, :]).then_inc(init[f"x{c}"], 16)
        load_ffn(sp, FFNS[0])
        load_units(sp, U_M1, units1)
        load_ffn(sp, FFNS[1])
        load_ffn(sp, FFNS[2])
        load_units(sp, U_M2, units2)
        load_ffn(sp, FFNS[3])
        for c in range(CH):
            sp.wait_ge(fin_s["kept_act"], 2 * (c + 1))
            sp.dma_start(out[0, c * P:(c + 1) * P, :], fin["otok"][:, c, :]).then_inc(fin_s["stored"], 16)
        sp.wait_ge(fin_s["stored"], 16 * CH)

    def prog_gpsimd(pool):
        with pool.Fori(0, UNITS // SLOTS) as i:
            for s in range(SLOTS):
                pool.wait_ge(hi_done, SLOTS * i + (s + 1))
                pool.tensor_tensor(wlo[:, s, :], raw[:, s, :], whi[:, s, :].bitcast(F32), ALU.subtract) \
                    .then_inc(lo_done, 1)

    cursor = [0]

    def split_hi(act, u, reg=None, stride=0):
        s = u % SLOTS
        if reg is None:
            if u >= UNITS:
                return
            act.wait_ge(raw_loaded[s], 16 * (u // SLOTS + 1))
            if u >= SLOTS:
                act.wait_ge(unit_done, STARTED + u - SLOTS + 1)
        else:
            act.wait_ge(raw_loaded[s], reg * (16 * stride // SLOTS) + 16 * (u // SLOTS + 1))
            act.wait_ge(unit_done, STARTED + reg * stride + (u - SLOTS + 1))
        act.activation(whi[:, s, :], raw[:, s, :], ACT.Copy).then_inc(hi_done, 1)

    def split_to(act, last):
        while cursor[0] <= min(last + AHEAD, UNITS - 1):
            split_hi(act, cursor[0])
            cursor[0] += 1

    def act_norm(act, i, n, source, offset, by_tiles):
        s, at = norm_s, norm_at[i]
        if by_tiles:
            for k in range(KD):
                act.wait_ge(source, offset + k + 1)
                if k >= 2:
                    act.wait_ge(s["sq_used"], at["sq_used"] + k - 1)
                act.activation(tile(sq, k % 2, n), tile(hT, k, n), ACT.Square).then_inc(s["sq_ready"], 1)
            act.wait_ge(s["sq_used"], at["sq_used"] + KD)
        else:
            act.wait_ge(s["sq_used"], at["sq_used"] + 1)
        act.activation(tile(rbc, 0, n), bank(6, n), ACT.Sqrt, scale=1.0 / D, bias=eps[:, :]) \
           .then_inc(s["root_ready"], 1)
        if i == 6:
            return
        for k in range(KD):
            act.wait_ge(s["t_ready"], at["t_ready"] + k + 1)
            act.activation(tile(xhi, k, n), tile(wb, k % 2, n), ACT.Copy).then_inc(s["hi_ready"], 1)

    def act_ffn(act, i):
        f, s, at = FFNS[i], ffn_s, ffn_at[i]
        n, u0 = f["n"], f["u0"]
        split_to(act, u0 - 1)
        with act.Fori(0, KF // 2) as r:
            for b in range(2):
                for e in (2 * b + AHEAD, 2 * b + AHEAD + 1):
                    split_hi(act, u0 + e, r, 4)
                act.wait_ge(unit_done, STARTED + r * 4 + (u0 + 2 * b + 1))
                act.wait_ge(s["banks_free"], at["banks_free"] + r * 2 + (b + 1))
                act.activation(tile(wa, b, n), bank(2 * b if n == TOK else b, n), ACT.Silu) \
                   .then_inc(s["silu_done"], 1)
                act.wait_ge(s["banks_free"], at["banks_free"] + r * 2 + (b + 3))
                act.activation(tile(hid_hi, r * 2 + b, n), tile(wb, b, n), ACT.Copy).then_inc(s["hi_ready"], 1)
        cursor[0] += NU_UP

    def act_out(act, i, n, value, u0, per):
        s, at = out_s, out_at[i]
        split_to(act, u0 - 1)
        with act.Fori(0, 2) as r:
            for j in range(4):
                for e in range(per):
                    if u0 + per * j + AHEAD + e < UNITS - 4 * per:
                        split_hi(act, u0 + per * j + AHEAD + e, r, 4 * per)
                act.wait_ge(s["v_ready"], at["v_ready"] + r * 4 + (j + 3))
                act.wait_ge(s["acc_done"], at["acc_done"] + r * 4 + (j + 1))
                act.activation(tile(sq, j % 2, n), tile(value, r * 4 + j, n), ACT.Square) \
                   .then_inc(s["sq_ready"], 1)
        cursor[0] += 8 * per

    def act_out_last(act, i, n, value, u0, per):
        s, at = out_s, out_at[i]
        for d in range(KD):
            split_to(act, u0 + per * (d + 1) - 1)
            act.wait_ge(s["v_ready"], at["v_ready"] + d + 3)
            act.wait_ge(s["acc_done"], at["acc_done"] + d + 1)
            act.activation(tile(sq, d % 2, n), tile(value, d, n), ACT.Square).then_inc(s["sq_ready"], 1)

    def act_res(act, i, n):
        s, at = res_s, res_at[i]
        act.wait_ge(s["stat"], at["stat"] + 1)
        act.activation(tile(rbc, 0, n), bank(6, n), ACT.Sqrt, scale=1.0 / D, bias=eps[:, :]) \
           .then_inc(s["root_ready"], 1)

    def act_mlstm(act):
        s, u0 = a1, U_M1
        act.wait_ge(s["pad"], 1)
        for m in range(8):
            split_to(act, u0 + m)
            act.wait_ge(unit_done, STARTED + u0 + m + 1)
            if m >= 2:
                act.wait_ge(s["conv_done"], m - 1)
            act.activation(zpad(m % 2)[:, 3:3 + TOK].rearrange("p (a n) -> p a n", a=2), bank(2 * (m % 2), TOK),
                           ACT.Copy).then_inc(s["z_ready"], 1)
            if m >= 1:
                act.wait_ge(s["conv_done"], m)
                act.activation(m1["qkT"][:, (m - 1) * TOK:m * TOK], cacc((m - 1) % 2), ACT.Silu) \
                   .then_inc(s["qk_ready"], 1)
        act.wait_ge(s["conv_done"], 8)
        act.activation(m1["qkT"][:, 7 * TOK:8 * TOK], cacc(1), ACT.Silu).then_inc(s["qk_ready"], 1)
        split_to(act, u0 + 8)
        act.wait_ge(s["neg_abs"], 1)
        link(act, "act", act.activation(gc, gc, ACT.Exp))
        act.activation(gc, gc, ACT.Ln, bias=ones[0:HEADS, 0:1]).then_inc(s["softplus"], 1)
        for n in range(2):
            split_to(act, u0 + 9 + 4 * n + 3)
            act.wait_ge(unit_done, STARTED + u0 + 9 + 4 * n + 4)
            for c in V_ORDER:
                dst = m1["v_meta"][:, n * 512:(n + 1) * 512] if c < 0 else m1["v_real"][:, c, n * 512:(n + 1) * 512]
                b = V_BANK[n][c]
                act.activation(dst, ps[0:META if c < 0 else P, b, :], ACT.Copy).then_inc(s["v_ready"], 1)
        act.wait_ge(s["nm_ready"], 1)
        act.activation(gc, gc, ACT.Exp, scale=-1.0).then_inc(s["em_ready"], 1)
        for m in range(8):
            split_to(act, u0 + 17 + m)
            act.wait_ge(unit_done, STARTED + u0 + 17 + m + 1)
            act.activation(m1["og"][:, m, :], ps[:, 1 + m % 2, :], ACT.Sigmoid).then_inc(s["og_ready"], 1)
        act.wait_ge(s["acol_ready"], 1)
        for h in range(HEADS):
            act.wait_ge(s["bc_done"], h + 1)
            if h >= 2:
                act.wait_ge(s["num_done"], h - 1)
            for j in range(CH + 1):
                rows, t0 = (META, 0) if j == 0 else (P, P * (j - 1))
                act.activation(e_tile(h, j), ps[0:rows, 0, t0:SEQ], ACT.Exp,
                               bias=m1["acol"][0:rows, j * HEADS + h:j * HEADS + h + 1]).then_inc(s["E_ready"], 1)
        for h in range(HEADS):
            act.wait_ge(s["y_ready"], h + 1)
            act.activation(tile(xhi, h, SEQ), tile(wb, h % 2, SEQ), ACT.Copy).then_inc(s["y_hi"], 1)

    def act_mix2(act):
        s, u0 = a2, U_M2
        dst = [m2["cq"][:, 0, :], m2["cq"][:, 1, :], m2["ckv"][:, :], m2["kpe"][NOPE:QK_DIM, :]]
        dst += [m2["rq"][:, m, :] for m in range(4)] + [m2["rk"][:, m, :] for m in range(4)]
        act.wait_ge(s["lg1"], 1)
        link(act, "act", act.activation(m2["lgt"][:, :], m2["lgt"][:, :], ACT.Exp))
        act.activation(m2["lgt"][:, :], m2["lgt"][:, :], ACT.Ln, bias=ones[:, 0:1]).then_inc(s["lg2"], 1)
        for e, d in enumerate(dst):
            split_to(act, u0 + e)
            act.wait_ge(unit_done, STARTED + u0 + e + 1)
            rows = ROPE_DIM if e == 3 else P
            act.activation(d, ps[0:rows, e % 2, :], ACT.Copy, scale=RET_DIM ** -0.5 if e >= 8 else 1.0) \
               .then_inc(s["raw_ready"], 1)
            if e == 1:
                for k in range(2):
                    act.wait_ge(s["raw_ready"], k + 1)
                    act.activation(sq[:, k * TOK:k * TOK + SEQ], m2["cq"][:, k, :], ACT.Square).then_inc(s["csq"], 1)
            if e == 2:
                act.wait_ge(s["raw_ready"], 3)
                act.wait_ge(s["cstat"], 1)
                act.activation(sq[:, 0:SEQ], m2["ckv"][:, :], ACT.Square).then_inc(s["csq"], 1)
            if e == 3:
                for j, (co, si) in enumerate((("cosm", "sinm"), ("cosr", "sinr"))):
                    act.wait_ge(s["angle"], 2 * j + 2)
                    act.activation(m2[si][:, :], m2[si][:, :], ACT.Sin).then_inc(s["trig"], 1)
                    act.activation(m2[co][:, :], m2[co][:, :], ACT.Sin, scale=-1.0, bias=halfpi[:, :]) \
                       .then_inc(s["trig"], 1)
            if e == 5:
                for j, rank in enumerate((Q_RANK, KV_RANK)):
                    act.wait_ge(s["cstat"], j + 1)
                    act.activation(wb[:, j * TOK:j * TOK + SEQ], ps[:, 2 + j, :], ACT.Sqrt, scale=1.0 / rank,
                                   bias=eps[:, :]).then_inc(s["croot"], 1)
            if e == 8:
                for k in range(3):
                    act.wait_ge(s["cnorm"], k + 1)
                    act.activation(m2["cq_hi"][:, k, :] if k < 2 else m2["ckv_hi"][:, :],
                                   m2["cq"][:, k, :] if k < 2 else m2["ckv"][:, :], ACT.Copy).then_inc(s["chi"], 1)
        split_to(act, u0 + 15)
        act.wait_ge(unit_done, STARTED + u0 + 16)
        for c in range(CH):
            act.activation(m2["rv"][:, c, :], ps[:, 2 + c, :], ACT.Copy).then_inc(s["rv_ready"], 1)
        for m in range(4):
            split_to(act, u0 + 16 + m)
            act.wait_ge(unit_done, STARTED + u0 + 17 + m)
            act.activation(m2["rg"][:, m, :], ps[:, m % 2, :], ACT.Silu).then_inc(s["raw_ready"], 1)
        for h in range(HEADS):
            act.wait_ge(s["arg"], h + 1)
            act.activation(m2["dec"][:, :], m2["dec"][:, :], ACT.Exp).then_inc(s["dec_ready"], 1)
            if h % 2 == 1:
                m = h // 2
                act.wait_ge(s["o_done"], m + 1)
                act.activation(wa[:, 0:SEQ], ps[:, m % 2, :], ACT.Copy).then_inc(s["ob_ready"], 1)
                act.wait_ge(s["cent"], m + 1)
                act.activation(sq[:, 0:SEQ], wa[:, 0:SEQ], ACT.Square).then_inc(s["csq2"], 1)
                act.wait_ge(s["var"], m + 1)
                act.activation(rbc[:, 0:SEQ], ps[:, 7, :], ACT.Sqrt, bias=eps[:, :]).then_inc(s["rroot"], 1)
                act.wait_ge(s["r_ready"], m + 1)
                act.activation(tile(xhi, 4 + m, SEQ), wa[:, 0:SEQ], ACT.Copy).then_inc(s["r_hi"], 1)

    def act_mla(act):
        s, u0 = a3, U_M2 + 20
        act.wait_ge(a2["r_split"], 4)
        for h in range(HEADS):
            split_to(act, u0 + h // 4)
            if h % 4 == 3:
                act.wait_ge(unit_done, STARTED + u0 + h // 4 + 1)
            else:
                act.wait_ge(s["q_part"], 3 * (h // 4) + h % 4 + 1)
            act.activation(m3["qT"][:, h, :], ps[0:QK_DIM, h % 2, :], ACT.Copy).then_inc(s["q_raw"], 1)
        for h in range(HEADS):
            act.wait_ge(s["k_part"], h + 1)
            act.activation(m3["kT"][0:NOPE, h, :], ps[0:NOPE, 4 + h % 2, :], ACT.Copy).then_inc(s["k_ready"], 1)
        for c in range(CH):
            if c < CH - 1:
                act.wait_ge(s["v_part"], c + 1)
            else:
                act.wait_ge(unit_done, STARTED + u0 + 3)
            act.activation(m3["vm"][:, c, :], ps[:, 6 + c % 2, :], ACT.Copy).then_inc(s["v_ready"], 1)
        split_to(act, u0 + 2)

        def exps(h):
            for c in range(CH):
                g = CH * h + c
                act.wait_ge(s["max_ready"], g + 1)
                if h >= 1 and c == 0:
                    act.wait_ge(s["turned"], h)
                act.activation(m3["PR"][:, c * SEQ:(c + 1) * SEQ], ps[:, c % 2, :], ACT.Exp, scale=MLA_SCALE,
                               bias=small[:, c:c + 1], accum_out=small[:, 8 + c:9 + c]).then_inc(s["P_exp"], 1)

        exps(0)
        for h in range(HEADS):
            act.wait_ge(s["turned"], h + 1)
            if h >= 1:
                act.wait_ge(s["o_done"], h)
            for k in range(2):
                act.activation(m3["PT"][:, k * SEQ:(k + 1) * SEQ], ps[:, 2 + k, :], ACT.Copy).then_inc(s["PT_act"], 1)
            if h + 1 < HEADS:
                exps(h + 1)
            if h % 2 == 1:
                act.wait_ge(s["o_done"], h + 1)
                act.activation(tile(xhi, h // 2, SEQ), ps[:, 6 + (h // 2) % 2, :], ACT.Copy).then_inc(s["o_hi"], 1)

    def prog_scalar(act):
        act.dma_start(meta_tok[:, :], dram["meta_tokens"]).then_inc(init["meta"], 16)
        act.dma_start(ident[:, :], dram["const"][:, CONST["ident"]]).then_inc(init["const"], 16)
        act.dma_start(ones[:, :], dram["const"][:, CONST["ones"]]).then_inc(init["const"], 16)
        act.dma_start(gateb[:, :], dram["a_gate_b"].rearrange("a (t h) -> h (a t)", t=2),
                      allow_slow_non_contiguous=True).then_inc(init["const"], 16)
        rows = {
            "norm_gains": dram["norm_gains"].rearrange("a g (k p) -> (a g k) p", p=P),
            "a_conv_w": dram["a_conv_w"].rearrange("a j (k p) -> (a j k) p", p=P),
            "final_norm_2": dram["final_norm_2"].rearrange("(k p) -> k p", p=P),
        }
        for name, n in VEC_ROWS:
            src = rows[name] if name in rows else dram[name].rearrange("a (k p) -> (a k) p", p=P)
            act.dma_start(vrows[VEC[name]:VEC[name] + n, :], src).then_inc(init["vecs"], 16)
        split_to(act, -1)
        act_norm(act, 0, TOK, init["h_ready"], 1, True)
        act_ffn(act, 0)
        act_out(act, 0, TOK, ybuf, NU_UP, 3)
        act_res(act, 0, TOK)
        act_norm(act, 1, TOK, res_s["h_ready"], res_at[0]["h_ready"], True)
        for name in ("tri", "selcol"):
            act.dma_start(m1[name][:, :], dram["const"][:, CONST[name]]).then_inc(a1["const"], 16)
        act.dma_start(m1["selrow"][:, :], dram["const"][0:HEADS, CONST["selrow"]]).then_inc(a1["const"], 16)
        act_mlstm(act)
        act_out(act, 1, SEQ, m1["num"], U_M1 + 25, 1)
        act_res(act, 1, SEQ)
        act_norm(act, 2, SEQ, res_s["h_ready"], res_at[1]["h_ready"], True)
        act_ffn(act, 1)
        act_out(act, 2, SEQ, ybuf, FFNS[1]["u0"] + NU_UP, 3)
        act_res(act, 2, SEQ)
        act_norm(act, 3, SEQ, res_s["h_ready"], res_at[2]["h_ready"], True)
        act_ffn(act, 2)
        act_out(act, 3, SEQ, hT, FFNS[2]["u0"] + NU_UP, 3)
        for name in ("permpe", "perm", "block", "invf", "relpos", "relneg"):
            act.dma_start(m2[name][:, :], dram["const"][:, CONST[name]]).then_inc(a2["const"], 16)
        act.dma_start(m2["RS"][:, 0, :].bitcast(I32), dram["positions_2"].broadcast_to([P, SEQ])) \
           .then_inc(a2["pos"], 16)
        for j, name in enumerate(("ret_decay_fwd_2", "ret_decay_bwd_2")):
            act.dma_start(m2["lg"][:, j * HEADS:(j + 1) * HEADS], dram[name].broadcast_to([P, HEADS])) \
               .then_inc(a2["decay"], 16)
        act_norm(act, 4, SEQ, None, 0, False)
        act_mix2(act)
        act_mla(act)
        act_out(act, 4, SEQ, hT, U_M2 + 23, 1)
        act_norm(act, 5, SEQ, None, 0, False)
        act_ffn(act, 3)
        act_out_last(act, 5, SEQ, hT, FFNS[3]["u0"] + NU_UP, 3)
        act_norm(act, 6, SEQ, None, 0, False)
        for c in range(CH):
            for j in range(2):
                g = 2 * c + j
                act.wait_ge(fin_s["turned"], g + 1)
                act.activation(fin["otok"][:, c, j * 512:(j + 1) * 512], ps[:, g % 4, :], ACT.Copy) \
                   .then_inc(fin_s["kept_act"], 1)

    def zpad(b):
        return m1["E"][:, b * 532:b * 532 + 3 + TOK]

    def cacc(b):
        return m1["E"][:, 1064 + b * TOK:1064 + (b + 1) * TOK]

    def e_tile(h, j):
        o = (h % 2) * sum(EW) + EO[j]
        return m1["E"][0:META if j == 0 else P, o:o + EW[j]]

    ga, gb = wa[0:HEADS, 0:TOK], wa[0:HEADS, TOK:2 * TOK]
    gc, go = wb[0:HEADS, 0:TOK], wb[0:HEADS, TOK:2 * TOK]
    V_ORDER = [0, -1, 1, 2, 3]
    V_BANK = [{0: 0, 1: 1, 2: 2, 3: 3, -1: 4}, {0: 5, 1: 6, 2: 7, 3: 0, -1: 4}]
    QK_BANK = [4, 5, 6, 7, 2]

    def dve_norm(v, i, n, name, g0):
        s, at = norm_s, norm_at[i]
        v.wait_ge(s["root_ready"], at["root_ready"] + 1)
        v.reciprocal(tile(rbc, 0, n), tile(rbc, 0, n)).then_inc(s["recip"], 1)
        v.wait_ge(s["recip"], at["recip"] + 1)
        if i == 6:
            for k in range(KD):
                v.scalar_tensor_tensor(out=fin["fin"][:, k, :], in0=tile(hT, k, n), scalar=gain(name, g0 + k),
                                       in1=tile(rbc, 0, n), op0=ALU.mult, op1=ALU.mult).then_inc(fin_s["t_ready"], 1)
            return
        for k in range(KD + 1):
            if k < KD:
                if k >= 2:
                    v.wait_ge(s["x_ready"], at["x_ready"] + k - 1)
                v.scalar_tensor_tensor(out=tile(wb, k % 2, n), in0=tile(hT, k, n), scalar=gain(name, g0 + k),
                                       in1=tile(rbc, 0, n), op0=ALU.mult, op1=ALU.mult).then_inc(s["t_ready"], 1)
            if k >= 1:
                v.wait_ge(s["hi_ready"], at["hi_ready"] + k)
                v.tensor_tensor(tile(xlo, k - 1, n), tile(wb, (k - 1) % 2, n), tile(xhi, k - 1, n).bitcast(F32),
                                ALU.subtract).then_inc(s["x_ready"], 1)

    def dve_ffn(v, i):
        f, s, at, n, u0 = FFNS[i], ffn_s, ffn_at[i], FFNS[i]["n"], FFNS[i]["u0"]
        v.wait_ge(norm_s["x_ready"], norm_at[NORM_OF_FFN[i]]["x_ready"] + KD)
        v.memset(cell[:, :], 0.0).then_inc(s["banks_free"], 2)
        v.memset(small[:, 0:1], 0.0).then_inc(s["hid_ready"], 2)
        with v.Fori(0, KF // 2) as r:
            for b in range(2):
                v.wait_ge(s["silu_done"], at["silu_done"] + r * 2 + (b + 1))
                v.wait_ge(unit_done, STARTED + r * 4 + (u0 + 2 * b + 2))
                v.wait_ge(s["hid_ready"], at["hid_ready"] + r * 2 + (b + 1))
                v.tensor_tensor(tile(wb, b, n), tile(wa, b, n), bank(4 + 2 * b if n == TOK else 2 + b, n), ALU.mult) \
                 .then_inc(s["banks_free"], 1)
                v.wait_ge(s["hi_ready"], at["hi_ready"] + r * 2 + (b + 1))
                v.tensor_tensor(tile(hid_lo, r * 2 + b, n), tile(wb, b, n),
                                tile(hid_hi, r * 2 + b, n).bitcast(F32), ALU.subtract).then_inc(s["hid_ready"], 1)

    def dve_out(v, i, n, value, u0, per, add):
        s, at = out_s, out_at[i]
        v.memset(tile(acc, 0, n), 0.0).then_inc(s["acc_done"], 2)
        v.memset(cell[:, :], 0.0).then_inc(s["v_ready"], 2)
        with v.Fori(0, 2) as r:
            for j in range(4):
                v.wait_ge(unit_done, STARTED + r * (4 * per) + (u0 + per * (j + 1)))
                if add is None:
                    ins = v.tensor_copy(tile(value, r * 4 + j, n), out_bank(i, j, n))
                else:
                    ins = v.scalar_tensor_tensor(out=tile(value, r * 4 + j, n), in0=out_bank(i, j, n), scalar=add,
                                                 in1=tile(value, r * 4 + j, n), op0=ALU.mult, op1=ALU.add)
                ins.then_inc(s["v_ready"], 1)
                v.wait_ge(s["sq_ready"], at["sq_ready"] + r * 4 + (j + 1))
                v.wait_ge(s["acc_done"], at["acc_done"] + r * 4 + (j + 2))
                v.tensor_tensor(tile(acc, 0, n), tile(acc, 0, n), tile(sq, j % 2, n), ALU.add) \
                 .then_inc(s["acc_done"], 1)

    def dve_res(v, i, n, value, g0, factor):
        s, at = res_s, res_at[i]
        v.wait_ge(s["root_ready"], at["root_ready"] + 1)
        v.reciprocal(tile(rbc, 0, n), tile(rbc, 0, n)).then_inc(s["recip"], 1)
        v.wait_ge(s["recip"], at["recip"] + 1)
        for k in range(KD + 1):
            if k < KD:
                if k >= 2:
                    v.wait_ge(s["h_ready"], at["h_ready"] + k - 1)
                v.scalar_tensor_tensor(out=tile(wa, k % 2, n), in0=tile(value, k, n), scalar=gain("norm_gains", g0 + k),
                                       in1=tile(rbc, 0, n), op0=ALU.mult, op1=ALU.mult).then_inc(s["t_ready"], 1)
            if k >= 1:
                v.wait_ge(s["t_ready"], at["t_ready"] + k)
                v.scalar_tensor_tensor(out=tile(hT, k - 1, n), in0=tile(wa, (k - 1) % 2, n), scalar=factor,
                                       in1=tile(hT, k - 1, n), op0=ALU.mult, op1=ALU.add).then_inc(s["h_ready"], 1)

    def dve_mlstm(v):
        s, u0 = a1, U_M1
        v.wait_ge(norm_s["x_ready"], norm_at[1]["x_ready"] + KD)
        v.memset(zpad(0)[:, 0:3], 0.0)
        v.memset(zpad(1)[:, 0:3], 0.0)
        v.memset(go, 1.0).then_inc(s["pad"], 1)
        for m in range(8):
            b = m % 2
            v.wait_ge(s["z_ready"], m + 1)
            if m >= 2:
                v.wait_ge(s["qk_ready"], m - 1)
            w = [gain("a_conv_w", 8 * j + m) for j in range(CONV)]
            link(v, "dve", v.tensor_scalar(cacc(b), zpad(b)[:, 3:3 + TOK], w[3], gain("a_conv_b", m), ALU.mult, ALU.add))
            for j in (2, 1):
                link(v, "dve", v.scalar_tensor_tensor(out=cacc(b), in0=zpad(b)[:, j:j + TOK], scalar=w[j], in1=cacc(b),
                                                      op0=ALU.mult, op1=ALU.add))
            v.scalar_tensor_tensor(out=cacc(b), in0=zpad(b)[:, 0:TOK], scalar=w[0], in1=cacc(b), op0=ALU.mult,
                                   op1=ALU.add).then_inc(s["conv_done"], 1)
        v.wait_ge(unit_done, STARTED + u0 + 9)
        g2 = [x.rearrange("p (a n) -> p a n", a=2) for x in (ga, gb)]
        link(v, "dve", v.tensor_scalar(g2[0], bank(4, TOK, HEADS), gateb[:, 0:1], None, ALU.add))
        v.tensor_scalar(g2[1], bank(6, TOK, HEADS), gateb[:, 1:2], None, ALU.add).then_inc(s["gates_read"], 1)
        v.wait_ge(s["gates_read"], 1)
        v.scalar_tensor_tensor(out=gc, in0=gb, scalar=-1.0, in1=gb, op0=ALU.mult, op1=ALU.min).then_inc(s["neg_abs"], 1)
        v.wait_ge(s["softplus"], 1)
        link(v, "dve", v.scalar_tensor_tensor(out=gb, in0=gb, scalar=0.0, in1=gc, op0=ALU.min, op1=ALU.subtract))
        link(v, "dve", v.tensor_tensor_scan(gc, go, gb, 0.0, ALU.mult, ALU.add))
        link(v, "dve", v.tensor_tensor(ga, ga, gc, ALU.subtract))
        link(v, "dve", v.tensor_tensor_scan(gb, ga, ga, 0.0, ALU.max, ALU.max))
        link(v, "dve", v.tensor_tensor(gc, gc, gb, ALU.add))
        v.tensor_scalar(gb, gb, -1.0, None, ALU.mult).then_inc(s["nm_ready"], 1)
        v.wait_ge(s["a_turned"], 1)
        v.memset(m1["acol"][:, :], 0.0).then_inc(s["rden"], 1)
        v.wait_ge(s["rden"], 1)
        link(v, "dve", v.tensor_copy(m1["acol"][0:META, 0:HEADS], ps[0:META, 3, 0:HEADS]))
        v.tensor_copy(m1["acol"][:, HEADS:], ps[:, 3, HEADS:(CH + 1) * HEADS]).then_inc(s["acol_ready"], 1)

        def keep(h):
            v.wait_ge(s["num_done"], h + 1)
            v.wait_ge(s["og_ready"], h + 1)
            v.tensor_tensor(tile(m1["num"], h, SEQ), ps[:, 1, :], m1["og"][:, h, :], ALU.mult).then_inc(s["num_kept"], 1)

        v.wait_ge(a1["const"], 48)
        for h in range(HEADS):
            for j in range(CH + 1):
                g = (CH + 1) * h + j
                e = e_tile(h, j)
                v.wait_ge(s["E_ready"], g + 1)
                if j >= 1:
                    link(v, "dve", v.scalar_tensor_tensor(out=e[:, 0:P], in0=e[:, 0:P], scalar=1.0, in1=m1["tri"][:, :],
                                                          op0=ALU.min, op1=ALU.mult))
                v.wait_ge(s["dots"], g + 1)
                v.scalar_tensor_tensor(out=e, in0=ps[0:META if j == 0 else P, QK_BANK[j], 0:EW[j]],
                                       scalar=A_DK ** -0.5, in1=e, op0=ALU.mult, op1=ALU.mult).then_inc(s["S_ready"], 1)
            if h >= 1:
                keep(h - 1)
        keep(HEADS - 1)
        v.wait_ge(s["em_ready"], 1)
        em = gc[:, META:TOK]
        den = ps[0:HEADS, 3, :]
        dn = ga[:, META:TOK]
        link(v, "dve", v.scalar_tensor_tensor(out=dn, in0=den, scalar=-1.0, in1=em, op0=ALU.mult, op1=ALU.max))
        link(v, "dve", v.tensor_tensor(dn, den, dn, ALU.max))
        v.reciprocal(dn, dn).then_inc(s["rden"], 1)
        for h in range(HEADS + 1):
            if h < HEADS:
                v.wait_ge(s["rb_done"], h + 1)
                if h >= 2:
                    v.wait_ge(s["y_split"], h - 1)
                v.tensor_tensor(tile(wb, h % 2, SEQ), tile(m1["num"], h, SEQ), ps[:, 4 + h % 4, :], ALU.mult) \
                 .then_inc(s["y_ready"], 1)
            if h >= 1:
                v.wait_ge(s["y_hi"], h)
                v.tensor_tensor(tile(xlo, h - 1, SEQ), tile(wb, (h - 1) % 2, SEQ), tile(xhi, h - 1, SEQ).bitcast(F32),
                                ALU.subtract).then_inc(s["y_split"], 1)

    MAGIC = 12582912.0
    TWO_PI = 6.283185307179586
    PI_1 = 6.25
    PI_2 = float(np.float32(np.round((TWO_PI - PI_1) * 2.0 ** 16) / 2.0 ** 16))
    PI_3 = TWO_PI - PI_1 - PI_2
    PI_SAFE = 3.1415925

    def dve_mix2(v):
        s, u0 = a2, U_M2
        v.wait_ge(s["decay"], 32)
        v.scalar_tensor_tensor(out=m2["lgt"][:, :], in0=m2["lg"][:, :], scalar=-1.0, in1=m2["lg"][:, :],
                               op0=ALU.mult, op1=ALU.min).then_inc(s["lg1"], 1)
        v.wait_ge(s["pos"], 16)
        v.wait_ge(s["const"], 96)
        posi, posf = m2["RS"][:, 0, :].bitcast(I32), m2["RS"][:, 1, :]
        turn = m2["RS"][:, 2, :]
        link(v, "dve", v.tensor_copy(posf, posi))
        for j, (co, si) in enumerate((("cosm", "sinm"), ("cosr", "sinr"))):
            ang, ab = m2[si][:, :], m2[co][:, :]
            link(v, "dve", v.tensor_scalar(ang, posf, m2["invf"][:, j:j + 1], None, ALU.mult))
            link(v, "dve", v.tensor_scalar(turn, ang, 1.0 / TWO_PI, None, ALU.mult))
            link(v, "dve", v.tensor_scalar(turn, turn, MAGIC, None, ALU.add))
            link(v, "dve", v.tensor_scalar(turn, turn, MAGIC, None, ALU.subtract))
            for part in (PI_1, PI_2, PI_3):
                link(v, "dve", v.scalar_tensor_tensor(out=ang, in0=turn, scalar=-part, in1=ang, op0=ALU.mult, op1=ALU.add))
            v.tensor_scalar(ang, ang, -PI_SAFE, PI_SAFE, ALU.max, ALU.min).then_inc(s["angle"], 1)
            v.wait_ge(s["angle"], 2 * j + 1)
            v.scalar_tensor_tensor(out=ab, in0=ang, scalar=-1.0, in1=ang, op0=ALU.mult, op1=ALU.max) \
             .then_inc(s["angle"], 1)
        v.wait_ge(s["lg2"], 1)
        v.scalar_tensor_tensor(out=m2["lg"][:, :], in0=m2["lg"][:, :], scalar=0.0, in1=m2["lgt"][:, :],
                               op0=ALU.min, op1=ALU.subtract).then_inc(s["lg_ready"], 1)

        def latent(k):
            x = m2["cq"][:, k, :] if k < 2 else m2["ckv"][:, :]
            hi = m2["cq_hi"][:, k, :] if k < 2 else m2["ckv_hi"][:, :]
            lo = m2["cq_lo"][:, k, :] if k < 2 else m2["ckv_lo"][:, :]
            return x, hi, lo

        def rope(r):
            rows = slice(NOPE, QK_DIM) if r == 0 else slice(0, P)
            co, si = ("cosm", "sinm") if r == 0 else ("cosr", "sinr")
            x = (m2["kpe"][rows, :] if r == 0 else (m2["rq"] if r < 5 else m2["rk"])[:, (r - 1) % 4, :])
            tmp = wa[rows, 0:SEQ]
            v.wait_ge(s["swapped"], r + 1)
            v.tensor_tensor(tmp, m2[si][rows, :], ps[rows, 6 + r % 2, :], ALU.mult).then_inc(s["swap_used"], 1)
            link(v, "dve", v.tensor_tensor(x, x, m2[co][rows, :], ALU.mult))
            v.wait_ge(s["swap_used"], r + 1)
            v.tensor_tensor(x, x, tmp, ALU.add).then_inc(s["roped"], 1)

        v.wait_ge(s["trig"], 4)
        for r in range(2):
            rope(r)
            v.wait_ge(s["roped"], r + 1)
        v.wait_ge(s["croot"], 2)
        for j in range(2):
            link(v, "dve", v.reciprocal(wb[:, j * TOK:j * TOK + SEQ], wb[:, j * TOK:j * TOK + SEQ]))
        for k in range(3):
            x = latent(k)[0]
            r0 = 0 if k < 2 else TOK
            v.scalar_tensor_tensor(out=x, in0=x, scalar=gain("q_norm_2", k) if k < 2 else gain("kv_norm_2", 0),
                                   in1=wb[:, r0:r0 + SEQ], op0=ALU.mult, op1=ALU.mult).then_inc(s["cnorm"], 1)
        for r in range(2, 5):
            rope(r)
            v.wait_ge(s["roped"], r + 1)
        for k in range(3):
            x, hi, lo = latent(k)
            v.wait_ge(s["chi"], k + 1)
            v.tensor_tensor(lo, x, hi.bitcast(F32), ALU.subtract).then_inc(s["csplit"], 1)
        for r in range(5, 9):
            rope(r)
            v.wait_ge(s["roped"], r + 1)

        def decay_arg(h):
            if h >= 1:
                v.wait_ge(s["RS_ready"], CH * h)
            link(v, "dve", v.tensor_scalar(m2["dec"][:, :], m2["relpos"][:, :], m2["lg"][:, h:h + 1], None, ALU.mult))
            v.scalar_tensor_tensor(out=m2["dec"][:, :], in0=m2["relneg"][:, :], scalar=m2["lg"][:, HEADS + h:HEADS + h + 1],
                                   in1=m2["dec"][:, :], op0=ALU.mult, op1=ALU.add).then_inc(s["arg"], 1)

        v.wait_ge(s["lg_ready"], 1)
        for h in range(HEADS):
            decay_arg(h)
            v.wait_ge(s["dec_ready"], h + 1)
            for c in range(CH):
                g = CH * h + c
                v.wait_ge(s["dots"], g + 1)
                if h >= 1:
                    v.wait_ge(s["dec_used"], g - CH + 1)
                o = (SEQ - P) - P * c
                v.tensor_tensor(m2["RS"][:, c, :], m2["dec"][:, o:o + SEQ], ps[:, 2 + c, :], ALU.mult) \
                 .then_inc(s["RS_ready"], 1)
            if h % 2 == 1:
                m = h // 2
                ob = wa[:, 0:SEQ]
                v.wait_ge(s["mean"], m + 1)
                v.tensor_tensor(ob, ob, ps[:, 6, :], ALU.subtract).then_inc(s["cent"], 1)
                v.wait_ge(s["raw_ready"], 13 + m)
                v.wait_ge(s["cent"], m + 1)
                v.wait_ge(s["csq2"], m + 1)
                link(v, "dve", v.tensor_tensor(ob, ob, m2["rg"][:, m, :], ALU.mult))
                v.wait_ge(s["rroot"], m + 1)
                link(v, "dve", v.reciprocal(rbc[:, 0:SEQ], rbc[:, 0:SEQ]))
                v.tensor_tensor(ob, ob, rbc[:, 0:SEQ], ALU.mult).then_inc(s["r_ready"], 1)
                v.wait_ge(s["r_hi"], m + 1)
                v.tensor_tensor(tile(xlo, 4 + m, SEQ), ob, tile(xhi, 4 + m, SEQ).bitcast(F32), ALU.subtract) \
                 .then_inc(s["r_split"], 1)

    def dve_mla(v):
        s, u0 = a3, U_M2 + 20
        v.wait_ge(a2["r_split"], 4)
        for h in range(HEADS):
            link(v, "dve", v.tensor_copy(m3["kT"][NOPE:QK_DIM, h, :], m3["kpe"][NOPE:QK_DIM, :]))
        v.memset(cell[:, :], 0.0).then_inc(s["kpe_ready"], 1)
        rows = slice(NOPE, QK_DIM)
        for h in range(HEADS):
            x, tmp = m3["qT"][rows, h, :], wa[rows, 0:SEQ]
            v.wait_ge(s["swapped"], h + 1)
            if h >= 1:
                v.wait_ge(s["q_ready"], h)
            link(v, "dve", v.tensor_tensor(tmp, m3["sinm"][rows, :], ps[rows, 2 + h % 2, :], ALU.mult))
            link(v, "dve", v.tensor_tensor(x, x, m3["cosm"][rows, :], ALU.mult))
            v.tensor_tensor(x, x, tmp, ALU.add).then_inc(s["q_ready"], 1)

        def scale(h, c):
            v.wait_ge(s["P_exp"], CH * h + c + 1)
            link(v, "dve", v.reciprocal(small[:, 16 + c:17 + c], small[:, 8 + c:9 + c]))
            x = m3["PR"][:, c * SEQ:(c + 1) * SEQ]
            v.tensor_scalar(x, x, small[:, 16 + c:17 + c], None, ALU.mult).then_inc(s["P_ready"], 1)

        def maxima(h):
            for c in range(CH):
                g = CH * h + c
                v.wait_ge(s["dots"], g + 1)
                link(v, "dve", v.reduce_max(small[:, 24 + c:25 + c], ps[:, c % 2, :], AX_X))
                if h >= 1 and c == 0:
                    v.wait_ge(s["P_exp"], CH * h)
                v.tensor_scalar(small[:, c:c + 1], small[:, 24 + c:25 + c], -MLA_SCALE, None, ALU.mult) \
                 .then_inc(s["max_ready"], 1)
                if c >= 1:
                    scale(h, c - 1)
            scale(h, CH - 1)

        maxima(0)
        for h in range(HEADS):
            v.wait_ge(s["turned"], h + 1)
            if h >= 1:
                v.wait_ge(s["o_done"], h)
            for k in range(2, 4):
                v.tensor_copy(m3["PT"][:, k * SEQ:(k + 1) * SEQ], ps[:, 2 + k, :]).then_inc(s["PT_dve"], 1)
            if h + 1 < HEADS:
                maxima(h + 1)
            if h % 2 == 1:
                m = h // 2
                v.wait_ge(s["o_hi"], m + 1)
                v.tensor_tensor(tile(xlo, m, SEQ), ps[:, 6 + m % 2, :], tile(xhi, m, SEQ).bitcast(F32), ALU.subtract) \
                 .then_inc(s["o_split"], 1)

    def prog_vector(v):
        v.memset(eps[:, :], EPS).then_inc(init["eps"], 1)
        v.memset(halfpi[:, :], TWO_PI / 4).then_inc(init["eps"], 1)
        v.wait_ge(init["turned"], 1)
        v.tensor_copy(vec[:, :], ps[:, 5, 0:NVEC]).then_inc(init["h_ready"], 1)
        hv = hT[:, :].rearrange("p (k t) -> p k t", k=KD)
        v.wait_ge(init["turned"], 2)
        link(v, "dve", v.tensor_copy(hv[:, :, 0:META], ps[:, 4, 0:KD * META].rearrange("p (k t) -> p k t", k=KD)))
        for k in range(KD):
            v.wait_ge(init["turned"], 3 + k)
            v.tensor_copy(hv[:, k, META:TOK], ps[:, k % 4, :]).then_inc(init["h_ready"], 1)
        dve_norm(v, 0, TOK, *FFNS[0]["norm"])
        dve_ffn(v, 0)
        dve_out(v, 0, TOK, ybuf, NU_UP, 3, None)
        dve_res(v, 0, TOK, ybuf, 8, 0.5)
        dve_norm(v, 1, TOK, "norm_gains", 16)
        dve_mlstm(v)
        dve_out(v, 1, SEQ, m1["num"], U_M1 + 25, 1, None)
        dve_res(v, 1, SEQ, m1["num"], 24, 1.0)
        dve_norm(v, 2, SEQ, "norm_gains", 32)
        dve_ffn(v, 1)
        dve_out(v, 2, SEQ, ybuf, FFNS[1]["u0"] + NU_UP, 3, None)
        dve_res(v, 2, SEQ, ybuf, 40, 0.5)
        dve_norm(v, 3, SEQ, "ffn1_norm_2", 0)
        dve_ffn(v, 2)
        dve_out(v, 3, SEQ, hT, FFNS[2]["u0"] + NU_UP, 3, 0.5)
        dve_norm(v, 4, SEQ, "mix_norm_2", 0)
        dve_mix2(v)
        dve_mla(v)
        dve_out(v, 4, SEQ, hT, U_M2 + 23, 1, 1.0)
        dve_norm(v, 5, SEQ, "ffn2_norm_2", 0)
        dve_ffn(v, 3)
        dve_out(v, 5, SEQ, hT, FFNS[3]["u0"] + NU_UP, 3, 0.5)
        dve_norm(v, 6, SEQ, "final_norm_2", 0)

    NORM_OF_FFN = [0, 2, 3, 5]

    def out_bank(i, j, n):
        return bank(2 * (j % 2) if n == TOK else 4 + j % 2, n)

    def product(pe, outs, lhs, rhs, first, last):
        n = 0
        for l, r in ((0, 0), (0, 1), (1, 0)):
            for o, x in zip(outs, rhs):
                ins = pe.matmul(o, lhs[l], x[r], start=first and n == 0, stop=last and n == 2)
            n += 1
        return ins

    def w_tile(u, k, n=P, c0=0, width=P):
        return [w[:, u % SLOTS, k * n + c0:k * n + c0 + width] for w in (whi, wlo)]

    def x_cols(k, o, w):
        return [x[:, k * TOK + o:k * TOK + o + w] for x in (xhi, xlo)]

    def project(pe, b, n, u, norm=None, width=P, wn=P):
        for k in range(KD):
            if norm is not None:
                pe.wait_ge(norm_s["x_ready"], norm_at[norm]["x_ready"] + k + 1)
            p = pieces(b, n)
            ins = product(pe, [o[0:width] for o, _, _ in p], w_tile(u, k, wn, 0, width), [x_cols(k, o, w) for _, o, w in p],
                          k == 0, k == KD - 1)
        return ins

    def stat_tiles(pe, i, n):
        s, at = norm_s, norm_at[i]
        for k in range(KD):
            pe.wait_ge(s["sq_ready"], at["sq_ready"] + k + 1)
            for o, c, w in pieces(6, n):
                ins = pe.matmul(o, ones[:, :], sq[:, (k % 2) * TOK + c:(k % 2) * TOK + c + w], start=k == 0, stop=k == KD - 1)
            ins.then_inc(s["sq_used"], 1)

    def stat_acc(pe, i, n, done):
        pe.wait_ge(out_s["acc_done"], out_at[i]["acc_done"] + KD + 2)
        for o, c, w in pieces(6, n):
            ins = pe.matmul(o, ones[:, :], acc[:, c:c + w], start=True, stop=True)
        ins.then_inc(done, 1)

    def pe_ffn(pe, i, norm):
        f, s, at, n, u0 = FFNS[i], ffn_s, ffn_at[i], FFNS[i]["n"], FFNS[i]["u0"]
        with pe.Fori(0, KF // 2) as r:
            for b in range(2):
                for g in range(2):
                    u = u0 + 2 * b + g
                    pe.wait_ge(lo_done, r * 4 + (u + 1))
                    pe.wait_ge(s["banks_free"], at["banks_free"] + r * 2 + (b + 1))
                    p = pieces((4 * g + 2 * b) if n == TOK else (2 * g + b), n)
                    for k in range(KD):
                        if b == 0 and g == 0:
                            pe.wait_ge(norm_s["x_ready"], norm_at[norm]["x_ready"] + k + 1)
                        ins = product(pe, [o for o, _, _ in p], w_tile(u, k), [x_cols(k, o, w) for _, o, w in p],
                                      k == 0, k == KD - 1)
                    ins.then_inc(unit_done, 1)
        u0 += NU_UP
        v_at = out_at[[0, 2, 3, 5][i]]["v_ready"]
        with pe.Fori(0, 2) as r:
            for j in range(4):
                pe.wait_ge(out_s["v_ready"], v_at + r * 4 + (j + 1))
                b = 2 * (j % 2) if n == TOK else 4 + j % 2
                p = pieces(b, n)
                for q, (k0, kn) in enumerate(FFN_PIECES):
                    u = u0 + 3 * j + q
                    pe.wait_ge(lo_done, r * 12 + (u + 1))
                    for k in range(k0, k0 + kn):
                        if j == 0:
                            pe.wait_ge(s["hid_ready"], at["hid_ready"] + k + 3)
                        ins = product(pe, [o for o, _, _ in p], w_tile(u, k - k0),
                                      [[x[:, k * TOK + o:k * TOK + o + w] for x in (hid_hi, hid_lo)] for _, o, w in p],
                                      k == 0, k == KF - 1)
                    ins.then_inc(unit_done, 1)

    def pe_out(pe, i, u0, order, ready):
        s, at = out_s, out_at[i]
        with pe.Fori(0, 2) as r:
            for j in range(4):
                pe.wait_ge(s["v_ready"], at["v_ready"] + r * 4 + (j + 1))
                pe.wait_ge(lo_done, r * 4 + (u0 + j + 1))
                for q, k in enumerate(order):
                    if j == 0:
                        sem, count = ready(k)
                        pe.wait_ge(sem, count)
                    ins = product(pe, [ps[:, 4 + j % 2, :]], w_tile(u0 + j, k), [x_cols(k, META, SEQ)], q == 0, q == KD - 1)
                ins.then_inc(unit_done, 1)

    def pe_mlstm(pe):
        s, u0 = a1, U_M1
        for m in range(8):
            pe.wait_ge(lo_done, u0 + m + 1)
            if m >= 2:
                pe.wait_ge(s["z_ready"], m - 1)
            project(pe, 2 * (m % 2), TOK, u0 + m, 1 if m == 0 else None).then_inc(unit_done, 1)
        pe.wait_ge(lo_done, u0 + 9)
        for g in range(2):
            for k in range(KD):
                p = pieces(4 + 2 * g, TOK)
                ins = product(pe, [o[0:HEADS] for o, _, _ in p], w_tile(u0 + 8, k, 2 * HEADS, g * HEADS, HEADS),
                              [x_cols(k, o, w) for _, o, w in p], k == 0, k == KD - 1)
        ins.then_inc(unit_done, 1)
        pe.wait_ge(s["z_ready"], 8)
        pe.wait_ge(s["gates_read"], 1)
        for n in range(2):
            for j in range(4):
                u = u0 + 9 + 4 * n + j
                pe.wait_ge(lo_done, u + 1)
                for kk in range(2):
                    k = 2 * j + kk
                    for c in (0, 1, 2, 3, -1):
                        if n == 1 and k == 0 and c in (3, -1):
                            pe.wait_ge(s["v_ready"], 1 if c == 3 else 2)
                        rows = META if c < 0 else P
                        x = x_cols(k, 0 if c < 0 else META + P * c, rows)
                        ins = product(pe, [ps[0:rows, V_BANK[n][c], :]], x, [w_tile(u, kk, 512, 0, 512)], k == 0, k == KD - 1)
                ins.then_inc(unit_done, 1)
        pe.wait_ge(s["v_ready"], 5)
        pe.wait_ge(s["nm_ready"], 1)
        pe.transpose(ps[0:META, 3, 0:HEADS], ga[:, 0:META], ident[0:HEADS, 0:HEADS])
        for c in range(CH):
            ins = pe.transpose(ps[:, 3, (c + 1) * HEADS:(c + 2) * HEADS], ga[:, META + P * c:META + P * (c + 1)],
                               ident[0:HEADS, 0:HEADS])
        ins.then_inc(s["a_turned"], 1)
        for m in range(8):
            pe.wait_ge(lo_done, u0 + 17 + m + 1)
            if m >= 2:
                pe.wait_ge(s["og_ready"], m - 1)
            project(pe, 1 + m % 2, SEQ, u0 + 17 + m, None).then_inc(unit_done, 1)

        def broadcast(h):
            pe.matmul(ps[:, 0, :], m1["selrow"][:, h * P:(h + 1) * P], gb[:, META:TOK], start=True, stop=True) \
              .then_inc(s["bc_done"], 1)

        def dots(h, j):
            rows = slice(64 * (h % 2), 64 * (h % 2) + 64)
            ks, q0 = (0, META) if j == 0 else (META + P * (j - 1), META + P * (j - 1))
            kw = META if j == 0 else P
            kt, qt = (4 + h // 2) * TOK, (h // 2) * TOK
            pe.matmul(ps[0:kw, QK_BANK[j], 0:EW[j]], m1["qkT"][rows, kt + ks:kt + ks + kw],
                      m1["qkT"][rows, qt + q0:qt + q0 + EW[j]], start=True, stop=True).then_inc(s["dots"], 1)

        pe.wait_ge(s["qk_ready"], 8)
        pe.wait_ge(s["const"], 48)
        pe.wait_ge(s["v_ready"], 10)
        pe.wait_ge(s["og_ready"], 8)
        broadcast(0)
        for j in range(CH + 1):
            dots(0, j)
        pe.wait_ge(s["acol_ready"], 1)
        for h in range(HEADS):
            if h + 1 < HEADS:
                pe.wait_ge(s["E_ready"], (CH + 1) * (h + 1))
                broadcast(h + 1)
            for j in range(CH + 1):
                pe.wait_ge(s["S_ready"], (CH + 1) * h + j + 1)
                if h + 1 < HEADS:
                    dots(h + 1, j)
            if h >= 1:
                pe.wait_ge(s["num_kept"], h)
            for j in range(CH + 1):
                t0 = 0 if j == 0 else P * (j - 1)
                e = e_tile(h, j)
                rows = META if j == 0 else P
                pe.matmul(ps[0:HEADS, 3, t0:SEQ], m1["selcol"][0:rows, h * HEADS:(h + 1) * HEADS], e,
                          start=h == 0 and j == 0, stop=h == HEADS - 1 and j == CH, skip_group_check=True)
                vv = m1["v_meta"] if j == 0 else m1["v_real"][:, j - 1, :]
                ins = pe.matmul(ps[:, 1, t0:SEQ], vv[0:rows, h * P:(h + 1) * P], e, start=j == 0, stop=j == CH,
                                skip_group_check=True)
            ins.then_inc(s["num_done"], 1)
        pe.wait_ge(s["rden"], 2)
        for h in range(HEADS):
            if h >= 4:
                pe.wait_ge(s["y_ready"], h - 3)
            pe.matmul(ps[:, 4 + h % 4, :], m1["selrow"][:, h * P:(h + 1) * P], ga[:, META:TOK], start=True, stop=True) \
              .then_inc(s["rb_done"], 1)

    def pe_mix2(pe):
        s, u0 = a2, U_M2

        def swap(r):
            pe.wait_ge(s["raw_ready"], r + 4)
            if r >= 2:
                pe.wait_ge(s["swap_used"], r - 1)
            if r == 0:
                pe.wait_ge(s["const"], 96)
                ins = pe.matmul(ps[0:QK_DIM, 6, :], m2["permpe"][NOPE:QK_DIM, :], m2["kpe"][NOPE:QK_DIM, :], start=True, stop=True)
            else:
                x = (m2["rq"] if r < 5 else m2["rk"])[:, (r - 1) % 4, :]
                ins = pe.matmul(ps[:, 6 + r % 2, :], m2["perm"][:, :], x, start=True, stop=True)
            ins.then_inc(s["swapped"], 1)

        for e in range(12):
            pe.wait_ge(lo_done, u0 + e + 1)
            if e >= 2:
                pe.wait_ge(s["raw_ready"], e - 1)
            ready = 4 if e == 0 else None
            if e == 3:
                ins = project(pe, e % 2, SEQ, u0 + e, None, ROPE_DIM, ROPE_DIM)
            else:
                ins = project(pe, e % 2, SEQ, u0 + e, ready)
            ins.then_inc(unit_done, 1)
            if e == 2:
                for k in range(2):
                    pe.wait_ge(s["csq"], k + 1)
                    ins = pe.matmul(ps[:, 2, :], ones[:, :], sq[:, k * TOK:k * TOK + SEQ], start=k == 0, stop=k == 1)
                ins.then_inc(s["cstat"], 1)
            if e == 3:
                pe.wait_ge(s["csq"], 3)
                pe.matmul(ps[:, 3, :], ones[:, :], sq[:, 0:SEQ], start=True, stop=True).then_inc(s["cstat"], 1)
            if e >= 4:
                swap(e - 4)
        pe.wait_ge(s["croot"], 2)
        for j in range(4):
            pe.wait_ge(lo_done, u0 + 12 + j + 1)
            for kk in range(2):
                k = 2 * j + kk
                for c in range(CH):
                    ins = product(pe, [ps[:, 2 + c, :]], x_cols(k, META + P * c, P), [w_tile(u0 + 12 + j, kk, 512, 0, 512)],
                                  k == 0, k == KD - 1)
            ins.then_inc(unit_done, 1)
            if j == 0:
                swap(8)
        for m in range(4):
            pe.wait_ge(lo_done, u0 + 16 + m + 1)
            pe.wait_ge(s["raw_ready"], 11 + m)
            project(pe, m % 2, SEQ, u0 + 16 + m, None).then_inc(unit_done, 1)

        def dots(h, c):
            rows = slice(64 * (h % 2), 64 * (h % 2) + 64)
            pe.matmul(ps[:, 2 + c, :], m2["rk"][rows, h // 2, c * P:(c + 1) * P], m2["rq"][rows, h // 2, :],
                      start=True, stop=True).then_inc(s["dots"], 1)

        pe.wait_ge(s["rv_ready"], 4)
        pe.wait_ge(s["roped"], 9)
        pe.wait_ge(s["raw_ready"], 16)
        for c in range(CH):
            dots(0, c)
        for h in range(HEADS):
            m = h // 2
            rows = slice(64 * (h % 2), 64 * (h % 2) + 64)
            if h % 2 == 0 and m >= 2:
                pe.wait_ge(s["ob_ready"], m - 1)
            for c in range(CH):
                pe.wait_ge(s["RS_ready"], CH * h + c + 1)
                if h + 1 < HEADS:
                    dots(h + 1, c)
                pe.matmul(ps[rows, m % 2, :], m2["rv"][:, c, h * RET_DIM:(h + 1) * RET_DIM], m2["RS"][:, c, :],
                          start=c == 0, stop=c == CH - 1).then_inc(s["dec_used"], 1)
            if h % 2 == 1:
                pe.wait_ge(s["dec_used"], CH * (h + 1))
                pe.matmul(ps[0:1, 6, 0:2], ones[:, 0:1], ones[:, 0:2], start=True, stop=True).then_inc(s["o_done"], 1)
                pe.wait_ge(s["ob_ready"], m + 1)
                pe.matmul(ps[:, 6, :], m2["block"][:, :], wa[:, 0:SEQ], start=True, stop=True).then_inc(s["mean"], 1)
                pe.wait_ge(s["csq2"], m + 1)
                pe.matmul(ps[:, 7, :], m2["block"][:, :], sq[:, 0:SEQ], start=True, stop=True).then_inc(s["var"], 1)

    def pe_mla(pe):
        s, u0 = a3, U_M2 + 20
        rows = slice(NOPE, QK_DIM)

        def swap(h):
            pe.wait_ge(s["q_raw"], h + 1)
            if h >= 2:
                pe.wait_ge(s["q_ready"], h - 1)
            pe.matmul(ps[0:QK_DIM, 2 + h % 2, :], m3["permpe"][rows, :], m3["qT"][rows, h, :], start=True, stop=True) \
              .then_inc(s["swapped"], 1)

        pe.wait_ge(a2["csplit"], 3)
        for h in range(HEADS):
            u, hh = u0 + h // 4, h % 4
            if hh == 0:
                pe.wait_ge(lo_done, u + 1)
            if h >= 2:
                pe.wait_ge(s["q_raw"], h - 1)
            for k in range(2):
                ins = product(pe, [ps[0:QK_DIM, h % 2, :]], w_tile(u, k, 4 * QK_DIM, hh * QK_DIM, QK_DIM),
                              [[m2["cq_hi"][:, k, :], m2["cq_lo"][:, k, :]]], k == 0, k == 1)
            ins.then_inc(unit_done if hh == 3 else s["q_part"], 1)
            if h >= 1:
                swap(h - 1)
        swap(HEADS - 1)
        u = u0 + 2
        pe.wait_ge(lo_done, u + 1)
        lat = [m2["ckv_hi"][:, :], m2["ckv_lo"][:, :]]
        for h in range(HEADS):
            if h >= 2:
                pe.wait_ge(s["k_ready"], h - 1)
            product(pe, [ps[0:NOPE, 4 + h % 2, :]], w_tile(u, 0, UNIT, h * P, NOPE), [lat], True, True) \
                .then_inc(s["k_part"], 1)
        wv = [w[:, u % SLOTS, :].rearrange("p (h c) -> p h c", h=HEADS)[:, :, NOPE:NOPE + V_DIM] for w in (whi, wlo)]
        for c in range(CH):
            if c >= 2:
                pe.wait_ge(s["v_ready"], c - 1)
            o = ps[:, 6 + c % 2, :].rearrange("p (h c) -> p h c", h=HEADS)
            product(pe, [o], [x[:, c * P:(c + 1) * P] for x in lat], [wv], True, True) \
                .then_inc(s["v_part"] if c < CH - 1 else unit_done, 1)

        def dots(h):
            for c in range(CH):
                g = CH * h + c
                if g >= 2:
                    pe.wait_ge(s["P_exp"], g - 1)
                pe.matmul(ps[:, c % 2, :], m3["qT"][:, h, c * P:(c + 1) * P], m3["kT"][:, h, :], start=True, stop=True) \
                  .then_inc(s["dots"], 1)

        pe.wait_ge(s["q_ready"], HEADS)
        pe.wait_ge(s["k_ready"], HEADS)
        pe.wait_ge(s["kpe_ready"], 1)
        pe.wait_ge(s["v_ready"], CH)
        dots(0)
        for h in range(HEADS):
            if h >= 1:
                pe.wait_ge(s["PT_act"], 2 * h)
                pe.wait_ge(s["PT_dve"], 2 * h)
            for c in range(CH):
                pe.wait_ge(s["P_ready"], CH * h + c + 1)
                for k in range(CH):
                    ins = pe.transpose(ps[:, 2 + k, c * P:(c + 1) * P], m3["PR"][:, c * SEQ + k * P:c * SEQ + (k + 1) * P],
                                       ident[:, :])
            ins.then_inc(s["turned"], 1)
            if h + 1 < HEADS:
                dots(h + 1)
            m = h // 2
            if h % 2 == 0 and m >= 2:
                pe.wait_ge(s["o_split"], m - 1)
            for k in range(CH):
                pe.wait_ge(s["PT_act"] if k < 2 else s["PT_dve"], 2 * h + k % 2 + 1)
                ins = pe.matmul(ps[64 * (h % 2):64 * (h % 2) + 64, 6 + m % 2, :], m3["vm"][:, k, h * V_DIM:(h + 1) * V_DIM],
                                m3["PT"][:, k * SEQ:(k + 1) * SEQ], start=k == 0, stop=k == CH - 1)
            ins.then_inc(s["o_done"], 1)

    def prog_tensor(pe):
        pe.wait_ge(init["const"], 48)
        pe.wait_ge(init["vecs"], 16 * len(VEC_ROWS))
        pe.wait_ge(init["eps"], 2)
        pe.transpose(ps[0:16, 6, 0:16], ident[0:16, 0:16], ident[0:16, 0:16]).then_inc(unit_done, STARTED)
        pe.transpose(ps[:, 5, 0:NVEC], vrows[:, :], ident[0:NVEC, 0:NVEC]).then_inc(init["turned"], 1)
        pe.wait_ge(init["meta"], 16)
        for k in range(KD):
            ins = pe.transpose(ps[:, 4, k * META:(k + 1) * META], meta_tok[:, k * P:(k + 1) * P], ident[0:META, 0:META])
        ins.then_inc(init["turned"], 1)
        for c in range(CH):
            pe.wait_ge(init[f"x{c}"], 16)
        for k in range(KD):
            if k >= 4:
                pe.wait_ge(init["h_ready"], k - 2)
            for c in range(CH):
                ins = pe.transpose(ps[:, k % 4, c * P:(c + 1) * P], x_tok[:, c, k * P:(k + 1) * P], ident[:, :])
            ins.then_inc(init["turned"], 1)
        stat_tiles(pe, 0, TOK)
        pe_ffn(pe, 0, 0)
        stat_acc(pe, 0, TOK, res_s["stat"])
        stat_tiles(pe, 1, TOK)
        pe_mlstm(pe)
        pe_out(pe, 1, U_M1 + 25, range(KD), lambda k: (a1["y_split"], k + 1))
        stat_acc(pe, 1, SEQ, res_s["stat"])
        stat_tiles(pe, 2, SEQ)
        pe_ffn(pe, 1, 2)
        stat_acc(pe, 2, SEQ, res_s["stat"])
        stat_tiles(pe, 3, SEQ)
        pe_ffn(pe, 2, 3)
        stat_acc(pe, 3, SEQ, norm_s["sq_used"])
        pe_mix2(pe)
        pe_mla(pe)
        pe_out(pe, 4, U_M2 + 23, [4, 5, 6, 7, 0, 1, 2, 3],
               lambda k: (a3["o_split"], k + 1) if k < 4 else (a2["r_split"], k - 3))
        stat_acc(pe, 4, SEQ, norm_s["sq_used"])
        pe_ffn(pe, 3, 5)
        stat_acc(pe, 5, SEQ, norm_s["sq_used"])
        for c in range(CH):
            for j in range(2):
                g = 2 * c + j
                if g >= 4:
                    pe.wait_ge(fin_s["kept_act"], g - 3)
                for k in range(4):
                    pe.wait_ge(fin_s["t_ready"], 4 * j + k + 1)
                    ins = pe.transpose(ps[:, g % 4, k * P:(k + 1) * P], fin["fin"][:, 4 * j + k, c * P:(c + 1) * P], ident[:, :])
                ins.then_inc(fin_s["turned"], 1)

    with ctx:
        block = ctx.enter_context(nc.Block())

        @block.sync
        def _(sp):
            prog_sync(sp)

        @block.gpsimd
        def _(pool):
            prog_gpsimd(pool)

        @block.scalar
        def _(act):
            prog_scalar(act)

        @block.vector
        def _(v):
            prog_vector(v)

        @block.tensor
        def _(pe):
            prog_tensor(pe)


_UNUSED = {"b_w_in", "b_f_bias", "b_lb_raw", "b_g_norm", "b_w_out"}


def kernel(**inputs):
    import concourse.bacc as _bacc
    from concourse.bass_utils import run_bass_kernel_spmd as _run

    nc = _bacc.Bacc("TRN2", target_bir_lowering=False, num_devices=1)
    arrays, dram = {}, {}
    for name, value in inputs.items():
        a = np.ascontiguousarray(value)
        if name in _UNUSED or a.size == 0:
            continue
        arrays[f"in_{name}"] = a
        dram[name] = nc.dram_tensor(f"in_{name}", a.shape, mybir.dt.from_np(a.dtype), kind="ExternalInput").ap()
    arrays["in_const"] = constants()
    dram["const"] = nc.dram_tensor("in_const", (P, NCONST), F32, kind="ExternalInput").ap()
    out = nc.dram_tensor("out_0", (1, SEQ, D), F32, kind="ExternalOutput").ap()
    program(nc, dram, out)
    r = _run(nc, [arrays], core_ids=[0])
    return r.results[0]["out_0"]
```

```python
from contextlib import ExitStack

import numpy as np

import concourse.bass as bass
from concourse import mybir

F32 = mybir.dt.float32
F32R = mybir.dt.float32r
I32 = mybir.dt.int32
ACT = mybir.ActivationFunctionType
ALU = mybir.AluOpType
AX_X = mybir.AxisListType.X

P = 128
D = 1024
KD = D // P
META = 16
SEQ = 512
TOK = META + SEQ
HALF = TOK // 2
DFF = 2816
KF = DFF // P
EPS = 1e-6
CH = SEQ // P

HEADS = 8
A_DK = 64
A_QK = HEADS * A_DK
A_V = D
CONV = 4

Q_RANK, KV_RANK, ROPE_DIM, NOPE, V_DIM = 256, 128, 32, 64, 64
QK_DIM = NOPE + ROPE_DIM
MLA_SCALE = QK_DIM ** -0.5
RET_DIM = 64
RET = HEADS * RET_DIM
ROPE_THETA = 10000.0
WIN = SEQ + SEQ - P

SLOTS = 4
UNIT = 1024
STARTED = 1
AHEAD = SLOTS - 1

VEC_ROWS = [("norm_gains", 48), ("ffn1_norm_2", 8), ("mix_norm_2", 8), ("ffn2_norm_2", 8), ("final_norm_2", 8),
            ("q_norm_2", 2), ("kv_norm_2", 1), ("a_conv_b", 8), ("a_conv_w", 32)]
VEC = {}
_n = 0
for _name, _rows in VEC_ROWS:
    VEC[_name] = _n
    _n += _rows
NVEC = _n

CONST = {}
_n = 0
for _name, _cols in [("ident", P), ("ones", P), ("tri", P), ("selrow", HEADS * P), ("selcol", HEADS * HEADS),
                     ("perm", P), ("permpe", QK_DIM), ("block", P), ("invf", 2), ("relpos", WIN), ("relneg", WIN)]:
    CONST[_name] = slice(_n, _n + _cols)
    _n += _cols
NCONST = _n


def constants():
    c = np.zeros((P, NCONST), np.float32)
    p = np.arange(P)
    c[:, CONST["ident"]] = np.eye(P)
    c[:, CONST["ones"]] = 1.0
    c[:, CONST["tri"]] = p[None, :] >= p[:, None]
    for h in range(HEADS):
        c[h, CONST["selrow"].start + h * P:CONST["selrow"].start + (h + 1) * P] = 1.0
        c[:, CONST["selcol"].start + h * HEADS + h] = 1.0

    def swap(name, rows, half):
        for m in rows:
            first = (m % (2 * half)) < half
            c[m + half if first else m - half, CONST[name].start + m] = -1.0 if first else 1.0

    swap("perm", range(P), RET_DIM // 2)
    swap("permpe", range(NOPE, QK_DIM), ROPE_DIM // 2)
    for b in range(P // RET_DIM):
        rows = slice(b * RET_DIM, (b + 1) * RET_DIM)
        c[rows, CONST["block"].start + b * RET_DIM:CONST["block"].start + (b + 1) * RET_DIM] = 1.0 / RET_DIM

    def inv(half):
        return (np.float32(ROPE_THETA) ** (-np.arange(half, dtype=np.float32) / np.float32(half))).astype(np.float32)

    c[NOPE:QK_DIM, CONST["invf"].start] = np.tile(inv(ROPE_DIM // 2), 2)
    c[:, CONST["invf"].start + 1] = np.tile(inv(RET_DIM // 2), P // (RET_DIM // 2))
    rel = np.arange(WIN)[None, :] - (SEQ - P) - p[:, None]
    c[:, CONST["relpos"]] = np.maximum(rel, 0)
    c[:, CONST["relneg"]] = np.maximum(-rel, 0)
    return c


def program(nc, dram, out, stop=99):
    ctx = ExitStack()

    def sb(name, shape, dt=F32):
        return ctx.enter_context(nc.sbuf_tensor(name, shape, dt))

    def region(tensors):
        with ExitStack() as r:
            return {n: r.enter_context(nc.sbuf_tensor(n, s, dt)) for n, s, dt in tensors}

    def region_parts(first, parts):
        with ExitStack() as r:
            common = {n: r.enter_context(nc.sbuf_tensor(n, s, dt)) for n, s, dt in first}
            return [{**common, **region(part)} for part in parts]

    def sems(stage, names):
        return {n: ctx.enter_context(nc.semaphore(f"{stage}_{n}")) for n in names}

    hT = sb("hT", [P, KD * TOK])
    raw = sb("raw", [P, SLOTS, UNIT])
    whi = sb("whi", [P, SLOTS, UNIT], F32R)
    wlo = sb("wlo", [P, SLOTS, UNIT], F32R)
    wa = sb("wa", [P, 2 * TOK])
    wb = sb("wb", [P, 2 * TOK])
    sq = sb("sq", [P, 2 * TOK])
    acc = sb("acc", [P, TOK])
    rbc = sb("rbc", [P, TOK])
    vec = sb("vec", [P, NVEC])
    ident = sb("ident", [P, P])
    ones = sb("ones", [P, P])
    eps = sb("eps", [P, 1])
    halfpi = sb("halfpi", [P, 1])
    cell = sb("cell", [P, 4])
    rcol = sb("rcol", [P, CH + 1])
    diag = sq[:, 0:TOK]
    small = sb("small", [P, 32])
    gateb = sb("gateb", [HEADS, 2])
    with ExitStack() as r:
        ybuf = r.enter_context(nc.sbuf_tensor("ybuf", [P, KD * TOK], F32))
    xhi = sb("xhi", [P, KD * TOK], F32R)
    xlo = sb("xlo", [P, KD * TOK], F32R)
    t = region([("x_tok", [P, CH, D], F32), ("meta_tok", [META, D], F32), ("vrows", [NVEC, P], F32)])
    x_tok, meta_tok, vrows = t["x_tok"], t["meta_tok"], t["vrows"]
    t = region([("behind_inputs", [P, CH * D + D + P], F32), ("sqbuf", [P, KD * TOK], F32)])
    sqbuf = t["sqbuf"]
    t = region([("hid_hi", [P, KF * TOK], F32R), ("hid_lo", [P, KF * TOK], F32R)])
    hid_hi, hid_lo = t["hid_hi"], t["hid_lo"]
    EW = [SEQ] + [SEQ - P * c for c in range(CH)]
    EO = [sum(EW[:j]) for j in range(len(EW))]
    m1 = region([("qkT", [P, KD * TOK], F32), ("v_real", [P, CH, D], F32), ("v_meta", [META, D], F32),
                 ("og", [P, KD, SEQ], F32), ("num", [P, KD * TOK], F32), ("E", [P, 2 * sum(EW)], F32),
                 ("tri", [P, P], F32), ("selrow", [HEADS, HEADS * P], F32),
                 ("selcol", [P, HEADS * HEADS], F32), ("acol", [P, (CH + 1) * HEADS], F32)])
    shared = [("cq", [P, 2, SEQ], F32), ("cq_hi", [P, 2, SEQ], F32R), ("cq_lo", [P, 2, SEQ], F32R),
              ("ckv", [P, SEQ], F32), ("ckv_hi", [P, SEQ], F32R), ("ckv_lo", [P, SEQ], F32R),
              ("cosm", [P, SEQ], F32), ("sinm", [P, SEQ], F32), ("kpe", [P, SEQ], F32),
              ("permpe", [P, QK_DIM], F32)]
    m2, m3 = region_parts(shared, [[("cosr", [P, SEQ], F32), ("sinr", [P, SEQ], F32), ("perm", [P, P], F32),
                          ("invf", [P, 2], F32), ("lg", [P, 2 * HEADS], F32), ("lgt", [P, 2 * HEADS], F32),
                          ("rq", [P, 4, SEQ], F32), ("rk", [P, 4, SEQ], F32), ("rv", [P, CH, RET], F32),
                          ("relpos", [P, WIN], F32), ("relneg", [P, WIN], F32),
                          ("dec", [P, 2, WIN], F32), ("decb", [P, WIN], F32), ("RS", [P, CH, SEQ], F32),
                          ("rg", [P, 4, SEQ], F32), ("block", [P, P], F32)], [("qT", [QK_DIM, HEADS, SEQ], F32), ("kT", [QK_DIM, HEADS, SEQ], F32),
                          ("vm", [P, CH, RET], F32), ("PR", [P, 2, CH * SEQ], F32), ("PT", [P, CH * SEQ], F32)]])
    fin = region([("fin", [P, KD, SEQ], F32), ("otok", [P, CH, D], F32)])
    ps = ctx.enter_context(nc.psum_tensor("ps", [P, 8, 512], F32))

    def cols(n):
        return (0, TOK) if n == TOK else (META, SEQ)

    def tile(buf, k, n, start=0):
        o, w = cols(n)
        ap = buf[:, bass.ds(k * TOK + o, w)]
        return ap.rearrange("p (a n) -> p a n", a=2) if n == TOK else ap

    def bank(b, n, rows=P):
        return ps[0:rows, b:b + 2, 0:HALF] if n == TOK else ps[0:rows, b, :]

    def pieces(b, n):
        if n == TOK:
            return [(ps[:, b + c, 0:HALF], HALF * c, HALF) for c in range(2)]
        return [(ps[:, b, :], META, SEQ)]

    def gain(name, k):
        return vec[:, VEC[name] + k:VEC[name] + k + 1]

    def kcols(w, c0, n, k0=0, kn=KD):
        return w[k0 * P:(k0 + kn) * P, c0:c0 + n].rearrange("(k p) n -> p k n", p=P)

    FFN_PIECES = [(0, 8), (8, 8), (16, KF - 16)]
    NU_UP, NU_DOWN = 2 * KF, KD * len(FFN_PIECES)
    NU_FFN = NU_UP + NU_DOWN
    w1, w2 = dram["a_w_in"][0], dram["w_in_2"][0]
    VCOL = 2 * A_QK
    OCOL = VCOL + A_V
    GCOL = OCOL + A_V
    units1 = [kcols(w1, m * P, P) for m in range(8)] + [kcols(w1, GCOL, 2 * HEADS)]
    units1 += [kcols(w1, VCOL + 512 * n, 512, 2 * j, 2) for n in range(2) for j in range(4)]
    units1 += [kcols(w1, OCOL + m * P, P) for m in range(8)]
    units1 += [kcols(dram["a_w_out"][0], m * P, P) for m in range(8)]
    c_kv, c_kpe = Q_RANK, Q_RANK + KV_RANK
    c_rq = c_kpe + ROPE_DIM
    c_rk, c_rv, c_rg = c_rq + RET, c_rq + 2 * RET, c_rq + 3 * RET
    units2 = [kcols(w2, m * P, P) for m in range(2)] + [kcols(w2, c_kv, P), kcols(w2, c_kpe, ROPE_DIM)]
    units2 += [kcols(w2, c + m * P, P) for c in (c_rq, c_rk) for m in range(4)]
    units2 += [kcols(w2, c_rv, 512, 2 * j, 2) for j in range(4)]
    units2 += [kcols(w2, c_rg + m * P, P) for m in range(4)]
    units2 += [kcols(dram["w_uq_2"][0], 384 * j, 384, 0, 2) for j in range(2)]
    units2 += [kcols(dram["w_ukv_2"][0], 0, 1024, 0, 1)]
    units2 += [kcols(dram["w_o_2"][0], m * P, P) for m in range(8)]
    f_in, f_out = dram["ffn_w_in"][0], dram["ffn_w_out"][0]
    FFNS = [
        dict(gate=f_in[0], gc=0, up=f_in[0], uc=DFF, down=f_out[0], n=TOK, norm=("norm_gains", 0), post=8),
        dict(gate=f_in[1], gc=0, up=f_in[1], uc=DFF, down=f_out[1], n=SEQ, norm=("norm_gains", 32), post=40),
        dict(gate=dram["ffn1_w_gate_2"][0], gc=0, up=dram["ffn1_w_up_2"][0], uc=0, down=dram["ffn1_w_down_2"][0],
             n=SEQ, norm=("ffn1_norm_2", 0), post=None),
        dict(gate=dram["ffn2_w_gate_2"][0], gc=0, up=dram["ffn2_w_up_2"][0], uc=0, down=dram["ffn2_w_down_2"][0],
             n=SEQ, norm=("ffn2_norm_2", 0), post=None),
    ]
    U_M1 = NU_FFN
    FFNS[0]["u0"] = 0
    FFNS[1]["u0"] = U_M1 + len(units1)
    FFNS[2]["u0"] = FFNS[1]["u0"] + NU_FFN
    U_M2 = FFNS[2]["u0"] + NU_FFN
    FFNS[3]["u0"] = U_M2 + len(units2)
    UNITS = FFNS[3]["u0"] + NU_FFN
    assert UNITS % SLOTS == 0

    raw_loaded = [ctx.enter_context(nc.semaphore(f"raw_loaded{s}")) for s in range(SLOTS)]
    hi_done, lo_done, unit_done, unused = (ctx.enter_context(nc.semaphore(n))
                                           for n in ("hi_done", "lo_done", "unit_done", "unused"))

    def slot_view(buf, u, a, n):
        return buf[:, u % SLOTS, 0:a * n].rearrange("p (a n) -> p a n", a=a)

    init = sems("init", ["x0", "x1", "x2", "x3", "meta", "vecs", "const", "turned", "h_ready", "eps"])
    NORM = ["sq_ready", "summed", "hi_ready", "x_ready"]
    OUTP = ["v_ready", "sq_ready", "acc_done"]
    norm_s, out_s = sems("norm", NORM), sems("out", OUTP)
    res_s = sems("res", ["t_ready", "h_ready"])
    ffn_s = sems("ffn", ["gate_scaled", "silu_done", "banks_free", "product", "hi_ready", "hid_ready"])
    r_s = sems("rms", ["sums", "root", "recip", "diag", "spread", "ready"])
    norm_at = [dict(sq_ready=KD * i, summed=i, hi_ready=KD * i, x_ready=KD * i) for i in range(6)]
    out_at = [dict(v_ready=(KD + 2) * i, sq_ready=KD * i, acc_done=(KD + 2) * i) for i in range(6)]
    res_at = [dict(t_ready=KD * i, h_ready=KD * i) for i in range(3)]
    ffn_at = [dict(gate_scaled=KF * i, silu_done=KF * i, banks_free=(KF + 2) * i, product=KF * i, hi_ready=KF * i,
                   hid_ready=(KF + 2) * i) for i in range(4)]
    N0, R0, N1, R1, N2, R2, N3, N4, N5, N6 = range(10)
    R_TOK = {N0: TOK, R0: TOK, N1: TOK}
    r_at = [dict(sums=i, root=i, recip=i, diag=i, spread=i,
                 ready=sum(2 if j in R_TOK else 1 for j in range(i))) for i in range(10)]
    a1 = sems("mlstm", ["const", "z_ready", "conv_done", "qk_ready", "pad", "gates_read", "neg_abs", "softplus",
                        "nm_ready", "em_ready", "v_ready", "og_raw", "og_ready", "a_turned", "acol_ready", "bc_done",
                        "E_ready", "dots", "S_ready", "num_done", "num_kept", "rden", "rb_done", "y_ready",
                        "y_hi", "y_split"])
    a2 = sems("mix2", ["const", "pos", "decay", "raw_ready", "swapped", "swap_used", "roped", "angle", "trig",
                       "csq", "cstat", "croot", "cnorm", "chi", "csplit", "rg_ready", "rv_ready", "lg1", "lg2", "lg_ready",
                       "arg", "dec_ready", "dots", "RS_ready", "o_done", "ob_ready", "mean", "cent", "csq2",
                       "var", "rroot", "r_ready", "r_hi", "r_split", "dec_used"])
    a3 = sems("mla", ["q_part", "q_raw", "swapped", "q_ready", "k_part", "k_ready", "kpe_ready", "v_part",
                      "v_ready", "dots", "max_ready", "P_exp", "P_ready", "turned", "PT_act", "PT_dve",
                      "o_done", "o_hi", "o_split"])
    fin_s = sems("fin", ["t_ready", "turned", "kept_act", "stored"])
    steps = {e: ctx.enter_context(nc.semaphore(f"{e}_step")) for e in ("dve", "act")}
    step_count = {"dve": 0, "act": 0}

    def link(e, name, ins):
        step_count[name] += 1
        ins.then_inc(steps[name], 1)
        e.wait_ge(steps[name], step_count[name])

    def load_ffn(sp, f):
        u0 = f["u0"]
        first = 0
        if u0 == 0:
            for j in range(SLOTS):
                src = kcols(f["gate"] if j % 2 == 0 else f["up"], (f["gc"] if j % 2 == 0 else f["uc"]) + (j // 2) * P, P)
                sp.dma_start(slot_view(raw, j, KD, P), src).then_inc(raw_loaded[j], 16)
            first = 1
        with sp.Fori(first, KF // 2) as i:
            for j in range(4):
                u = u0 + j
                sp.wait_ge(lo_done, 4 * i + (u - SLOTS + 1))
                w, c = (f["gate"], f["gc"]) if j % 2 == 0 else (f["up"], f["uc"])
                src = w.rearrange("(k p) n -> p k n", p=P)[:, :, bass.ds(i * (2 * P) + (c + (j // 2) * P), P)]
                sp.dma_start(slot_view(raw, u, KD, P), src).then_inc(raw_loaded[u % SLOTS], 16)
        u0 += NU_UP
        with sp.Fori(0, 2) as i:
            for j in range(4):
                for q, (k0, kn) in enumerate(FFN_PIECES):
                    u = u0 + 3 * j + q
                    sp.wait_ge(lo_done, 12 * i + (u - SLOTS + 1))
                    src = f["down"][k0 * P:(k0 + kn) * P, :].rearrange("(k p) n -> p k n", p=P)
                    sp.dma_start(slot_view(raw, u, kn, P), src[:, :, bass.ds(i * (4 * P) + j * P, P)]) \
                      .then_inc(raw_loaded[u % SLOTS], 16)

    def load_units(sp, u0, units):
        for j, src in enumerate(units):
            u = u0 + j
            sp.wait_ge(lo_done, u - SLOTS + 1)
            sp.dma_start(slot_view(raw, u, src.shape[1], src.shape[2]), src).then_inc(raw_loaded[u % SLOTS], 16)

    def prog_sync(sp):
        for c in range(CH):
            sp.dma_start(x_tok[:, c, :], dram["x"][0, c * P:(c + 1) * P, :]).then_inc(init[f"x{c}"], 16)
        load_ffn(sp, FFNS[0])
        load_units(sp, U_M1, units1)
        load_ffn(sp, FFNS[1])
        load_ffn(sp, FFNS[2])
        load_units(sp, U_M2, units2)
        load_ffn(sp, FFNS[3])
        for c in range(CH):
            sp.wait_ge(fin_s["kept_act"], 2 * (c + 1))
            sp.dma_start(out[0, c * P:(c + 1) * P, :], fin["otok"][:, c, :]).then_inc(fin_s["stored"], 16)
        sp.wait_ge(fin_s["stored"], 16 * CH)

    def pool_lo(pool, u0, u1):
        def lo(u, r=0):
            pool.wait_ge(hi_done, SLOTS * r + (u + 1))
            pool.tensor_tensor(wlo[:, u % SLOTS, :], raw[:, u % SLOTS, :], whi[:, u % SLOTS, :].bitcast(F32),
                               ALU.subtract).then_inc(lo_done, 1)

        whole = (u1 - u0) // SLOTS
        if whole > 0:
            with pool.Fori(0, whole) as r:
                for j in range(SLOTS):
                    lo(u0 + j, r)
        for u in range(u0 + whole * SLOTS, u1):
            lo(u)

    def pool_res(pool, i, n):
        for k in range(KD):
            pool.wait_ge(res_s["t_ready"], res_at[i]["t_ready"] + k + 1)
            pool.tensor_tensor(tile(hT, k, n), tile(hT, k, n), tile(wa, k % 2, n), ALU.add).then_inc(res_s["h_ready"], 1)

    def pool_decays(pool, h):
        dec = m2["dec"][:, h % 2, :]
        pool.wait_ge(a2["arg"], 2 * (h + 1))
        pool.tensor_tensor(dec, dec, m2["decb"][:, :], ALU.mult).then_inc(a2["dec_ready"], 1)

    def prog_gpsimd(pool):
        u = 0
        for i, (start, n) in enumerate(((U_M1, TOK), (FFNS[1]["u0"], SEQ), (FFNS[2]["u0"], SEQ))):
            pool_lo(pool, u, start + AHEAD)
            u = start + AHEAD
            pool_res(pool, i, n)
        pool_lo(pool, u, U_M2 + 20 + AHEAD - 1)
        for h in range(HEADS):
            pool_decays(pool, h)
        pool_lo(pool, U_M2 + 20 + AHEAD - 1, UNITS)

    cursor = [0]

    def split_hi(act, u, reg=None, stride=0):
        s = u % SLOTS
        if reg is None:
            if u >= UNITS:
                return
            act.wait_ge(raw_loaded[s], 16 * (u // SLOTS + 1))
            if u >= SLOTS:
                act.wait_ge(unit_done, STARTED + u - SLOTS + 1)
        else:
            act.wait_ge(raw_loaded[s], reg * (16 * stride // SLOTS) + 16 * (u // SLOTS + 1))
            act.wait_ge(unit_done, STARTED + reg * stride + (u - SLOTS + 1))
        act.activation(whi[:, s, :], raw[:, s, :], ACT.Copy).then_inc(hi_done, 1)

    def split_to(act, last):
        while cursor[0] <= min(last + AHEAD, UNITS - 1):
            split_hi(act, cursor[0])
            cursor[0] += 1

    def act_root(act, i):
        at, n = r_at[i], R_TOK.get(i, SEQ)
        c0 = 0 if n == TOK else 1
        act.wait_ge(r_s["sums"], at["sums"] + 1)
        act.activation(rcol[:, c0:], ps[:, 7, c0:CH + 1], ACT.Sqrt, scale=1.0 / D, bias=eps[:, :]) \
           .then_inc(r_s["root"], 1)
        if i == N6:
            return
        act.wait_ge(r_s["spread"], at["spread"] + 1)
        act.activation(rbc[:, META:TOK], ps[:, 6, :], ACT.Copy).then_inc(r_s["ready"], 1)
        if n == TOK:
            act.activation(rbc[:, 0:META], ps[:, 7, 16:16 + META], ACT.Copy).then_inc(r_s["ready"], 1)

    def act_norm(act, i, n, source, offset, squares, name, g0):
        s, at = norm_s, norm_at[i]
        for k in range(KD):
            act.wait_ge(source, offset + k + 1)
            act.activation(tile(xhi, k, n), tile(hT, k, n), ACT.Copy, scale=gain(name, g0 + k)) \
               .then_inc(s["hi_ready"], 1)
            if squares:
                act.activation(tile(sqbuf, k, n), tile(hT, k, n), ACT.Square).then_inc(s["sq_ready"], 1)

    def act_ffn(act, i):
        f, s, at = FFNS[i], ffn_s, ffn_at[i]
        n, u0 = f["n"], f["u0"]

        def gated(r, b):
            act.wait_ge(s["gate_scaled"], at["gate_scaled"] + r * 2 + (b + 1))
            act.activation(tile(wa, b, n), tile(wa, b, n), ACT.Silu).then_inc(s["silu_done"], 1)
            act.wait_ge(s["product"], at["product"] + r * 2 + (b + 1))
            act.activation(tile(hid_hi, r * 2 + b, n), tile(wb, b, n), ACT.Copy).then_inc(s["hi_ready"], 1)

        for b in range(2):
            split_to(act, u0 + 2 * b + 1)
            gated(0, b)
        with act.Fori(1, KF // 2) as r:
            for b in range(2):
                for e in (2 * b + AHEAD, 2 * b + AHEAD + 1):
                    split_hi(act, u0 + e, r, 4)
                gated(r, b)
        cursor[0] += NU_UP - 4

    def act_out(act, i, n, add, u0, per):
        s, at = out_s, out_at[i]
        split_to(act, u0 - 1)

        def square(d, j):
            act.wait_ge(s["acc_done"], at["acc_done"] + d + (j + 1))
            if add:
                act.wait_ge(s["v_ready"], at["v_ready"] + d + (j + 3))
                value = tile(hT, d + j, n)
            else:
                act.wait_ge(unit_done, STARTED + d * per + (u0 + per * (j + 1)))
                value = out_bank(i, j % 4, n)
            act.activation(tile(sq, j % 2, n), value, ACT.Square).then_inc(s["sq_ready"], 1)

        if u0 + 8 * per >= UNITS:
            for j in range(KD):
                split_to(act, u0 + per * (j + 1) - 1)
                square(0, j)
            return
        with act.Fori(0, 2) as r:
            for j in range(4):
                for e in range(per):
                    split_hi(act, u0 + per * j + AHEAD + e, r, 4 * per)
                square(r * 4, j)
        cursor[0] += 8 * per

    def act_mlstm(act):
        s, u0 = a1, U_M1
        for m in range(8):
            split_to(act, u0 + m)
            if m >= 1:
                act.wait_ge(s["conv_done"], m)
                act.activation(m1["qkT"][:, (m - 1) * TOK:m * TOK], cacc((m - 1) % 2), ACT.Silu) \
                   .then_inc(s["qk_ready"], 1)
        act.wait_ge(s["conv_done"], 8)
        act.activation(m1["qkT"][:, 7 * TOK:8 * TOK], cacc(1), ACT.Silu).then_inc(s["qk_ready"], 1)
        split_to(act, u0 + 8)
        act.wait_ge(s["neg_abs"], 1)
        link(act, "act", act.activation(gc, gc, ACT.Exp))
        act.activation(gc, gc, ACT.Ln, bias=ones[0:HEADS, 0:1]).then_inc(s["softplus"], 1)
        for n in range(2):
            split_to(act, u0 + 9 + 4 * n + 3)
            act.wait_ge(unit_done, STARTED + u0 + 9 + 4 * n + 4)
            for c in V_ORDER:
                dst = m1["v_meta"][:, n * 512:(n + 1) * 512] if c < 0 else m1["v_real"][:, c, n * 512:(n + 1) * 512]
                b = V_BANK[n][c]
                rows = META if c < 0 else P
                act.activation(dst, ps[0:rows, b, :], ACT.Copy, scale=rcol[0:rows, c + 1 if c >= 0 else 0:c + 2 if c >= 0 else 1]) \
                   .then_inc(s["v_ready"], 1)
        act.wait_ge(s["nm_ready"], 1)
        act.activation(gc, gc, ACT.Exp, scale=-1.0).then_inc(s["em_ready"], 1)
        for m in range(8):
            split_to(act, u0 + 17 + m)
            act.wait_ge(s["og_raw"], m + 1)
            act.activation(m1["og"][:, m, :], m1["og"][:, m, :], ACT.Sigmoid).then_inc(s["og_ready"], 1)
        act.wait_ge(s["acol_ready"], 1)
        for h in range(HEADS):
            act.wait_ge(s["bc_done"], h + 1)
            if h >= 2:
                act.wait_ge(s["num_done"], h - 1)
            for j in range(CH + 1):
                rows, t0 = (META, 0) if j == 0 else (P, P * (j - 1))
                act.activation(e_tile(h, j), ps[0:rows, 0, t0:SEQ], ACT.Exp,
                               bias=m1["acol"][0:rows, j * HEADS + h:j * HEADS + h + 1]).then_inc(s["E_ready"], 1)
        for h in range(HEADS):
            act.wait_ge(s["y_ready"], h + 1)
            act.activation(tile(xhi, h, SEQ), tile(wb, h % 2, SEQ), ACT.Copy).then_inc(s["y_hi"], 1)

    def act_mix2(act):
        s, u0 = a2, U_M2
        act.wait_ge(s["lg1"], 1)
        link(act, "act", act.activation(m2["lgt"][:, :], m2["lgt"][:, :], ACT.Exp))
        act.activation(m2["lgt"][:, :], m2["lgt"][:, :], ACT.Ln, bias=ones[:, 0:1]).then_inc(s["lg2"], 1)
        for e in range(12):
            split_to(act, u0 + e)
            if e == 1:
                for k in range(2):
                    act.wait_ge(s["raw_ready"], k + 1)
                    act.activation(sq[:, k * TOK:k * TOK + SEQ], m2["cq"][:, k, :], ACT.Square).then_inc(s["csq"], 1)
            if e == 2:
                act.wait_ge(s["raw_ready"], 3)
                act.wait_ge(s["cstat"], 1)
                act.activation(sq[:, 0:SEQ], m2["ckv"][:, :], ACT.Square).then_inc(s["csq"], 1)
            if e == 4:
                for j, (co, si) in enumerate((("cosm", "sinm"), ("cosr", "sinr"))):
                    act.wait_ge(s["angle"], 2 * j + 2)
                    act.activation(m2[si][:, :], m2[si][:, :], ACT.Sin).then_inc(s["trig"], 1)
                    act.activation(m2[co][:, :], m2[co][:, :], ACT.Sin, scale=-1.0, bias=halfpi[:, :]) \
                       .then_inc(s["trig"], 1)
            if e == 5:
                for j, rank in enumerate((Q_RANK, KV_RANK)):
                    act.wait_ge(s["cstat"], j + 1)
                    inv = wb[:, j * TOK:j * TOK + SEQ]
                    link(act, "act", act.activation(inv, ps[:, 2 + j, :], ACT.Ln, scale=1.0 / rank, bias=eps[:, :]))
                    act.activation(inv, inv, ACT.Exp, scale=-0.5).then_inc(s["croot"], 1)
            if e == 8:
                for k in range(3):
                    act.wait_ge(s["cnorm"], k + 1)
                    act.activation(m2["cq_hi"][:, k, :] if k < 2 else m2["ckv_hi"][:, :],
                                   m2["cq"][:, k, :] if k < 2 else m2["ckv"][:, :], ACT.Copy).then_inc(s["chi"], 1)
        split_to(act, u0 + 15)
        act.wait_ge(unit_done, STARTED + u0 + 16)
        for c in range(CH):
            act.activation(m2["rv"][:, c, :], ps[:, 2 + c, :], ACT.Copy, scale=rcol[:, c + 1:c + 2]) \
               .then_inc(s["rv_ready"], 1)
        for m in range(4):
            split_to(act, u0 + 16 + m)
            act.wait_ge(s["raw_ready"], 13 + m)
            act.activation(m2["rg"][:, m, :], m2["rg"][:, m, :], ACT.Silu).then_inc(s["rg_ready"], 1)
        act.wait_ge(s["lg_ready"], 1)
        def decays(h):
            if h >= 1:
                act.wait_ge(s["dec_ready"], h)
            if h >= 2:
                act.wait_ge(s["RS_ready"], CH * (h - 1))
            act.activation(m2["dec"][:, h % 2, :], m2["relpos"][:, :], ACT.Exp, scale=m2["lg"][:, h:h + 1]) \
               .then_inc(s["arg"], 1)
            act.activation(m2["decb"][:, :], m2["relneg"][:, :], ACT.Exp, scale=m2["lg"][:, HEADS + h:HEADS + h + 1]) \
               .then_inc(s["arg"], 1)

        for h in range(3):
            decays(h)
        for h in range(2, HEADS + 1):
            m = h // 2 - 1
            if h % 2 == 0:
                act.wait_ge(s["o_done"], m + 1)
                act.activation(tile(wa, m % 2, SEQ), ps[:, m % 2, :], ACT.Copy).then_inc(s["ob_ready"], 1)
            if h + 1 < HEADS:
                decays(h + 1)
            if h % 2 == 0:
                act.wait_ge(s["cent"], m + 1)
                act.activation(tile(sq, m % 2, SEQ), tile(wa, m % 2, SEQ), ACT.Square).then_inc(s["csq2"], 1)
            else:
                act_deviation(act, m)
                act_ret_hi(act, m)

    def act_deviation(act, m):
        act.wait_ge(a2["var"], m + 1)
        link(act, "act", act.activation(rbc[:, 0:SEQ], ps[:, 7, :], ACT.Ln, bias=eps[:, :]))
        act.activation(rbc[:, 0:SEQ], rbc[:, 0:SEQ], ACT.Exp, scale=-0.5).then_inc(a2["rroot"], 1)

    def act_ret_hi(act, m):
        act.wait_ge(a2["r_ready"], m + 1)
        act.activation(tile(xhi, 4 + m, SEQ), tile(wa, m % 2, SEQ), ACT.Copy).then_inc(a2["r_hi"], 1)

    def act_mla(act):
        s, u0 = a3, U_M2 + 20
        act.wait_ge(a2["dec_used"], CH * HEADS)
        for h in range(HEADS):
            if h == 1:
                act_deviation(act, 3)
            if h == 3:
                act_ret_hi(act, 3)
            split_to(act, u0 + h // 4)
            if h % 4 == 3:
                act.wait_ge(unit_done, STARTED + u0 + h // 4 + 1)
            else:
                act.wait_ge(s["q_part"], 3 * (h // 4) + h % 4 + 1)
            act.activation(m3["qT"][:, h, :], ps[0:QK_DIM, h % 2, :], ACT.Copy).then_inc(s["q_raw"], 1)
        for h in range(HEADS):
            act.wait_ge(s["k_part"], h + 1)
            act.activation(m3["kT"][0:NOPE, h, :], ps[0:NOPE, 4 + h % 2, :], ACT.Copy).then_inc(s["k_ready"], 1)
        for c in range(CH):
            if c < CH - 1:
                act.wait_ge(s["v_part"], c + 1)
            else:
                act.wait_ge(unit_done, STARTED + u0 + 3)
            act.activation(m3["vm"][:, c, :], ps[:, 6 + c % 2, :], ACT.Copy).then_inc(s["v_ready"], 1)
        split_to(act, u0 + 2)

        def scores_exp(h, c):
            if h >= 2:
                act.wait_ge(s["turned"], CH * (h - 2) + c + 1)
            act.wait_ge(s["max_ready"], CH * h + c + 1)
            act.activation(m3["PR"][:, h % 2, c * SEQ:(c + 1) * SEQ], ps[:, c % 2, :], ACT.Exp, scale=MLA_SCALE,
                           bias=small[:, c:c + 1], accum_out=small[:, 8 + c:9 + c]).then_inc(s["P_exp"], 1)

        def keep_turned(h, c):
            if h >= 1:
                act.wait_ge(s["o_done"], h)
            act.wait_ge(s["turned"], CH * h + c + 1)
            act.activation(m3["PT"][:, c * SEQ:(c + 1) * SEQ], ps[:, 2 + c, :], ACT.Copy).then_inc(s["PT_act"], 1)

        def out_hi(m):
            act.wait_ge(s["o_done"], 2 * m + 2)
            act.activation(tile(xhi, m, SEQ), ps[:, 6 + m % 2, :], ACT.Copy).then_inc(s["o_hi"], 1)

        for c in range(CH):
            scores_exp(0, c)
        for h in range(HEADS):
            if h + 1 < HEADS:
                scores_exp(h + 1, 0)
            keep_turned(h, 0)
            if h % 2 == 0 and h >= 2:
                out_hi(h // 2 - 1)
            if h + 1 < HEADS:
                scores_exp(h + 1, 1)
                scores_exp(h + 1, 2)
            keep_turned(h, 2)
            keep_turned(h, 3)
            if h + 1 < HEADS:
                scores_exp(h + 1, 3)
        out_hi(HEADS // 2 - 1)

    def prog_scalar(act):
        act.dma_start(meta_tok[:, :], dram["meta_tokens"]).then_inc(init["meta"], 16)
        act.dma_start(ident[:, :], dram["const"][:, CONST["ident"]]).then_inc(init["const"], 16)
        act.dma_start(ones[:, :], dram["const"][:, CONST["ones"]]).then_inc(init["const"], 16)
        act.dma_start(gateb[:, :], dram["a_gate_b"].rearrange("a (t h) -> h (a t)", t=2),
                      allow_slow_non_contiguous=True).then_inc(init["const"], 16)
        rows = {
            "norm_gains": dram["norm_gains"].rearrange("a g (k p) -> (a g k) p", p=P),
            "a_conv_w": dram["a_conv_w"].rearrange("a j (k p) -> (a j k) p", p=P),
            "final_norm_2": dram["final_norm_2"].rearrange("(k p) -> k p", p=P),
        }
        for name, n in VEC_ROWS:
            src = rows[name] if name in rows else dram[name].rearrange("a (k p) -> (a k) p", p=P)
            act.dma_start(vrows[VEC[name]:VEC[name] + n, :], src).then_inc(init["vecs"], 16)
        split_to(act, -1)
        act_norm(act, 0, TOK, init["h_ready"], 1, True, "norm_gains", 0)
        split_to(act, FFNS[0]["u0"])
        act_root(act, N0)
        act_ffn(act, 0)
        act_out(act, 0, TOK, False, NU_UP, 3)
        act_root(act, R0)
        act_norm(act, 1, TOK, res_s["h_ready"], res_at[0]["h_ready"], True, "norm_gains", 16)
        split_to(act, U_M1)
        act_root(act, N1)
        for name in ("tri", "selcol"):
            act.dma_start(m1[name][:, :], dram["const"][:, CONST[name]]).then_inc(a1["const"], 16)
        act.dma_start(m1["selrow"][:, :], dram["const"][0:HEADS, CONST["selrow"]]).then_inc(a1["const"], 16)
        act_mlstm(act)
        act_out(act, 1, SEQ, False, U_M1 + 25, 1)
        act_root(act, R1)
        act_norm(act, 2, SEQ, res_s["h_ready"], res_at[1]["h_ready"], True, "norm_gains", 32)
        split_to(act, FFNS[1]["u0"])
        act_root(act, N2)
        act_ffn(act, 1)
        act_out(act, 2, SEQ, False, FFNS[1]["u0"] + NU_UP, 3)
        act_root(act, R2)
        act_norm(act, 3, SEQ, res_s["h_ready"], res_at[2]["h_ready"], True, "ffn1_norm_2", 0)
        split_to(act, FFNS[2]["u0"])
        act_root(act, N3)
        act_ffn(act, 2)
        act_out(act, 3, SEQ, True, FFNS[2]["u0"] + NU_UP, 3)
        act_norm(act, 4, SEQ, out_s["v_ready"], out_at[3]["v_ready"] + 2, False, "mix_norm_2", 0)
        split_to(act, U_M2)
        act_root(act, N4)
        for name in ("permpe", "perm", "block", "invf", "relpos", "relneg"):
            act.dma_start(m2[name][:, :], dram["const"][:, CONST[name]]).then_inc(a2["const"], 16)
        act.dma_start(m2["RS"][:, 0, :].bitcast(I32), dram["positions_2"].broadcast_to([P, SEQ])) \
           .then_inc(a2["pos"], 16)
        for j, name in enumerate(("ret_decay_fwd_2", "ret_decay_bwd_2")):
            act.dma_start(m2["lg"][:, j * HEADS:(j + 1) * HEADS], dram[name].broadcast_to([P, HEADS])) \
               .then_inc(a2["decay"], 16)
        act_mix2(act)
        act_mla(act)
        act_out(act, 4, SEQ, True, U_M2 + 23, 1)
        act_norm(act, 5, SEQ, out_s["v_ready"], out_at[4]["v_ready"] + 2, False, "ffn2_norm_2", 0)
        split_to(act, FFNS[3]["u0"])
        act_root(act, N5)
        act_ffn(act, 3)
        act_out(act, 5, SEQ, True, FFNS[3]["u0"] + NU_UP, 3)
        act_root(act, N6)
        act.wait_ge(r_s["recip"], r_at[N6]["recip"] + 1)
        for c in range(CH):
            for j in range(2):
                g = 2 * c + j
                act.wait_ge(fin_s["turned"], g + 1)
                act.activation(fin["otok"][:, c, j * 512:(j + 1) * 512], ps[:, g % 4, :], ACT.Copy,
                               scale=rcol[:, c + 1:c + 2]) \
                   .then_inc(fin_s["kept_act"], 1)

    def zpad(b):
        return m1["E"][:, b * 532:b * 532 + 3 + TOK]

    def cacc(b):
        return m1["E"][:, 1064 + b * TOK:1064 + (b + 1) * TOK]

    def e_tile(h, j):
        o = (h % 2) * sum(EW) + EO[j]
        return m1["E"][0:META if j == 0 else P, o:o + EW[j]]

    ga, gb = wa[0:HEADS, 0:TOK], wa[0:HEADS, TOK:2 * TOK]
    gc, go = wb[0:HEADS, 0:TOK], wb[0:HEADS, TOK:2 * TOK]
    V_ORDER = [0, -1, 1, 2, 3]
    V_BANK = [{0: 0, 1: 1, 2: 2, 3: 3, -1: 4}, {0: 5, 1: 6, 2: 7, 3: 0, -1: 4}]
    QK_BANK = [4, 5, 6, 7, 2]

    def dve_rms(v, i):
        s, at, n = r_s, r_at[i], R_TOK.get(i, SEQ)
        c0 = 0 if n == TOK else 1
        v.wait_ge(s["root"], at["root"] + 1)
        v.reciprocal(rcol[:, c0:], rcol[:, c0:]).then_inc(s["recip"], 1)
        if i == N6:
            return
        v.wait_ge(s["recip"], at["recip"] + 1)
        if n == TOK:
            v.tensor_scalar(diag[0:META, 0:META], ident[0:META, 0:META], rcol[0:META, 0:1], None, ALU.mult)
        for c in range(CH):
            ins = v.tensor_scalar(diag[:, META + c * P:META + (c + 1) * P], ident[:, :], rcol[:, c + 1:c + 2], None, ALU.mult)
        ins.then_inc(s["diag"], 1)

    def r_ready(v, i):
        v.wait_ge(r_s["ready"], r_at[i]["ready"] + (2 if i in R_TOK else 1))

    def lo_of_x(v, i, k, n, name, g0):
        v.wait_ge(norm_s["hi_ready"], norm_at[i]["hi_ready"] + k + 1)
        v.scalar_tensor_tensor(out=tile(xlo, k, n), in0=tile(hT, k, n), scalar=gain(name, g0 + k),
                               in1=tile(xhi, k, n).bitcast(F32), op0=ALU.mult, op1=ALU.subtract) \
         .then_inc(norm_s["x_ready"], 1)

    def sum_square(v, i, k, n):
        v.wait_ge(norm_s["sq_ready"], norm_at[i]["sq_ready"] + k + 1)
        ins = v.tensor_tensor(tile(acc, 0, n), tile(sqbuf if k == 1 else acc, 0, n), tile(sqbuf, k, n), ALU.add)
        if k < KD - 1:
            link(v, "dve", ins)
        else:
            ins.then_inc(norm_s["summed"], 1)

    def dve_norm(v, i, n, name, g0, squares=False):
        for k in range(KD):
            lo_of_x(v, i, k, n, name, g0)
            if squares and k >= 1:
                sum_square(v, i, k, n)

    def dve_ffn(v, i, rms):
        f, s, at, n, u0 = FFNS[i], ffn_s, ffn_at[i], FFNS[i]["n"], FFNS[i]["u0"]
        r_ready(v, rms)
        with v.Fori(0, KF // 2) as r:
            for b in range(2):
                v.wait_ge(unit_done, STARTED + r * 4 + (u0 + 2 * b + 1))
                v.wait_ge(s["banks_free"], at["banks_free"] + r * 2 + (b + 1))
                v.tensor_tensor(tile(wa, b, n), bank(2 * b if n == TOK else b, n), tile(rbc, 0, n), ALU.mult) \
                 .then_inc(s["gate_scaled"], 1)
                v.wait_ge(s["silu_done"], at["silu_done"] + r * 2 + (b + 1))
                v.wait_ge(unit_done, STARTED + r * 4 + (u0 + 2 * b + 2))
                v.wait_ge(s["hid_ready"], at["hid_ready"] + r * 2 + (b + 1))
                v.tensor_tensor(tile(wb, b, n), tile(wa, b, n), bank(4 + 2 * b if n == TOK else 2 + b, n), ALU.mult) \
                 .then_inc(s["banks_free"], 1)
                v.wait_ge(s["banks_free"], at["banks_free"] + r * 2 + (b + 3))
                v.tensor_tensor(tile(wb, b, n), tile(wb, b, n), tile(rbc, 0, n), ALU.mult).then_inc(s["product"], 1)
                v.wait_ge(s["hi_ready"], at["hi_ready"] + r * 2 + (b + 1))
                v.tensor_tensor(tile(hid_lo, r * 2 + b, n), tile(wb, b, n),
                                tile(hid_hi, r * 2 + b, n).bitcast(F32), ALU.subtract).then_inc(s["hid_ready"], 1)

    def free_ffn(v):
        v.memset(cell[:, 0:1], 0.0).then_inc(ffn_s["banks_free"], 2)
        v.memset(cell[:, 1:2], 0.0).then_inc(ffn_s["hid_ready"], 2)

    def free_out(v, i, n):
        v.memset(tile(acc, 0, n), 0.0).then_inc(out_s["acc_done"], 2)
        v.memset(cell[:, 2:3], 0.0).then_inc(out_s["v_ready"], 2)

    def dve_out(v, i, n, value, u0, per, gains=None, add=None):
        s, at = out_s, out_at[i]
        with v.Fori(0, 2) as r:
            for j in range(4):
                if add is None:
                    g0, factor = gains
                    v.wait_ge(s["sq_ready"], at["sq_ready"] + r * 4 + (j + 1))
                    g = vec[:, bass.ds(r * 4 + (VEC["norm_gains"] + g0 + j), 1)]
                    v.tensor_scalar(tile(value, r * 4 + j, n), out_bank(i, j, n), g, factor, ALU.mult, ALU.mult) \
                     .then_inc(s["v_ready"], 1)
                else:
                    v.wait_ge(unit_done, STARTED + r * (4 * per) + (u0 + per * (j + 1)))
                    v.scalar_tensor_tensor(out=tile(value, r * 4 + j, n), in0=out_bank(i, j, n), scalar=add,
                                           in1=tile(value, r * 4 + j, n), op0=ALU.mult, op1=ALU.add) \
                     .then_inc(s["v_ready"], 1)
                    v.wait_ge(s["sq_ready"], at["sq_ready"] + r * 4 + (j + 1))
                v.wait_ge(s["acc_done"], at["acc_done"] + r * 4 + (j + 2))
                v.tensor_tensor(tile(acc, 0, n), tile(acc, 0, n), tile(sq, j % 2, n), ALU.add) \
                 .then_inc(s["acc_done"], 1)

    def dve_res(v, i, n, value, rms, norm, name, g0):
        s, at = res_s, res_at[i]
        r_ready(v, rms)
        for k in range(KD + 2):
            if k < KD:
                if k >= 2:
                    v.wait_ge(s["h_ready"], at["h_ready"] + k - 1)
                v.tensor_tensor(tile(wa, k % 2, n), tile(value, k, n), tile(rbc, 0, n), ALU.mult).then_inc(s["t_ready"], 1)
            if k >= 2:
                lo_of_x(v, norm, k - 2, n, name, g0)

    def dve_mlstm(v):
        s, u0 = a1, U_M1
        v.wait_ge(norm_s["x_ready"], norm_at[1]["x_ready"] + KD)
        v.memset(zpad(0)[:, 0:3], 0.0)
        v.memset(zpad(1)[:, 0:3], 0.0)
        v.memset(go, 1.0).then_inc(s["pad"], 1)
        v.wait_ge(s["pad"], 1)
        r_ready(v, N1)
        for m in range(8):
            b = m % 2
            v.wait_ge(unit_done, STARTED + u0 + m + 1)
            if m >= 2:
                v.wait_ge(s["conv_done"], m - 1)
            v.tensor_tensor(zpad(b)[:, 3:3 + TOK].rearrange("p (a n) -> p a n", a=2), bank(2 * (m % 3), TOK),
                            tile(rbc, 0, TOK), ALU.mult).then_inc(s["z_ready"], 1)
            v.wait_ge(s["z_ready"], m + 1)
            if m >= 2:
                v.wait_ge(s["qk_ready"], m - 1)
            w = [gain("a_conv_w", 8 * j + m) for j in range(CONV)]
            link(v, "dve", v.tensor_scalar(cacc(b), zpad(b)[:, 3:3 + TOK], w[3], gain("a_conv_b", m), ALU.mult, ALU.add))
            for j in (2, 1):
                link(v, "dve", v.scalar_tensor_tensor(out=cacc(b), in0=zpad(b)[:, j:j + TOK], scalar=w[j], in1=cacc(b),
                                                      op0=ALU.mult, op1=ALU.add))
            v.scalar_tensor_tensor(out=cacc(b), in0=zpad(b)[:, 0:TOK], scalar=w[0], in1=cacc(b), op0=ALU.mult,
                                   op1=ALU.add).then_inc(s["conv_done"], 1)
        v.wait_ge(unit_done, STARTED + u0 + 9)
        g2 = [x.rearrange("p (a n) -> p a n", a=2) for x in (ga, gb)]
        rg2 = tile(rbc, 0, TOK)[0:HEADS]
        link(v, "dve", v.tensor_tensor(g2[0], bank(4, TOK, HEADS), rg2, ALU.mult))
        v.tensor_tensor(g2[1], bank(6, TOK, HEADS), rg2, ALU.mult).then_inc(s["gates_read"], 1)
        link(v, "dve", v.tensor_scalar(ga, ga, gateb[:, 0:1], None, ALU.add))
        v.wait_ge(s["gates_read"], 1)
        link(v, "dve", v.tensor_scalar(gb, gb, gateb[:, 1:2], None, ALU.add))
        v.scalar_tensor_tensor(out=gc, in0=gb, scalar=-1.0, in1=gb, op0=ALU.mult, op1=ALU.min).then_inc(s["neg_abs"], 1)
        v.wait_ge(s["softplus"], 1)
        link(v, "dve", v.scalar_tensor_tensor(out=gb, in0=gb, scalar=0.0, in1=gc, op0=ALU.min, op1=ALU.subtract))
        link(v, "dve", v.tensor_tensor_scan(gc, go, gb, 0.0, ALU.mult, ALU.add))
        link(v, "dve", v.tensor_tensor(ga, ga, gc, ALU.subtract))
        link(v, "dve", v.tensor_tensor_scan(gb, ga, ga, 0.0, ALU.max, ALU.max))
        link(v, "dve", v.tensor_tensor(gc, gc, gb, ALU.add))
        v.tensor_scalar(gb, gb, -1.0, None, ALU.mult).then_inc(s["nm_ready"], 1)
        v.memset(m1["acol"][:, :], 0.0).then_inc(s["rden"], 1)
        v.wait_ge(s["rden"], 1)
        v.wait_ge(s["a_turned"], 1)
        link(v, "dve", v.tensor_copy(m1["acol"][0:META, 0:HEADS], ps[0:META, 3, 0:HEADS]))
        v.tensor_copy(m1["acol"][:, HEADS:], ps[:, 3, HEADS:(CH + 1) * HEADS]).then_inc(s["acol_ready"], 1)

        for m in range(8):
            v.wait_ge(unit_done, STARTED + u0 + 17 + m + 1)
            v.tensor_tensor(m1["og"][:, m, :], ps[:, 1 + m % 2, :], rbc[:, META:TOK], ALU.mult).then_inc(s["og_raw"], 1)

        def keep(h):
            v.wait_ge(s["num_done"], h + 1)
            v.wait_ge(s["og_ready"], h + 1)
            v.tensor_tensor(tile(m1["num"], h, SEQ), ps[:, 1, :], m1["og"][:, h, :], ALU.mult).then_inc(s["num_kept"], 1)

        v.wait_ge(a1["const"], 48)
        for h in range(HEADS):
            for j in range(CH + 1):
                g = (CH + 1) * h + j
                e = e_tile(h, j)
                v.wait_ge(s["E_ready"], g + 1)
                if j >= 1:
                    link(v, "dve", v.scalar_tensor_tensor(out=e[:, 0:P], in0=e[:, 0:P], scalar=1.0, in1=m1["tri"][:, :],
                                                          op0=ALU.min, op1=ALU.mult))
                v.wait_ge(s["dots"], g + 1)
                v.scalar_tensor_tensor(out=e, in0=ps[0:META if j == 0 else P, QK_BANK[j], 0:EW[j]],
                                       scalar=A_DK ** -0.5, in1=e, op0=ALU.mult, op1=ALU.mult).then_inc(s["S_ready"], 1)
            if h >= 1:
                keep(h - 1)
        keep(HEADS - 1)
        v.wait_ge(s["em_ready"], 1)
        em = gc[:, META:TOK]
        den = ps[0:HEADS, 3, :]
        dn = ga[:, META:TOK]
        link(v, "dve", v.scalar_tensor_tensor(out=dn, in0=den, scalar=-1.0, in1=em, op0=ALU.mult, op1=ALU.max))
        link(v, "dve", v.tensor_tensor(dn, den, dn, ALU.max))
        v.reciprocal(dn, dn).then_inc(s["rden"], 1)
        for h in range(HEADS + 1):
            if h < HEADS:
                v.wait_ge(s["rb_done"], h + 1)
                if h >= 2:
                    v.wait_ge(s["y_split"], h - 1)
                v.tensor_tensor(tile(wb, h % 2, SEQ), tile(m1["num"], h, SEQ), ps[:, 4 + h % 4, :], ALU.mult) \
                 .then_inc(s["y_ready"], 1)
            if h == 6:
                v.wait_ge(s["y_ready"], 6)
                free_out(v, 1, SEQ)
            if h >= 1:
                v.wait_ge(s["y_hi"], h)
                v.tensor_tensor(tile(xlo, h - 1, SEQ), tile(wb, (h - 1) % 2, SEQ), tile(xhi, h - 1, SEQ).bitcast(F32),
                                ALU.subtract).then_inc(s["y_split"], 1)

    MAGIC = 12582912.0
    TWO_PI = 6.283185307179586
    PI_1 = 6.25
    PI_2 = float(np.float32(np.round((TWO_PI - PI_1) * 2.0 ** 16) / 2.0 ** 16))
    PI_3 = TWO_PI - PI_1 - PI_2
    PI_SAFE = 3.1415925

    def dve_mix2(v):
        s, u0 = a2, U_M2
        v.wait_ge(s["decay"], 32)
        v.scalar_tensor_tensor(out=m2["lgt"][:, :], in0=m2["lg"][:, :], scalar=-1.0, in1=m2["lg"][:, :],
                               op0=ALU.mult, op1=ALU.min).then_inc(s["lg1"], 1)
        v.wait_ge(s["pos"], 16)
        v.wait_ge(s["const"], 96)
        posi, posf = m2["RS"][:, 0, :].bitcast(I32), m2["RS"][:, 1, :]
        turn = m2["RS"][:, 2, :]
        link(v, "dve", v.tensor_copy(posf, posi))

        def angles(j, co, si):
            ang, ab = m2[si][:, :], m2[co][:, :]
            link(v, "dve", v.tensor_scalar(ang, posf, m2["invf"][:, j:j + 1], None, ALU.mult))
            link(v, "dve", v.tensor_scalar(turn, ang, 1.0 / TWO_PI, None, ALU.mult))
            link(v, "dve", v.tensor_scalar(turn, turn, MAGIC, None, ALU.add))
            link(v, "dve", v.tensor_scalar(turn, turn, MAGIC, None, ALU.subtract))
            for part in (PI_1, PI_2, PI_3):
                link(v, "dve", v.scalar_tensor_tensor(out=ang, in0=turn, scalar=-part, in1=ang, op0=ALU.mult, op1=ALU.add))
            v.tensor_scalar(ang, ang, -PI_SAFE, PI_SAFE, ALU.max, ALU.min).then_inc(s["angle"], 1)
            v.wait_ge(s["angle"], 2 * j + 1)
            v.scalar_tensor_tensor(out=ab, in0=ang, scalar=-1.0, in1=ang, op0=ALU.mult, op1=ALU.max) \
             .then_inc(s["angle"], 1)

        def latent(k):
            x = m2["cq"][:, k, :] if k < 2 else m2["ckv"][:, :]
            hi = m2["cq_hi"][:, k, :] if k < 2 else m2["ckv_hi"][:, :]
            lo = m2["cq_lo"][:, k, :] if k < 2 else m2["ckv_lo"][:, :]
            return x, hi, lo

        def rope(r):
            rows = slice(NOPE, QK_DIM) if r == 0 else slice(0, P)
            co, si = ("cosm", "sinm") if r == 0 else ("cosr", "sinr")
            x = (m2["kpe"][rows, :] if r == 0 else (m2["rq"] if r < 5 else m2["rk"])[:, (r - 1) % 4, :])
            tmp = wa[rows, 0:SEQ]
            if r < 2:
                v.wait_ge(s["trig"], 2 * r + 2)
            v.wait_ge(s["swapped"], r + 1)
            v.tensor_tensor(tmp, m2[si][rows, :], ps[rows, 6 + r % 2, :], ALU.mult).then_inc(s["swap_used"], 1)
            link(v, "dve", v.tensor_tensor(x, x, m2[co][rows, :], ALU.mult))
            v.wait_ge(s["swap_used"], r + 1)
            v.tensor_tensor(x, x, tmp, ALU.add).then_inc(s["roped"], 1)

        raws = [m2["cq"][:, 0, :], m2["cq"][:, 1, :], m2["ckv"][:, :], m2["kpe"][NOPE:QK_DIM, :]]
        raws += [m2[x][:, m, :] for x in ("rq", "rk") for m in range(4)] + [None] * 4
        raws += [m2["rg"][:, m, :] for m in range(4)]
        at_unit = list(range(12)) + [16, 17, 18, 19]

        def leave(e):
            rows = ROPE_DIM if e == 3 else P
            v.wait_ge(unit_done, STARTED + u0 + at_unit[e] + 1)
            dst = raws[at_unit[e]]
            v.scalar_tensor_tensor(out=dst, in0=ps[0:rows, e % 2, :], scalar=RET_DIM ** -0.5 if 8 <= e < 12 else 1.0,
                                   in1=rbc[0:rows, META:TOK], op0=ALU.mult, op1=ALU.mult).then_inc(s["raw_ready"], 1)

        def latents(step):
            if step == 0:
                v.wait_ge(s["croot"], 2)
                for k in range(3):
                    x = latent(k)[0]
                    r0 = 0 if k < 2 else TOK
                    v.scalar_tensor_tensor(out=x, in0=x, scalar=gain("q_norm_2", k) if k < 2 else gain("kv_norm_2", 0),
                                           in1=wb[:, r0:r0 + SEQ], op0=ALU.mult, op1=ALU.mult).then_inc(s["cnorm"], 1)
            else:
                for k in range(3):
                    x, hi, lo = latent(k)
                    v.wait_ge(s["chi"], k + 1)
                    v.tensor_tensor(lo, x, hi.bitcast(F32), ALU.subtract).then_inc(s["csplit"], 1)

        r_ready(v, N4)
        for e in range(16):
            leave(e)
            if e == 1:
                angles(0, "cosm", "sinm")
            if e == 2:
                angles(1, "cosr", "sinr")
                v.wait_ge(s["lg2"], 1)
                v.scalar_tensor_tensor(out=m2["lg"][:, :], in0=m2["lg"][:, :], scalar=0.0, in1=m2["lgt"][:, :],
                                       op0=ALU.min, op1=ALU.subtract).then_inc(s["lg_ready"], 1)
            if 5 <= e <= 13:
                rope(e - 5)
                v.wait_ge(s["roped"], e - 4)
            if e == 6:
                latents(0)
            if e == 9:
                latents(1)

        def center(m):
            ob = tile(wa, m % 2, SEQ)
            v.wait_ge(s["mean"], m + 1)
            v.tensor_tensor(ob, ob, ps[:, 6, :], ALU.subtract).then_inc(s["cent"], 1)

        def gate(m):
            ob = tile(wa, m % 2, SEQ)
            v.wait_ge(s["rg_ready"], m + 1)
            v.wait_ge(s["csq2"], m + 1)
            link(v, "dve", v.tensor_tensor(ob, ob, m2["rg"][:, m, :], ALU.mult))

        def normed(m):
            ob = tile(wa, m % 2, SEQ)
            v.wait_ge(s["rroot"], m + 1)
            v.tensor_tensor(ob, ob, rbc[:, 0:SEQ], ALU.mult).then_inc(s["r_ready"], 1)

        def ret_lo(m):
            v.wait_ge(s["r_hi"], m + 1)
            v.tensor_tensor(tile(xlo, 4 + m, SEQ), tile(wa, m % 2, SEQ), tile(xhi, 4 + m, SEQ).bitcast(F32), ALU.subtract) \
             .then_inc(s["r_split"], 1)

        after = {}
        for m in range(4):
            after.update({(2 * m + 3, 2): (center, m), (2 * m + 4, 0): (gate, m), (2 * m + 4, 3): (normed, m),
                          (2 * m + 5, 0): (ret_lo, m)})
        for h in range(HEADS + 4):
            if h < HEADS:
                v.wait_ge(s["dec_ready"], h + 1)
            for c in range(CH):
                g = CH * h + c
                if h < HEADS:
                    v.wait_ge(s["dots"], g + 1)
                    if h >= 1:
                        v.wait_ge(s["dec_used"], g - CH + 1)
                    o = (SEQ - P) - P * c
                    v.tensor_tensor(m2["RS"][:, c, :], m2["dec"][:, h % 2, o:o + SEQ], ps[:, 2 + c, :], ALU.mult) \
                     .then_inc(s["RS_ready"], 1)
                if (h, c) in after:
                    step, m = after[h, c]
                    step(m)

    def dve_mla(v):
        s, u0 = a3, U_M2 + 20
        for h in range(HEADS):
            link(v, "dve", v.tensor_copy(m3["kT"][NOPE:QK_DIM, h, :], m3["kpe"][NOPE:QK_DIM, :]))
        v.memset(cell[:, :], 0.0).then_inc(s["kpe_ready"], 1)
        rows = slice(NOPE, QK_DIM)
        for h in range(HEADS):
            x, tmp = m3["qT"][rows, h, :], wa[rows, 0:SEQ]
            v.wait_ge(s["swapped"], h + 1)
            v.wait_ge(*((s["q_ready"], h) if h >= 1 else (a2["r_split"], 4)))
            link(v, "dve", v.tensor_tensor(tmp, m3["sinm"][rows, :], ps[rows, 2 + h % 2, :], ALU.mult))
            link(v, "dve", v.tensor_tensor(x, x, m3["cosm"][rows, :], ALU.mult))
            v.tensor_tensor(x, x, tmp, ALU.add).then_inc(s["q_ready"], 1)

        def maximum(h, c):
            g = CH * h + c
            v.wait_ge(s["dots"], g + 1)
            link(v, "dve", v.reduce_max(small[:, 24 + c:25 + c], ps[:, c % 2, :], AX_X))
            if h >= 1:
                v.wait_ge(s["P_exp"], g - CH + 1)
            v.tensor_scalar(small[:, c:c + 1], small[:, 24 + c:25 + c], -MLA_SCALE, None, ALU.mult) \
             .then_inc(s["max_ready"], 1)

        def scale(h, c):
            v.wait_ge(s["P_exp"], CH * h + c + 1)
            link(v, "dve", v.reciprocal(small[:, 16 + c:17 + c], small[:, 8 + c:9 + c]))
            x = m3["PR"][:, h % 2, c * SEQ:(c + 1) * SEQ]
            v.tensor_scalar(x, x, small[:, 16 + c:17 + c], None, ALU.mult).then_inc(s["P_ready"], 1)

        def keep_turned(h, c):
            if h >= 1:
                v.wait_ge(s["o_done"], h)
            v.wait_ge(s["turned"], CH * h + c + 1)
            v.tensor_copy(m3["PT"][:, c * SEQ:(c + 1) * SEQ], ps[:, 2 + c, :]).then_inc(s["PT_dve"], 1)

        def out_lo(m):
            v.wait_ge(s["o_hi"], m + 1)
            v.tensor_tensor(tile(xlo, m, SEQ), ps[:, 6 + m % 2, :], tile(xhi, m, SEQ).bitcast(F32), ALU.subtract) \
             .then_inc(s["o_split"], 1)

        maximum(0, 0)
        for c in range(1, CH):
            maximum(0, c)
            scale(0, c - 1)
        maximum(1, 0)
        scale(0, CH - 1)
        for h in range(HEADS):
            if h + 1 < HEADS:
                maximum(h + 1, 1)
                scale(h + 1, 0)
            keep_turned(h, 1)
            if h % 2 == 0 and h >= 2:
                out_lo(h // 2 - 1)
            if h + 1 < HEADS:
                for c in (2, 3):
                    maximum(h + 1, c)
                    scale(h + 1, c - 1)
                if h + 2 < HEADS:
                    maximum(h + 2, 0)
                scale(h + 1, 3)
        out_lo(HEADS // 2 - 1)

    def prog_vector(v):
        v.memset(eps[:, :], EPS).then_inc(init["eps"], 1)
        v.memset(halfpi[:, :], TWO_PI / 4).then_inc(init["eps"], 1)
        v.wait_ge(init["turned"], 1)
        v.tensor_copy(vec[:, :], ps[:, 5, 0:NVEC]).then_inc(init["h_ready"], 1)
        hv = hT[:, :].rearrange("p (k t) -> p k t", k=KD)
        v.wait_ge(init["turned"], 2)
        link(v, "dve", v.tensor_copy(hv[:, :, 0:META], ps[:, 4, 0:KD * META].rearrange("p (k t) -> p k t", k=KD)))
        for k in range(KD):
            v.wait_ge(init["turned"], 3 + k)
            v.tensor_copy(hv[:, k, META:TOK], ps[:, k % 4, :]).then_inc(init["h_ready"], 1)
        free_ffn(v)
        dve_norm(v, 0, TOK, "norm_gains", 0, True)
        dve_rms(v, N0)
        dve_ffn(v, 0, N0)
        free_out(v, 0, TOK)
        dve_out(v, 0, TOK, ybuf, NU_UP, 3, gains=(8, 0.5))
        dve_rms(v, R0)
        dve_res(v, 0, TOK, ybuf, R0, 1, "norm_gains", 16)
        for k in range(1, KD):
            sum_square(v, 1, k, TOK)
        dve_rms(v, N1)
        dve_mlstm(v)
        dve_out(v, 1, SEQ, m1["num"], U_M1 + 25, 1, gains=(24, 1.0))
        dve_rms(v, R1)
        free_ffn(v)
        dve_res(v, 1, SEQ, m1["num"], R1, 2, "norm_gains", 32)
        for k in range(1, KD):
            sum_square(v, 2, k, SEQ)
        dve_rms(v, N2)
        free_out(v, 2, SEQ)
        dve_ffn(v, 1, N2)
        dve_out(v, 2, SEQ, ybuf, FFNS[1]["u0"] + NU_UP, 3, gains=(40, 0.5))
        dve_rms(v, R2)
        free_ffn(v)
        dve_res(v, 2, SEQ, ybuf, R2, 3, "ffn1_norm_2", 0)
        for k in range(1, KD):
            sum_square(v, 3, k, SEQ)
        dve_rms(v, N3)
        free_out(v, 3, SEQ)
        dve_ffn(v, 2, N3)
        dve_out(v, 3, SEQ, hT, FFNS[2]["u0"] + NU_UP, 3, add=0.5)
        dve_norm(v, 4, SEQ, "mix_norm_2", 0)
        dve_rms(v, N4)
        dve_mix2(v)
        free_out(v, 4, SEQ)
        dve_mla(v)
        dve_out(v, 4, SEQ, hT, U_M2 + 23, 1, add=1.0)
        free_ffn(v)
        dve_norm(v, 5, SEQ, "ffn2_norm_2", 0)
        dve_rms(v, N5)
        free_out(v, 5, SEQ)
        dve_ffn(v, 3, N5)
        dve_out(v, 5, SEQ, hT, FFNS[3]["u0"] + NU_UP, 3, add=0.5)
        for k in range(KD):
            v.tensor_scalar(fin["fin"][:, k, :], tile(hT, k, SEQ), gain("final_norm_2", k), None, ALU.mult) \
             .then_inc(fin_s["t_ready"], 1)
        dve_rms(v, N6)

    NORM_OF_FFN = [0, 2, 3, 5]

    def out_bank(i, j, n):
        return bank(2 * (j % 2) if n == TOK else 4 + j % 2, n)

    def product(pe, outs, lhs, rhs, first, last):
        n = 0
        for l, r in ((0, 0), (0, 1), (1, 0)):
            for o, x in zip(outs, rhs):
                ins = pe.matmul(o, lhs[l], x[r], start=first and n == 0, stop=last and n == 2)
            n += 1
        return ins

    def w_tile(u, k, n=P, c0=0, width=P):
        return [w[:, u % SLOTS, k * n + c0:k * n + c0 + width] for w in (whi, wlo)]

    def x_cols(k, o, w):
        return [x[:, k * TOK + o:k * TOK + o + w] for x in (xhi, xlo)]

    def project(pe, b, n, u, norm=None, width=P, wn=P):
        for k in range(KD):
            if norm is not None:
                pe.wait_ge(norm_s["x_ready"], norm_at[norm]["x_ready"] + k + 1)
            p = pieces(b, n)
            ins = product(pe, [o[0:width] for o, _, _ in p], w_tile(u, k, wn, 0, width), [x_cols(k, o, w) for _, o, w in p],
                          k == 0, k == KD - 1)
        return ins

    def sum_acc(pe, i, n, norm=False):
        if norm:
            pe.wait_ge(norm_s["summed"], norm_at[i]["summed"] + 1)
        else:
            pe.wait_ge(out_s["acc_done"], out_at[i]["acc_done"] + KD + 2)
        chunks = ([(0, 0)] if n == TOK else []) + [(c + 1, META + c * P) for c in range(CH)]
        for c, o in chunks:
            ins = pe.matmul(ps[:, 7, c:c + 1], acc[:, o:o + P], ones[:, 0:1], start=True, stop=True, skip_group_check=True)
        ins.then_inc(r_s["sums"], 1)

    def spread(pe, rms):
        pe.wait_ge(r_s["diag"], r_at[rms]["diag"] + 1)
        if rms in R_TOK:
            pe.matmul(ps[:, 7, 16:16 + META], ones[0:META, :], diag[0:META, 0:META], start=True, stop=True)
        pe.matmul(ps[:, 6, :], ones[:, :], diag[:, META:TOK], start=True, stop=True).then_inc(r_s["spread"], 1)

    def pe_ffn(pe, i, norm, rms, acc_of=None):
        f, s, at, n, u0 = FFNS[i], ffn_s, ffn_at[i], FFNS[i]["n"], FFNS[i]["u0"]

        def unit(r, b, g, between=None):
            u = u0 + 2 * b + g
            pe.wait_ge(lo_done, r * 4 + (u + 1))
            pe.wait_ge(s["banks_free"], at["banks_free"] + r * 2 + (b + 1))
            p = pieces((4 * g + 2 * b) if n == TOK else (2 * g + b), n)
            for k in range(KD):
                if between is not None:
                    between(k)
                ins = product(pe, [o for o, _, _ in p], w_tile(u, k), [x_cols(k, o, w) for _, o, w in p],
                              k == 0, k == KD - 1)
            ins.then_inc(unit_done, 1)

        def operand(k):
            pe.wait_ge(norm_s["x_ready"], norm_at[norm]["x_ready"] + k + 1)

        def sums(k):
            if k == KD - 1:
                sum_acc(pe, norm, n, True)

        def spreading(k):
            if k == KD - 3:
                spread(pe, rms)

        if acc_of is not None:
            sum_acc(pe, acc_of, n)
        unit(0, 0, 0, operand)
        unit(0, 0, 1, sums if acc_of is None else None)
        unit(0, 1, 0, spreading)
        if n == TOK:
            pe.wait_ge(r_s["ready"], r_at[rms]["ready"] + 2)
        unit(0, 1, 1)
        with pe.Fori(1, KF // 2) as r:
            for b in range(2):
                for g in range(2):
                    unit(r, b, g)
        u0 += NU_UP
        v_at = out_at[[0, 2, 3, 5][i]]["v_ready"]
        with pe.Fori(0, 2) as r:
            for j in range(4):
                pe.wait_ge(out_s["v_ready"], v_at + r * 4 + (j + 1))
                b = 2 * (j % 2) if n == TOK else 4 + j % 2
                p = pieces(b, n)
                for q, (k0, kn) in enumerate(FFN_PIECES):
                    u = u0 + 3 * j + q
                    pe.wait_ge(lo_done, r * 12 + (u + 1))
                    for k in range(k0, k0 + kn):
                        if j == 0:
                            pe.wait_ge(s["hid_ready"], at["hid_ready"] + k + 3)
                        ins = product(pe, [o for o, _, _ in p], w_tile(u, k - k0),
                                      [[x[:, k * TOK + o:k * TOK + o + w] for x in (hid_hi, hid_lo)] for _, o, w in p],
                                      k == 0, k == KF - 1)
                    ins.then_inc(unit_done, 1)

    def pe_out(pe, i, u0, order, ready):
        s, at = out_s, out_at[i]
        with pe.Fori(0, 2) as r:
            for j in range(4):
                pe.wait_ge(s["v_ready"], at["v_ready"] + r * 4 + (j + 1))
                pe.wait_ge(lo_done, r * 4 + (u0 + j + 1))
                for q, k in enumerate(order):
                    if j == 0:
                        sem, count = ready(k)
                        pe.wait_ge(sem, count)
                    ins = product(pe, [ps[:, 4 + j % 2, :]], w_tile(u0 + j, k), [x_cols(k, META, SEQ)], q == 0, q == KD - 1)
                ins.then_inc(unit_done, 1)

    def pe_mlstm(pe):
        s, u0 = a1, U_M1
        for m in range(8):
            pe.wait_ge(lo_done, u0 + m + 1)
            if m >= 3:
                pe.wait_ge(s["z_ready"], m - 2)
            project(pe, 2 * (m % 3), TOK, u0 + m, 1 if m == 0 else None).then_inc(unit_done, 1)
            if m == 1:
                sum_acc(pe, 1, TOK, True)
            if m == 2:
                spread(pe, N1)
        pe.wait_ge(lo_done, u0 + 9)
        pe.wait_ge(r_s["ready"], r_at[N1]["ready"] + 2)
        pe.wait_ge(s["z_ready"], 6)
        for g in range(2):
            for k in range(KD):
                p = pieces(4 + 2 * g, TOK)
                ins = product(pe, [o[0:HEADS] for o, _, _ in p], w_tile(u0 + 8, k, 2 * HEADS, g * HEADS, HEADS),
                              [x_cols(k, o, w) for _, o, w in p], k == 0, k == KD - 1)
        ins.then_inc(unit_done, 1)
        pe.wait_ge(s["z_ready"], 8)
        pe.wait_ge(s["gates_read"], 1)
        for n in range(2):
            for j in range(4):
                u = u0 + 9 + 4 * n + j
                pe.wait_ge(lo_done, u + 1)
                for kk in range(2):
                    k = 2 * j + kk
                    for c in (0, 1, 2, 3, -1):
                        if n == 1 and k == 0 and c in (3, -1):
                            pe.wait_ge(s["v_ready"], 1 if c == 3 else 2)
                        rows = META if c < 0 else P
                        x = x_cols(k, 0 if c < 0 else META + P * c, rows)
                        ins = product(pe, [ps[0:rows, V_BANK[n][c], :]], x, [w_tile(u, kk, 512, 0, 512)], k == 0, k == KD - 1)
                ins.then_inc(unit_done, 1)
        pe.wait_ge(s["v_ready"], 5)
        pe.wait_ge(s["nm_ready"], 1)
        pe.transpose(ps[0:META, 3, 0:HEADS], ga[:, 0:META], ident[0:HEADS, 0:HEADS])
        for c in range(CH):
            ins = pe.transpose(ps[:, 3, (c + 1) * HEADS:(c + 2) * HEADS], ga[:, META + P * c:META + P * (c + 1)],
                               ident[0:HEADS, 0:HEADS])
        ins.then_inc(s["a_turned"], 1)
        for m in range(8):
            pe.wait_ge(lo_done, u0 + 17 + m + 1)
            if m >= 2:
                pe.wait_ge(s["og_raw"], m - 1)
            project(pe, 1 + m % 2, SEQ, u0 + 17 + m, None).then_inc(unit_done, 1)

        def broadcast(h):
            pe.matmul(ps[:, 0, :], m1["selrow"][:, h * P:(h + 1) * P], gb[:, META:TOK], start=True, stop=True) \
              .then_inc(s["bc_done"], 1)

        def dots(h, j):
            rows = slice(64 * (h % 2), 64 * (h % 2) + 64)
            ks, q0 = (0, META) if j == 0 else (META + P * (j - 1), META + P * (j - 1))
            kw = META if j == 0 else P
            kt, qt = (4 + h // 2) * TOK, (h // 2) * TOK
            pe.matmul(ps[0:kw, QK_BANK[j], 0:EW[j]], m1["qkT"][rows, kt + ks:kt + ks + kw],
                      m1["qkT"][rows, qt + q0:qt + q0 + EW[j]], start=True, stop=True).then_inc(s["dots"], 1)

        pe.wait_ge(s["qk_ready"], 8)
        pe.wait_ge(s["const"], 48)
        pe.wait_ge(s["v_ready"], 10)
        pe.wait_ge(s["og_raw"], 8)
        broadcast(0)
        for j in range(CH + 1):
            dots(0, j)
        pe.wait_ge(s["acol_ready"], 1)
        for h in range(HEADS):
            if h + 1 < HEADS:
                pe.wait_ge(s["E_ready"], (CH + 1) * (h + 1))
                broadcast(h + 1)
            for j in range(CH + 1):
                pe.wait_ge(s["S_ready"], (CH + 1) * h + j + 1)
                if h + 1 < HEADS:
                    dots(h + 1, j)
            if h >= 1:
                pe.wait_ge(s["num_kept"], h)
            for j in range(CH + 1):
                t0 = 0 if j == 0 else P * (j - 1)
                e = e_tile(h, j)
                rows = META if j == 0 else P
                pe.matmul(ps[0:HEADS, 3, t0:SEQ], m1["selcol"][0:rows, h * HEADS:(h + 1) * HEADS], e,
                          start=h == 0 and j == 0, stop=h == HEADS - 1 and j == CH, skip_group_check=True)
                vv = m1["v_meta"] if j == 0 else m1["v_real"][:, j - 1, :]
                ins = pe.matmul(ps[:, 1, t0:SEQ], vv[0:rows, h * P:(h + 1) * P], e, start=j == 0, stop=j == CH,
                                skip_group_check=True)
            ins.then_inc(s["num_done"], 1)
        pe.wait_ge(s["rden"], 2)
        for h in range(HEADS):
            if h >= 4:
                pe.wait_ge(s["y_ready"], h - 3)
            pe.matmul(ps[:, 4 + h % 4, :], m1["selrow"][:, h * P:(h + 1) * P], ga[:, META:TOK], start=True, stop=True) \
              .then_inc(s["rb_done"], 1)

    def pe_mix2(pe):
        s, u0 = a2, U_M2

        def swap(r):
            pe.wait_ge(s["raw_ready"], r + 4)
            if r >= 2:
                pe.wait_ge(s["swap_used"], r - 1)
            if r == 0:
                pe.wait_ge(s["const"], 96)
                ins = pe.matmul(ps[0:QK_DIM, 6, :], m2["permpe"][NOPE:QK_DIM, :], m2["kpe"][NOPE:QK_DIM, :], start=True, stop=True)
            else:
                x = (m2["rq"] if r < 5 else m2["rk"])[:, (r - 1) % 4, :]
                ins = pe.matmul(ps[:, 6 + r % 2, :], m2["perm"][:, :], x, start=True, stop=True)
            ins.then_inc(s["swapped"], 1)

        for e in range(12):
            pe.wait_ge(lo_done, u0 + e + 1)
            if e >= 2:
                pe.wait_ge(s["raw_ready"], e - 1)
            ready = 4 if e == 0 else None
            if e == 3:
                ins = project(pe, e % 2, SEQ, u0 + e, None, ROPE_DIM, ROPE_DIM)
            else:
                ins = project(pe, e % 2, SEQ, u0 + e, ready)
            ins.then_inc(unit_done, 1)
            if e == 0:
                spread(pe, N4)
            if e == 2:
                for k in range(2):
                    pe.wait_ge(s["csq"], k + 1)
                    ins = pe.matmul(ps[:, 2, :], ones[:, :], sq[:, k * TOK:k * TOK + SEQ], start=k == 0, stop=k == 1)
                ins.then_inc(s["cstat"], 1)
            if e == 3:
                pe.wait_ge(s["csq"], 3)
                pe.matmul(ps[:, 3, :], ones[:, :], sq[:, 0:SEQ], start=True, stop=True).then_inc(s["cstat"], 1)
            if e >= 4:
                swap(e - 4)
        pe.wait_ge(s["croot"], 2)
        for j in range(4):
            pe.wait_ge(lo_done, u0 + 12 + j + 1)
            for kk in range(2):
                k = 2 * j + kk
                for c in range(CH):
                    ins = product(pe, [ps[:, 2 + c, :]], x_cols(k, META + P * c, P), [w_tile(u0 + 12 + j, kk, 512, 0, 512)],
                                  k == 0, k == KD - 1)
            ins.then_inc(unit_done, 1)
            if j == 0:
                swap(8)
        for m in range(4):
            pe.wait_ge(lo_done, u0 + 16 + m + 1)
            pe.wait_ge(s["raw_ready"], 11 + m)
            project(pe, m % 2, SEQ, u0 + 16 + m, None).then_inc(unit_done, 1)

        def dots(h, c):
            rows = slice(64 * (h % 2), 64 * (h % 2) + 64)
            pe.matmul(ps[:, 2 + c, :], m2["rk"][rows, h // 2, c * P:(c + 1) * P], m2["rq"][rows, h // 2, :],
                      start=True, stop=True).then_inc(s["dots"], 1)

        pe.wait_ge(s["rv_ready"], 4)
        pe.wait_ge(s["roped"], 9)
        pe.wait_ge(s["raw_ready"], 16)
        for c in range(CH):
            dots(0, c)
        for h in range(HEADS):
            m = h // 2
            rows = slice(64 * (h % 2), 64 * (h % 2) + 64)
            if h % 2 == 0 and m >= 2:
                pe.wait_ge(s["ob_ready"], m - 1)
            for c in range(CH):
                pe.wait_ge(s["RS_ready"], CH * h + c + 1)
                if h + 1 < HEADS:
                    dots(h + 1, c)
                pe.matmul(ps[rows, m % 2, :], m2["rv"][:, c, h * RET_DIM:(h + 1) * RET_DIM], m2["RS"][:, c, :],
                          start=c == 0, stop=c == CH - 1).then_inc(s["dec_used"], 1)
                if h >= 2 and c == 1:
                    (pe_mean if h % 2 == 0 else pe_variance)(pe, m - 1)
            if h % 2 == 1:
                pe.wait_ge(s["dec_used"], CH * (h + 1))
                pe.transpose(ps[0:2, 6, 0:2], ident[0:2, 0:2], ident[0:2, 0:2]).then_inc(s["o_done"], 1)

    def pe_mean(pe, m):
        pe.wait_ge(a2["ob_ready"], m + 1)
        pe.matmul(ps[:, 6, :], m2["block"][:, :], tile(wa, m % 2, SEQ), start=True, stop=True).then_inc(a2["mean"], 1)

    def pe_variance(pe, m):
        pe.wait_ge(a2["csq2"], m + 1)
        pe.matmul(ps[:, 7, :], m2["block"][:, :], tile(sq, m % 2, SEQ), start=True, stop=True).then_inc(a2["var"], 1)

    def pe_mla(pe):
        s, u0 = a3, U_M2 + 20
        rows = slice(NOPE, QK_DIM)

        def swap(h):
            pe.wait_ge(s["q_raw"], h + 1)
            if h >= 2:
                pe.wait_ge(s["q_ready"], h - 1)
            pe.matmul(ps[0:QK_DIM, 2 + h % 2, :], m3["permpe"][rows, :], m3["qT"][rows, h, :], start=True, stop=True) \
              .then_inc(s["swapped"], 1)

        pe.wait_ge(a2["csplit"], 3)
        for h in range(HEADS):
            u, hh = u0 + h // 4, h % 4
            if hh == 0:
                pe.wait_ge(lo_done, u + 1)
            if h >= 2:
                pe.wait_ge(s["q_raw"], h - 1)
            for k in range(2):
                ins = product(pe, [ps[0:QK_DIM, h % 2, :]], w_tile(u, k, 4 * QK_DIM, hh * QK_DIM, QK_DIM),
                              [[m2["cq_hi"][:, k, :], m2["cq_lo"][:, k, :]]], k == 0, k == 1)
            ins.then_inc(unit_done if hh == 3 else s["q_part"], 1)
            if h == 0:
                pe_mean(pe, 3)
            if h == 1:
                pe_variance(pe, 3)
            if h >= 1:
                swap(h - 1)
        swap(HEADS - 1)
        u = u0 + 2
        pe.wait_ge(lo_done, u + 1)
        lat = [m2["ckv_hi"][:, :], m2["ckv_lo"][:, :]]
        for h in range(HEADS):
            if h >= 2:
                pe.wait_ge(s["k_ready"], h - 1)
            product(pe, [ps[0:NOPE, 4 + h % 2, :]], w_tile(u, 0, UNIT, h * P, NOPE), [lat], True, True) \
                .then_inc(s["k_part"], 1)
        wv = [w[:, u % SLOTS, :].rearrange("p (h c) -> p h c", h=HEADS)[:, :, NOPE:NOPE + V_DIM] for w in (whi, wlo)]
        for c in range(CH):
            if c >= 2:
                pe.wait_ge(s["v_ready"], c - 1)
            o = ps[:, 6 + c % 2, :].rearrange("p (h c) -> p h c", h=HEADS)
            product(pe, [o], [x[:, c * P:(c + 1) * P] for x in lat], [wv], True, True) \
                .then_inc(s["v_part"] if c < CH - 1 else unit_done, 1)

        def dots(h, c):
            g = CH * h + c
            if g >= 2:
                pe.wait_ge(s["P_exp"], g - 1)
            pe.matmul(ps[:, c % 2, :], m3["qT"][:, h, c * P:(c + 1) * P], m3["kT"][:, h, :], start=True, stop=True) \
              .then_inc(s["dots"], 1)

        def turn(h, c):
            if h >= 1:
                pe.wait_ge(*((s["PT_dve"], h) if c == 1 else (s["PT_act"], 3 * (h - 1) + max(c, 1))))
            pe.wait_ge(s["P_ready"], CH * h + c + 1)
            for k in range(CH):
                ins = pe.transpose(ps[:, 2 + c, k * P:(k + 1) * P],
                                   m3["PR"][:, h % 2, c * SEQ + k * P:c * SEQ + (k + 1) * P], ident[:, :])
            ins.then_inc(s["turned"], 1)

        pe.wait_ge(s["q_ready"], HEADS)
        pe.wait_ge(s["k_ready"], HEADS)
        pe.wait_ge(s["kpe_ready"], 1)
        pe.wait_ge(s["v_ready"], CH)
        for c in range(CH):
            dots(0, c)
        dots(1, 0)
        turned = m3["PT"][:, :].rearrange("p (c k n) -> p c k n", c=CH, k=CH)
        for h in range(HEADS):
            for c in range(CH):
                turn(h, c)
                nh, nc_ = (h + 1, c + 1) if c + 1 < CH else (h + 2, 0)
                if nh < HEADS:
                    dots(nh, nc_)
            m = h // 2
            if h % 2 == 0 and m >= 2:
                pe.wait_ge(s["o_split"], m - 1)
            pe.wait_ge(s["PT_dve"], h + 1)
            pe.wait_ge(s["PT_act"], 3 * h + 3)
            for k in range(CH):
                ins = pe.matmul(ps[64 * (h % 2):64 * (h % 2) + 64, 6 + m % 2, :], m3["vm"][:, k, h * V_DIM:(h + 1) * V_DIM],
                                turned[:, :, k, :], start=k == 0, stop=k == CH - 1)
            ins.then_inc(s["o_done"], 1)

    def prog_tensor(pe):
        pe.wait_ge(init["const"], 48)
        pe.wait_ge(init["vecs"], 16 * len(VEC_ROWS))
        pe.wait_ge(init["eps"], 2)
        pe.transpose(ps[0:16, 6, 0:16], ident[0:16, 0:16], ident[0:16, 0:16]).then_inc(unit_done, STARTED)
        pe.transpose(ps[:, 5, 0:NVEC], vrows[:, :], ident[0:NVEC, 0:NVEC]).then_inc(init["turned"], 1)
        pe.wait_ge(init["meta"], 16)
        for k in range(KD):
            ins = pe.transpose(ps[:, 4, k * META:(k + 1) * META], meta_tok[:, k * P:(k + 1) * P], ident[0:META, 0:META])
        ins.then_inc(init["turned"], 1)
        for c in range(CH):
            pe.wait_ge(init[f"x{c}"], 16)
        for k in range(KD):
            if k >= 4:
                pe.wait_ge(init["h_ready"], k - 2)
            for c in range(CH):
                ins = pe.transpose(ps[:, k % 4, c * P:(c + 1) * P], x_tok[:, c, k * P:(k + 1) * P], ident[:, :])
            ins.then_inc(init["turned"], 1)
        pe_ffn(pe, 0, 0, N0)
        sum_acc(pe, 0, TOK)
        spread(pe, R0)
        pe.wait_ge(r_s["ready"], r_at[R0]["ready"] + 2)
        pe_mlstm(pe)
        pe_out(pe, 1, U_M1 + 25, range(KD), lambda k: (a1["y_split"], k + 1))
        sum_acc(pe, 1, SEQ)
        spread(pe, R1)
        pe.wait_ge(r_s["ready"], r_at[R1]["ready"] + 1)
        pe_ffn(pe, 1, 2, N2)
        sum_acc(pe, 2, SEQ)
        spread(pe, R2)
        pe.wait_ge(r_s["ready"], r_at[R2]["ready"] + 1)
        pe_ffn(pe, 2, 3, N3)
        sum_acc(pe, 3, SEQ)
        pe_mix2(pe)
        pe_mla(pe)
        pe_out(pe, 4, U_M2 + 23, [4, 5, 6, 7, 0, 1, 2, 3],
               lambda k: (a3["o_split"], k + 1) if k < 4 else (a2["r_split"], k - 3))
        pe_ffn(pe, 3, 5, N5, 4)
        sum_acc(pe, 5, SEQ)
        for c in range(CH):
            for j in range(2):
                g = 2 * c + j
                if g >= 4:
                    pe.wait_ge(fin_s["kept_act"], g - 3)
                for k in range(4):
                    pe.wait_ge(fin_s["t_ready"], 4 * j + k + 1)
                    ins = pe.transpose(ps[:, g % 4, k * P:(k + 1) * P], fin["fin"][:, 4 * j + k, c * P:(c + 1) * P], ident[:, :])
                ins.then_inc(fin_s["turned"], 1)

    with ctx:
        block = ctx.enter_context(nc.Block())

        @block.sync
        def _(sp):
            prog_sync(sp)

        @block.gpsimd
        def _(pool):
            prog_gpsimd(pool)

        @block.scalar
        def _(act):
            prog_scalar(act)

        @block.vector
        def _(v):
            prog_vector(v)

        @block.tensor
        def _(pe):
            prog_tensor(pe)


_UNUSED = {"b_w_in", "b_f_bias", "b_lb_raw", "b_g_norm", "b_w_out"}


def kernel(**inputs):
    import concourse.bacc as _bacc
    from concourse.bass_utils import run_bass_kernel_spmd as _run

    nc = _bacc.Bacc("TRN2", target_bir_lowering=False, num_devices=1)
    arrays, dram = {}, {}
    for name, value in inputs.items():
        a = np.ascontiguousarray(value)
        if name in _UNUSED or a.size == 0:
            continue
        arrays[f"in_{name}"] = a
        dram[name] = nc.dram_tensor(f"in_{name}", a.shape, mybir.dt.from_np(a.dtype), kind="ExternalInput").ap()
    arrays["in_const"] = constants()
    dram["const"] = nc.dram_tensor("in_const", (P, NCONST), F32, kind="ExternalInput").ap()
    out = nc.dram_tensor("out_0", (1, SEQ, D), F32, kind="ExternalOutput").ap()
    program(nc, dram, out)
    r = _run(nc, [arrays], core_ids=[0])
    return r.results[0]["out_0"]
```

```python
from contextlib import ExitStack

import numpy as np

import concourse.bass as bass
from concourse import mybir

F32 = mybir.dt.float32
F32R = mybir.dt.float32r
I32 = mybir.dt.int32
ACT = mybir.ActivationFunctionType
ALU = mybir.AluOpType
AX_X = mybir.AxisListType.X

P = 128
D = 1024
KD = D // P
META = 16
SEQ = 512
TOK = META + SEQ
HALF = TOK // 2
DFF = 2816
KF = DFF // P
EPS = 1e-6
CH = SEQ // P

HEADS = 8
A_DK = 64
A_QK = HEADS * A_DK
A_V = D
CONV = 4
F_COL = 32
GATE_N = 2 * F_COL

Q_RANK, KV_RANK, ROPE_DIM, NOPE, V_DIM = 256, 128, 32, 64, 64
QK_DIM = NOPE + ROPE_DIM
MLA_SCALE = QK_DIM ** -0.5
RET_DIM = 64
RET = HEADS * RET_DIM
ROPE_THETA = 10000.0
WIN = SEQ + SEQ - P

SLOTS = 4
UNIT = 1024
STARTED = 1
AHEAD = SLOTS - 1

VEC_ROWS = [("norm_gains", 48), ("ffn1_norm_2", 8), ("mix_norm_2", 8), ("ffn2_norm_2", 8), ("final_norm_2", 8),
            ("q_norm_2", 2), ("kv_norm_2", 1), ("a_conv_b", 8), ("a_conv_w", 32)]
VEC = {}
_n = 0
for _name, _rows in VEC_ROWS:
    VEC[_name] = _n
    _n += _rows
NVEC = _n
NGAINS = VEC_ROWS[0][1]

CONST = {}
_n = 0
for _name, _cols in [("ident", P), ("ones", P), ("tri", P), ("selcol", HEADS * HEADS),
                     ("perm", P), ("permpe", QK_DIM), ("block", P), ("invf", 2), ("relpos", WIN), ("relneg", WIN)]:
    CONST[_name] = slice(_n, _n + _cols)
    _n += _cols
NCONST = _n


def constants():
    c = np.zeros((P, NCONST), np.float32)
    p = np.arange(P)
    c[:, CONST["ident"]] = np.eye(P)
    c[:, CONST["ones"]] = 1.0
    c[:, CONST["tri"]] = p[None, :] >= p[:, None]
    for h in range(HEADS):
        c[:, CONST["selcol"].start + h * HEADS + h] = 1.0

    def swap(name, rows, half):
        for m in rows:
            first = (m % (2 * half)) < half
            c[m + half if first else m - half, CONST[name].start + m] = -1.0 if first else 1.0

    swap("perm", range(P), RET_DIM // 2)
    swap("permpe", range(NOPE, QK_DIM), ROPE_DIM // 2)
    for b in range(P // RET_DIM):
        rows = slice(b * RET_DIM, (b + 1) * RET_DIM)
        c[rows, CONST["block"].start + b * RET_DIM:CONST["block"].start + (b + 1) * RET_DIM] = 1.0 / RET_DIM

    def inv(half):
        return (np.float32(ROPE_THETA) ** (-np.arange(half, dtype=np.float32) / np.float32(half))).astype(np.float32)

    c[NOPE:QK_DIM, CONST["invf"].start] = np.tile(inv(ROPE_DIM // 2), 2)
    c[:, CONST["invf"].start + 1] = np.tile(inv(RET_DIM // 2), P // (RET_DIM // 2))
    rel = np.arange(WIN)[None, :] - (SEQ - P) - p[:, None]
    c[:, CONST["relpos"]] = np.maximum(rel, 0)
    c[:, CONST["relneg"]] = np.maximum(-rel, 0)
    return c


def program(nc, dram, out):
    ctx = ExitStack()

    def sb(name, shape, dt=F32):
        return ctx.enter_context(nc.sbuf_tensor(name, shape, dt))

    def region(tensors):
        with ExitStack() as r:
            return {n: r.enter_context(nc.sbuf_tensor(n, s, dt)) for n, s, dt in tensors}

    def region_parts(first, parts):
        with ExitStack() as r:
            common = {n: r.enter_context(nc.sbuf_tensor(n, s, dt)) for n, s, dt in first}
            return [{**common, **region(part)} for part in parts]

    def sems(stage, names):
        return {n: ctx.enter_context(nc.semaphore(f"{stage}_{n}")) for n in names}

    hT = sb("hT", [P, KD * TOK])
    raw = sb("raw", [P, SLOTS, UNIT])
    whi = sb("whi", [P, SLOTS, UNIT], F32R)
    wlo = sb("wlo", [P, SLOTS, UNIT], F32R)
    wa = sb("wa", [P, 2 * TOK])
    wb = sb("wb", [P, 2 * TOK])
    sq = sb("sq", [P, 2 * TOK])
    acc = sb("acc", [P, TOK])
    rbc = sb("rbc", [P, TOK])
    vec = sb("vec", [P, NVEC])
    ident = sb("ident", [P, P])
    ones = sb("ones", [P, P])
    eps = sb("eps", [P, 1])
    halfpi = sb("halfpi", [P, 1])
    cell = sb("cell", [P, 4])
    rcol = sb("rcol", [P, CH + 1])
    small = sb("small", [P, 32])
    gateb = sb("gateb", [HEADS, 2])
    with ExitStack() as r:
        ybuf = r.enter_context(nc.sbuf_tensor("ybuf", [P, KD * TOK], F32))
    xhi = sb("xhi", [P, KD * TOK], F32R)
    xlo = sb("xlo", [P, KD * TOK], F32R)
    t = region([("x_tok", [P, CH, D], F32), ("meta_tok", [META, D], F32), ("vrows", [NVEC, P], F32)])
    x_tok, meta_tok, vrows = t["x_tok"], t["meta_tok"], t["vrows"]
    t = region([("behind_inputs", [P, CH * D + D + P], F32), ("sqbuf", [P, KD * TOK], F32)])
    sqbuf = t["sqbuf"]
    t = region([("hid_hi", [P, KF * TOK], F32R), ("hid_lo", [P, KF * TOK], F32R)])
    hid_hi, hid_lo = t["hid_hi"], t["hid_lo"]
    EW = [SEQ] + [SEQ - P * c for c in range(CH)]
    EO = [sum(EW[:j]) for j in range(len(EW))]
    m1_rest = [("v_hi", [P, CH, D], F32R), ("v_lo", [P, CH, D], F32R), ("vm_hi", [META, D], F32R),
               ("vm_lo", [META, D], F32R), ("y", [P, KD * TOK], F32), ("E", [P, 2 * sum(EW)], F32),
               ("tri", [P, P], F32),
               ("selcol", [P, HEADS * HEADS], F32), ("acol", [P, (CH + 1) * HEADS], F32),
               ("mcol", [P, CH * HEADS], F32)]
    m1_all = [("qkT", [P, KD * TOK], F32)] + m1_rest
    m1 = region(m1_all)
    m1r = region([(n + "_r", shape, F32R) for n, shape, _ in m1_all])
    Shi = region([("Shi", [P, 2 * sum(EW)], F32R)])["Shi"]
    shared = [("cq", [P, 2, SEQ], F32), ("cq_hi", [P, 2, SEQ], F32R), ("cq_lo", [P, 2, SEQ], F32R),
              ("ckv", [P, SEQ], F32), ("ckv_hi", [P, SEQ], F32R), ("ckv_lo", [P, SEQ], F32R),
              ("cosm", [P, SEQ], F32), ("sinm", [P, SEQ], F32), ("kpe", [P, SEQ], F32),
              ("permpe", [P, QK_DIM], F32)]
    m2, m3 = region_parts(shared, [[("cosr", [P, SEQ], F32), ("sinr", [P, SEQ], F32), ("perm", [P, P], F32),
                          ("invf", [P, 2], F32), ("lg", [P, 2 * HEADS], F32), ("lgt", [P, 2 * HEADS], F32),
                          ("rq", [P, 4, SEQ], F32), ("rk", [P, 4, SEQ], F32), ("rv", [P, CH, RET], F32),
                          ("relpos", [P, WIN], F32), ("relneg", [P, WIN], F32),
                          ("dec", [P, 2, WIN], F32), ("decb", [P, WIN], F32), ("RS", [P, CH, SEQ], F32),
                          ("rg", [P, 4, SEQ], F32), ("block", [P, P], F32)], [("qT", [QK_DIM, HEADS, SEQ], F32), ("kT", [QK_DIM, HEADS, SEQ], F32),
                          ("vm", [P, CH, RET], F32), ("PR", [P, 2, CH * SEQ], F32), ("PT", [P, CH * SEQ], F32)]])
    fin = region([("fin", [P, KD, SEQ], F32), ("otok", [P, CH, D], F32)])
    ps = ctx.enter_context(nc.psum_tensor("ps", [P, 8, 512], F32))

    def cols(n):
        return (0, TOK) if n == TOK else (META, SEQ)

    def tile(buf, k, n, start=0):
        o, w = cols(n)
        ap = buf[:, bass.ds(k * TOK + o, w)]
        return ap.rearrange("p (a n) -> p a n", a=2) if n == TOK else ap

    def bank(b, n, rows=P):
        return ps[0:rows, b:b + 2, 0:HALF] if n == TOK else ps[0:rows, b, :]

    def pieces(b, n):
        if n == TOK:
            return [(ps[:, b + c, 0:HALF], HALF * c, HALF) for c in range(2)]
        return [(ps[:, b, :], META, SEQ)]

    def gain(name, k):
        return vec[:, VEC[name] + k:VEC[name] + k + 1]

    def kcols(w, c0, n, k0=0, kn=KD):
        return w[k0 * P:(k0 + kn) * P, c0:c0 + n].rearrange("(k p) n -> p k n", p=P)

    FFN_PIECES = [(0, 8), (8, 8), (16, KF - 16)]
    NU_UP, NU_DOWN = 2 * KF, KD * len(FFN_PIECES)
    NU_FFN = NU_UP + NU_DOWN
    w1, w2 = dram["a_w_in"][0], dram["w_in_2"][0]
    VCOL = 2 * A_QK
    OCOL = VCOL + A_V
    GCOL = OCOL + A_V
    units1 = [kcols(w1, m * P, P) for m in range(8)] + ["gates"]
    units1 += [kcols(w1, VCOL + 512 * n, 512, 2 * j, 2) for n in range(2) for j in range(4)]
    units1 += [kcols(w1, OCOL + m * P, P) for m in range(8)]
    units1 += [kcols(dram["a_w_out"][0], m * P, P) for m in range(8)]
    c_kv, c_kpe = Q_RANK, Q_RANK + KV_RANK
    c_rq = c_kpe + ROPE_DIM
    c_rk, c_rv, c_rg = c_rq + RET, c_rq + 2 * RET, c_rq + 3 * RET
    units2 = [kcols(w2, m * P, P) for m in range(2)] + [kcols(w2, c_kv, P), kcols(w2, c_kpe, ROPE_DIM)]
    units2 += [kcols(w2, c + m * P, P) for c in (c_rq, c_rk) for m in range(4)]
    units2 += [kcols(w2, c_rv, 512, 2 * j, 2) for j in range(4)]
    units2 += [kcols(w2, c_rg + m * P, P) for m in range(4)]
    units2 += [kcols(dram["w_uq_2"][0], 384 * j, 384, 0, 2) for j in range(2)]
    units2 += [kcols(dram["w_ukv_2"][0], 0, 1024, 0, 1)]
    units2 += [kcols(dram["w_o_2"][0], m * P, P) for m in range(8)]
    f_in, f_out = dram["ffn_w_in"][0], dram["ffn_w_out"][0]
    FFNS = [
        dict(gate=f_in[0], gc=0, up=f_in[0], uc=DFF, down=f_out[0], n=TOK, norm=("norm_gains", 0), post=8),
        dict(gate=f_in[1], gc=0, up=f_in[1], uc=DFF, down=f_out[1], n=SEQ, norm=("norm_gains", 32), post=40),
        dict(gate=dram["ffn1_w_gate_2"][0], gc=0, up=dram["ffn1_w_up_2"][0], uc=0, down=dram["ffn1_w_down_2"][0],
             n=SEQ, norm=("ffn1_norm_2", 0), post=None),
        dict(gate=dram["ffn2_w_gate_2"][0], gc=0, up=dram["ffn2_w_up_2"][0], uc=0, down=dram["ffn2_w_down_2"][0],
             n=SEQ, norm=("ffn2_norm_2", 0), post=None),
    ]
    U_M1 = NU_FFN
    FFNS[0]["u0"] = 0
    FFNS[1]["u0"] = U_M1 + len(units1)
    FFNS[2]["u0"] = FFNS[1]["u0"] + NU_FFN
    U_M2 = FFNS[2]["u0"] + NU_FFN
    FFNS[3]["u0"] = U_M2 + len(units2)
    UNITS = FFNS[3]["u0"] + NU_FFN
    assert UNITS % SLOTS == 0

    raw_loaded = [ctx.enter_context(nc.semaphore(f"raw_loaded{s}")) for s in range(SLOTS)]
    hi_done, lo_done, unit_done = (ctx.enter_context(nc.semaphore(n)) for n in ("hi_done", "lo_done", "unit_done"))

    def slot_view(buf, u, a, n):
        return buf[:, u % SLOTS, 0:a * n].rearrange("p (a n) -> p a n", a=a)

    init = sems("init", ["x0", "x1", "x2", "x3", "meta", "ident", "gains", "vecs", "const", "turned", "h_ready", "eps"])
    NORM = ["sq_ready", "summed", "hi_ready", "x_ready"]
    OUTP = ["v_ready", "sq_ready", "acc_done"]
    norm_s, out_s = sems("norm", NORM), sems("out", OUTP)
    res_s = sems("res", ["t_ready", "h_ready"])
    ffn_s = sems("ffn", ["gate_scaled", "silu_done", "banks_free", "product", "hi_ready", "hid_ready"])
    r_s = sems("rms", ["sums", "root", "recip", "spread", "ready"])
    norm_at = [dict(sq_ready=KD * i, summed=i, hi_ready=KD * i, x_ready=KD * i) for i in range(6)]
    out_at = [dict(v_ready=(KD + 2) * i, sq_ready=KD * i, acc_done=(KD + 2) * i) for i in range(6)]
    res_at = [dict(t_ready=KD * i, h_ready=KD * i) for i in range(3)]
    ffn_at = [dict(gate_scaled=KF * i, silu_done=KF * i, banks_free=(KF + 2) * i, product=KF * i, hi_ready=KF * i,
                   hid_ready=(KF + 2) * i) for i in range(4)]
    N0, R0, N1, R1, N2, R2, N3, N4, N5, N6 = range(10)
    R_TOK = {N0: TOK, R0: TOK, N1: TOK}
    r_at = [dict(sums=i, root=i, recip=i, spread=i,
                 ready=sum(2 if j in R_TOK else 1 for j in range(i))) for i in range(10)]
    a1 = sems("mlstm", ["const", "f_loaded", "z_ready", "conv_done", "qk_ready", "pad", "gates_read", "neg_abs", "softplus",
                        "nm_ready", "em_ready", "v_ready", "v_split", "qk_hi", "qk_split", "S_hi", "S_split", "og_raw", "og_ready", "a_turned", "acol_ready", "bc_done",
                        "E_ready", "dots", "S_ready", "num_done", "num_kept", "rden", "d_turned", "rb_done", "y_ready",
                        "y_hi", "y_split"])
    a2 = sems("mix2", ["const", "pos", "decay", "raw_ready", "swapped", "swap_used", "roped", "angle", "trig",
                       "csq", "cstat", "croot", "cnorm", "chi", "csplit", "rg_ready", "rv_ready", "lg1", "lg2", "lg_ready",
                       "arg", "dec_ready", "dots", "RS_ready", "o_done", "ob_ready", "mean", "cent", "csq2",
                       "var", "rroot", "r_ready", "r_hi", "r_split", "dec_used"])
    a3 = sems("mla", ["q_part", "cosine", "q_raw", "swapped", "q_ready", "k_part", "k_ready", "kpe_ready", "v_part",
                      "v_ready", "dots", "max_ready", "P_exp", "P_ready", "turned", "PT_act", "PT_dve",
                      "o_done", "o_hi", "o_split"])
    fin_s = sems("fin", ["t_ready", "turned", "kept_act", "stored"])
    steps = {e: ctx.enter_context(nc.semaphore(f"{e}_step")) for e in ("dve", "act")}
    step_count = {"dve": 0, "act": 0}

    def link(e, name, ins):
        step_count[name] += 1
        ins.then_inc(steps[name], 1)
        e.wait_ge(steps[name], step_count[name])

    def load_ffn(sp, f):
        u0 = f["u0"]
        first = 0
        if u0 == 0:
            for j in range(SLOTS):
                src = kcols(f["gate"] if j % 2 == 0 else f["up"], (f["gc"] if j % 2 == 0 else f["uc"]) + (j // 2) * P, P)
                sp.dma_start(slot_view(raw, j, KD, P), src).then_inc(raw_loaded[j], 16)
            first = 1
        with sp.Fori(first, KF // 2) as i:
            for j in range(4):
                u = u0 + j
                sp.wait_ge(lo_done, 4 * i + (u - SLOTS + 1))
                w, c = (f["gate"], f["gc"]) if j % 2 == 0 else (f["up"], f["uc"])
                src = w.rearrange("(k p) n -> p k n", p=P)[:, :, bass.ds(i * (2 * P) + (c + (j // 2) * P), P)]
                sp.dma_start(slot_view(raw, u, KD, P), src).then_inc(raw_loaded[u % SLOTS], 16)
        u0 += NU_UP
        with sp.Fori(0, 2) as i:
            for j in range(4):
                for q, (k0, kn) in enumerate(FFN_PIECES):
                    u = u0 + 3 * j + q
                    sp.wait_ge(lo_done, 12 * i + (u - SLOTS + 1))
                    src = f["down"][k0 * P:(k0 + kn) * P, :].rearrange("(k p) n -> p k n", p=P)
                    sp.dma_start(slot_view(raw, u, kn, P), src[:, :, bass.ds(i * (4 * P) + j * P, P)]) \
                      .then_inc(raw_loaded[u % SLOTS], 16)

    def load_units(sp, u0, units):
        for j, src in enumerate(units):
            u = u0 + j
            sp.wait_ge(lo_done, u - SLOTS + 1)
            if src == "gates":
                dst = slot_view(raw, u, KD, GATE_N)
                sp.dma_start(dst[:, :, 0:HEADS], kcols(w1, GCOL, HEADS)).then_inc(raw_loaded[u % SLOTS], 16)
                sp.dma_start(dst[:, :, F_COL:F_COL + HEADS], kcols(w1, GCOL + HEADS, HEADS)).then_inc(a1["f_loaded"], 16)
                continue
            sp.dma_start(slot_view(raw, u, src.shape[1], src.shape[2]), src).then_inc(raw_loaded[u % SLOTS], 16)

    def prog_sync(sp):
        for c in range(CH):
            sp.dma_start(x_tok[:, c, :], dram["x"][0, c * P:(c + 1) * P, :]).then_inc(init[f"x{c}"], 16)
        load_ffn(sp, FFNS[0])
        load_units(sp, U_M1, units1)
        load_ffn(sp, FFNS[1])
        load_ffn(sp, FFNS[2])
        load_units(sp, U_M2, units2)
        load_ffn(sp, FFNS[3])
        for c in range(CH):
            sp.wait_ge(fin_s["kept_act"], 2 * (c + 1))
            sp.dma_start(out[0, c * P:(c + 1) * P, :], fin["otok"][:, c, :]).then_inc(fin_s["stored"], 16)
        sp.wait_ge(fin_s["stored"], 16 * CH)

    def pool_lo(pool, u0, u1):
        def lo(u, r=0):
            pool.wait_ge(hi_done, SLOTS * r + (u + 1))
            pool.tensor_tensor(wlo[:, u % SLOTS, :], raw[:, u % SLOTS, :], whi[:, u % SLOTS, :].bitcast(F32),
                               ALU.subtract).then_inc(lo_done, 1)

        whole = (u1 - u0) // SLOTS
        if whole > 0:
            with pool.Fori(0, whole) as r:
                for j in range(SLOTS):
                    lo(u0 + j, r)
        for u in range(u0 + whole * SLOTS, u1):
            lo(u)

    def pool_res(pool, i, n):
        for k in range(1, KD):
            pool.wait_ge(res_s["t_ready"], res_at[i]["t_ready"] + k + 1)
            pool.tensor_tensor(tile(hT, k, n), tile(hT, k, n), tile(wa, k % 2, n), ALU.add).then_inc(res_s["h_ready"], 1)

    def pool_products(pool):
        for h in range(HEADS):
            for q, (j, w) in enumerate(S_PARTS):
                e = e_tile(h, j, None, w)
                pool.wait_ge(a1["S_hi"], 3 * h + q + 1)
                pool.tensor_tensor(e_tile(h, j, m1r["E_r"], w), e, e_tile(h, j, Shi, w).bitcast(F32), ALU.subtract) \
                    .then_inc(a1["S_split"], 1)

    def pool_decays(pool, h):
        dec = m2["dec"][:, h % 2, :]
        pool.wait_ge(a2["arg"], 2 * (h + 1))
        pool.tensor_tensor(dec, dec, m2["decb"][:, :], ALU.mult).then_inc(a2["dec_ready"], 1)

    def pool_rope(pool):
        rows = slice(NOPE, QK_DIM)
        pool.wait_ge(a2["dec_used"], CH * HEADS)
        for h in range(HEADS):
            x = m3["qT"][rows, h, :]
            pool.wait_ge(a3["swapped"], h + 1)
            pool.tensor_tensor(x, x, m3["cosm"][rows, :], ALU.mult).then_inc(a3["cosine"], 1)
            pool.wait_ge(a3["cosine"], h + 1)

    def prog_gpsimd(pool):
        u = 0
        for i, (start, n) in enumerate(((U_M1, TOK), (FFNS[1]["u0"], SEQ), (FFNS[2]["u0"], SEQ))):
            if i == 1:
                pool_lo(pool, u, U_M1 + 25 + AHEAD)
                u = U_M1 + 25 + AHEAD
                pool_products(pool)
            pool_lo(pool, u, start + AHEAD)
            u = start + AHEAD
            pool_res(pool, i, n)
        pool_lo(pool, u, U_M2 + 16 + AHEAD)
        for h in range(2):
            pool_decays(pool, h)
        pool_lo(pool, U_M2 + 16 + AHEAD, U_M2 + 20 + AHEAD)
        for h in range(2, HEADS):
            pool_decays(pool, h)
        pool_rope(pool)
        pool_lo(pool, U_M2 + 20 + AHEAD, UNITS)

    cursor = [0]

    def split_hi(act, u, reg=None, stride=0):
        s = u % SLOTS
        if reg is None:
            if u >= UNITS:
                return
            act.wait_ge(raw_loaded[s], 16 * (u // SLOTS + 1))
            if u == U_M1 + 8:
                act.wait_ge(a1["f_loaded"], 16)
            if u >= SLOTS:
                act.wait_ge(unit_done, STARTED + u - SLOTS + 1)
        else:
            act.wait_ge(raw_loaded[s], reg * (16 * stride // SLOTS) + 16 * (u // SLOTS + 1))
            act.wait_ge(unit_done, STARTED + reg * stride + (u - SLOTS + 1))
        act.activation(whi[:, s, :], raw[:, s, :], ACT.Copy).then_inc(hi_done, 1)

    def split_to(act, last):
        while cursor[0] <= min(last + AHEAD, UNITS - 1):
            split_hi(act, cursor[0])
            cursor[0] += 1

    def act_root(act, i):
        at, n = r_at[i], R_TOK.get(i, SEQ)
        c0 = 0 if n == TOK else 1
        act.wait_ge(r_s["sums"], at["sums"] + 1)
        act.activation(rcol[:, c0:], ps[:, 7, c0:CH + 1], ACT.Sqrt, scale=1.0 / D, bias=eps[:, :]) \
           .then_inc(r_s["root"], 1)
        if i == N6:
            return
        act.wait_ge(r_s["spread"], at["spread"] + 1)
        if i in (R1, R2):
            act.wait_ge(res_s["t_ready"], res_at[1 if i == R1 else 2]["t_ready"] + 1)
        act.activation(rbc[:, META:TOK], ps[:, 6, :], ACT.Copy).then_inc(r_s["ready"], 1)
        if n == TOK:
            act.activation(rbc[:, 0:META], ps[:, 7, 16:16 + META], ACT.Copy).then_inc(r_s["ready"], 1)

    def act_norm(act, i, n, source, offset, squares, name, g0):
        s, at = norm_s, norm_at[i]
        for k in range(KD):
            act.wait_ge(source, offset + k + 1)
            act.activation(tile(xhi, k, n), tile(hT, k, n), ACT.Copy, scale=gain(name, g0 + k)) \
               .then_inc(s["hi_ready"], 1)
            if squares:
                act.activation(tile(sqbuf, k, n), tile(hT, k, n), ACT.Square).then_inc(s["sq_ready"], 1)

    def act_ffn(act, i):
        f, s, at = FFNS[i], ffn_s, ffn_at[i]
        n, u0 = f["n"], f["u0"]

        def gated(r, b):
            act.wait_ge(s["gate_scaled"], at["gate_scaled"] + r * 2 + (b + 1))
            act.activation(tile(wa, b, n), tile(wa, b, n), ACT.Silu).then_inc(s["silu_done"], 1)
            act.wait_ge(s["product"], at["product"] + r * 2 + (b + 1))
            act.activation(tile(hid_hi, r * 2 + b, n), tile(wb, b, n), ACT.Copy).then_inc(s["hi_ready"], 1)

        for b in range(2):
            split_to(act, u0 + 2 * b + 1)
            gated(0, b)
        with act.Fori(1, KF // 2) as r:
            for b in range(2):
                for e in (2 * b + AHEAD, 2 * b + AHEAD + 1):
                    split_hi(act, u0 + e, r, 4)
                gated(r, b)
        cursor[0] += NU_UP - 4

    def act_out(act, i, n, add, u0, per, norm=None):
        s, at = out_s, out_at[i]
        split_to(act, u0 - 1)

        def square(d, j):
            act.wait_ge(s["acc_done"], at["acc_done"] + d + (j + 2))
            if add:
                act.wait_ge(s["v_ready"], at["v_ready"] + d + (j + 3))
                value = tile(hT, d + j, n)
            else:
                act.wait_ge(unit_done, STARTED + d * per + (u0 + per * (j + 1)))
                value = out_bank(i, j % 4, n)
            act.activation(tile(sq, j % 2, n), value, ACT.Square).then_inc(s["sq_ready"], 1)
            if norm is not None:
                g = vec[:, bass.ds(d + (VEC[norm[1]] + j), 1)]
                act.activation(tile(xhi, d + j, n), value, ACT.Copy, scale=g).then_inc(norm_s["hi_ready"], 1)

        if u0 + 8 * per >= UNITS:
            for j in range(KD):
                split_to(act, u0 + per * (j + 1) - 1)
                square(0, j)
            return
        with act.Fori(0, 2) as r:
            for j in range(4):
                for e in range(per):
                    split_hi(act, u0 + per * j + AHEAD + e, r, 4 * per)
                square(r * 4, j)
        cursor[0] += 8 * per

    def act_mlstm(act):
        s, u0 = a1, U_M1
        for m in range(8):
            split_to(act, u0 + m)
            if m >= 1:
                act.wait_ge(s["conv_done"], m)
                act.activation(m1["qkT"][:, (m - 1) * TOK:m * TOK], cacc((m - 1) % 2), ACT.Silu) \
                   .then_inc(s["qk_ready"], 1)
        act.wait_ge(s["conv_done"], 8)
        act.activation(m1["qkT"][:, 7 * TOK:8 * TOK], cacc(1), ACT.Silu).then_inc(s["qk_ready"], 1)
        split_to(act, u0 + 8)
        act.wait_ge(s["neg_abs"], 1)
        link(act, "act", act.activation(gc, gc, ACT.Exp))
        act.activation(gc, gc, ACT.Ln, bias=ones[0:HEADS, 0:1]).then_inc(s["softplus"], 1)
        for n in range(2):
            split_to(act, u0 + 9 + 4 * n + 3)
            act.wait_ge(unit_done, STARTED + u0 + 9 + 4 * n + 4)
            for c in V_ORDER:
                hi, _, bank_, r = v_part(n, c)
                act.activation(hi, bank_, ACT.Copy, scale=r).then_inc(s["v_ready"], 1)
        act.wait_ge(s["nm_ready"], 1)
        act.activation(gc, gc, ACT.Exp, scale=-1.0).then_inc(s["em_ready"], 1)
        for m in range(8):
            split_to(act, u0 + 17 + m)
            act.wait_ge(s["og_raw"], m + 1)
            act.activation(tile(m1["y"], m, SEQ), tile(m1["y"], m, SEQ), ACT.Sigmoid).then_inc(s["og_ready"], 1)
        act.wait_ge(s["const"], 32)
        act.activation(m1r["selcol_r"][:, :], m1["selcol"][:, :], ACT.Copy).then_inc(s["qk_hi"], 1)
        act.wait_ge(unit_done, STARTED + u0 + 25)

        def qk_hi(i):
            m = i // 2 + 4 * (i % 2)
            act.activation(xhi[:, m * TOK:(m + 1) * TOK], m1["qkT"][:, m * TOK:(m + 1) * TOK], ACT.Copy).then_inc(s["qk_hi"], 1)

        qk_hi(0)
        qk_hi(1)
        act.wait_ge(s["acol_ready"], 2)
        for h in range(HEADS):
            act.wait_ge(s["bc_done"], h + 1)
            if h >= 2:
                act.wait_ge(s["num_done"], h - 1)
            for j in range(CH + 1):
                rows, t0 = (META, 0) if j == 0 else (P, P * (j - 1))
                act.activation(e_tile(h, j), ps[0:rows, 0, t0:SEQ], ACT.Exp,
                               bias=m1["acol"][0:rows, j * HEADS + h:j * HEADS + h + 1]).then_inc(s["E_ready"], 1)
            if h == 0:
                for i in range(2, 8):
                    qk_hi(i)
                act.wait_ge(s["qk_split"], 8)
            for j, w in S_PARTS:
                act.wait_ge(s["S_ready"], (CH + 1) * h + (j + 1 if j < 2 else CH + 1))
                act.activation(e_tile(h, j, Shi, w), e_tile(h, j, None, w), ACT.Copy).then_inc(s["S_hi"], 1)
        for h in range(HEADS):
            act.wait_ge(s["y_ready"], h + 1)
            act.activation(tile(xhi, h, SEQ), tile(wb, h % 2, SEQ), ACT.Copy).then_inc(s["y_hi"], 1)

    def act_mix2(act):
        s, u0 = a2, U_M2
        act.wait_ge(s["lg1"], 1)
        link(act, "act", act.activation(m2["lgt"][:, :], m2["lgt"][:, :], ACT.Exp))
        act.activation(m2["lgt"][:, :], m2["lgt"][:, :], ACT.Ln, bias=ones[:, 0:1]).then_inc(s["lg2"], 1)
        for e in range(12):
            split_to(act, u0 + e)
            if e == 1:
                for k in range(2):
                    act.wait_ge(s["raw_ready"], k + 1)
                    act.activation(sq[:, k * TOK:k * TOK + SEQ], m2["cq"][:, k, :], ACT.Square).then_inc(s["csq"], 1)
            if e == 2:
                act.wait_ge(s["raw_ready"], 3)
                act.wait_ge(s["cstat"], 1)
                act.activation(sq[:, 0:SEQ], m2["ckv"][:, :], ACT.Square).then_inc(s["csq"], 1)
            if e == 4:
                for j, (co, si) in enumerate((("cosm", "sinm"), ("cosr", "sinr"))):
                    act.wait_ge(s["angle"], 2 * j + 2)
                    act.activation(m2[si][:, :], m2[si][:, :], ACT.Sin).then_inc(s["trig"], 1)
                    act.activation(m2[co][:, :], m2[co][:, :], ACT.Sin, scale=-1.0, bias=halfpi[:, :]) \
                       .then_inc(s["trig"], 1)
            if e == 5:
                for j, rank in enumerate((Q_RANK, KV_RANK)):
                    act.wait_ge(s["cstat"], j + 1)
                    inv = wb[:, j * TOK:j * TOK + SEQ]
                    link(act, "act", act.activation(inv, ps[:, 2 + j, :], ACT.Ln, scale=1.0 / rank, bias=eps[:, :]))
                    act.activation(inv, inv, ACT.Exp, scale=-0.5).then_inc(s["croot"], 1)
            if e == 8:
                for k in range(3):
                    act.wait_ge(s["cnorm"], k + 1)
                    act.activation(m2["cq_hi"][:, k, :] if k < 2 else m2["ckv_hi"][:, :],
                                   m2["cq"][:, k, :] if k < 2 else m2["ckv"][:, :], ACT.Copy).then_inc(s["chi"], 1)
        split_to(act, u0 + 15)
        act.wait_ge(unit_done, STARTED + u0 + 16)
        for c in range(CH):
            act.activation(m2["rv"][:, c, :], ps[:, 2 + c, :], ACT.Copy, scale=rcol[:, c + 1:c + 2]) \
               .then_inc(s["rv_ready"], 1)
        act.wait_ge(s["lg_ready"], 1)
        def decays(h):
            if h >= 1:
                act.wait_ge(s["dec_ready"], h)
            if h >= 2:
                act.wait_ge(s["RS_ready"], CH * (h - 1))
            act.activation(m2["dec"][:, h % 2, :], m2["relpos"][:, :], ACT.Exp, scale=m2["lg"][:, h:h + 1]) \
               .then_inc(s["arg"], 1)
            act.activation(m2["decb"][:, :], m2["relneg"][:, :], ACT.Exp, scale=m2["lg"][:, HEADS + h:HEADS + h + 1]) \
               .then_inc(s["arg"], 1)

        decays(0)
        decays(1)
        for m in range(4):
            split_to(act, u0 + 16 + m)
            act.wait_ge(s["raw_ready"], 13 + m)
            act.activation(m2["rg"][:, m, :], m2["rg"][:, m, :], ACT.Silu).then_inc(s["rg_ready"], 1)
        decays(2)
        for h in range(2, HEADS + 1):
            m = h // 2 - 1
            if h % 2 == 0:
                act.wait_ge(s["o_done"], m + 1)
                act.activation(tile(wa, m % 2, SEQ), ps[:, m % 2, :], ACT.Copy).then_inc(s["ob_ready"], 1)
            if h + 1 < HEADS:
                decays(h + 1)
            if h % 2 == 0:
                if m < 3:
                    act_centered(act, m)
            else:
                act_deviation(act, m)
                act_ret_hi(act, m)

    def act_centered(act, m):
        act.wait_ge(a2["cent"], m + 1)
        act.activation(tile(sq, m % 2, SEQ), tile(wa, m % 2, SEQ), ACT.Square).then_inc(a2["csq2"], 1)

    def act_deviation(act, m):
        act.wait_ge(a2["var"], m + 1)
        link(act, "act", act.activation(rbc[:, 0:SEQ], ps[:, 7, :], ACT.Ln, bias=eps[:, :]))
        act.activation(rbc[:, 0:SEQ], rbc[:, 0:SEQ], ACT.Exp, scale=-0.5).then_inc(a2["rroot"], 1)

    def act_ret_hi(act, m):
        act.wait_ge(a2["r_ready"], m + 1)
        act.activation(tile(xhi, 4 + m, SEQ), tile(wa, m % 2, SEQ), ACT.Copy).then_inc(a2["r_hi"], 1)

    def act_mla(act):
        s, u0 = a3, U_M2 + 20
        act.wait_ge(a2["dec_used"], CH * HEADS)
        for h in range(HEADS):
            if h == 1:
                act_centered(act, 3)
            if h == 2:
                act_deviation(act, 3)
            if h == 4:
                act_ret_hi(act, 3)
            split_to(act, u0 + h // 4)
            if h % 4 == 3:
                act.wait_ge(unit_done, STARTED + u0 + h // 4 + 1)
            else:
                act.wait_ge(s["q_part"], 3 * (h // 4) + h % 4 + 1)
            act.activation(m3["qT"][:, h, :], ps[0:QK_DIM, MLA_Q_BANK[h % 2], :], ACT.Copy) \
               .then_inc(s["q_raw"], 1)
        for h in range(HEADS):
            act.wait_ge(s["k_part"], h + 1)
            act.activation(m3["kT"][0:NOPE, h, :], ps[0:NOPE, MLA_K_BANK[h % 2], :], ACT.Copy) \
               .then_inc(s["k_ready"], 1)
        for c in range(CH):
            if c < CH - 1:
                act.wait_ge(s["v_part"], c + 1)
            else:
                act.wait_ge(unit_done, STARTED + u0 + 3)
            act.activation(m3["vm"][:, c, :], ps[:, 6 + c % 2, :], ACT.Copy).then_inc(s["v_ready"], 1)
        split_to(act, u0 + 2)

        def scores_exp(h, c):
            if h >= 2:
                act.wait_ge(s["turned"], CH * (h - 2) + c + 1)
            act.wait_ge(s["max_ready"], CH * h + c + 1)
            act.activation(m3["PR"][:, h % 2, c * SEQ:(c + 1) * SEQ], ps[:, c % 2, :], ACT.Exp, scale=MLA_SCALE,
                           bias=small[:, c:c + 1], accum_out=small[:, 8 + c:9 + c]).then_inc(s["P_exp"], 1)

        def keep_turned(h, c):
            if h >= 1:
                act.wait_ge(s["o_done"], h)
            act.wait_ge(s["turned"], CH * h + c + 1)
            act.activation(m3["PT"][:, c * SEQ:(c + 1) * SEQ], ps[:, 2 + c, :], ACT.Copy).then_inc(s["PT_act"], 1)

        def out_hi(m):
            act.wait_ge(s["o_done"], 2 * m + 2)
            act.activation(tile(xhi, m, SEQ), ps[:, 6 + m % 2, :], ACT.Copy).then_inc(s["o_hi"], 1)

        for c in range(CH):
            scores_exp(0, c)
        for h in range(HEADS):
            if h + 1 < HEADS:
                scores_exp(h + 1, 0)
            keep_turned(h, 0)
            if h % 2 == 0 and h >= 2:
                out_hi(h // 2 - 1)
            if h + 1 < HEADS:
                scores_exp(h + 1, 1)
                scores_exp(h + 1, 2)
            keep_turned(h, 2)
            keep_turned(h, 3)
            if h + 1 < HEADS:
                scores_exp(h + 1, 3)
        out_hi(HEADS // 2 - 1)

    def prog_scalar(act):
        act.dma_start(ident[:, :], dram["const"][:, CONST["ident"]]).then_inc(init["ident"], 16)
        rows = {
            "norm_gains": dram["norm_gains"].rearrange("a g (k p) -> (a g k) p", p=P),
            "a_conv_w": dram["a_conv_w"].rearrange("a j (k p) -> (a j k) p", p=P),
            "final_norm_2": dram["final_norm_2"].rearrange("(k p) -> k p", p=P),
        }
        for name, n in VEC_ROWS:
            src = rows[name] if name in rows else dram[name].rearrange("a (k p) -> (a k) p", p=P)
            act.dma_start(vrows[VEC[name]:VEC[name] + n, :], src).then_inc(init["gains" if name == "norm_gains" else "vecs"], 16)
            if name == "norm_gains":
                act.dma_start(meta_tok[:, :], dram["meta_tokens"]).then_inc(init["meta"], 16)
        act.dma_start(ones[:, :], dram["const"][:, CONST["ones"]]).then_inc(init["const"], 16)
        act.dma_start(gateb[:, :], dram["a_gate_b"].rearrange("a (t h) -> h (a t)", t=2),
                      allow_slow_non_contiguous=True).then_inc(init["const"], 16)
        split_to(act, -1)
        act_norm(act, 0, TOK, init["h_ready"], 1, True, "norm_gains", 0)
        split_to(act, FFNS[0]["u0"])
        act_root(act, N0)
        act_ffn(act, 0)
        act_out(act, 0, TOK, False, NU_UP, 3)
        act_root(act, R0)
        act_norm(act, 1, TOK, res_s["h_ready"], res_at[0]["h_ready"], True, "norm_gains", 16)
        split_to(act, U_M1)
        act_root(act, N1)
        for name in ("tri", "selcol"):
            act.dma_start(m1[name][:, :], dram["const"][:, CONST[name]]).then_inc(a1["const"], 16)
        act_mlstm(act)
        act_out(act, 1, SEQ, False, U_M1 + 25, 1)
        act_root(act, R1)
        act_norm(act, 2, SEQ, res_s["h_ready"], res_at[1]["h_ready"], True, "norm_gains", 32)
        split_to(act, FFNS[1]["u0"])
        act_root(act, N2)
        act_ffn(act, 1)
        act_out(act, 2, SEQ, False, FFNS[1]["u0"] + NU_UP, 3)
        act_root(act, R2)
        act_norm(act, 3, SEQ, res_s["h_ready"], res_at[2]["h_ready"], True, "ffn1_norm_2", 0)
        split_to(act, FFNS[2]["u0"])
        act_root(act, N3)
        act_ffn(act, 2)
        act_out(act, 3, SEQ, True, FFNS[2]["u0"] + NU_UP, 3, norm=(4, "mix_norm_2"))
        act.dma_start(m2["RS"][:, 0, :].bitcast(I32), dram["positions_2"].broadcast_to([P, SEQ])) \
           .then_inc(a2["pos"], 16)
        for j, name in enumerate(("ret_decay_fwd_2", "ret_decay_bwd_2")):
            act.dma_start(m2["lg"][:, j * HEADS:(j + 1) * HEADS], dram[name].broadcast_to([P, HEADS])) \
               .then_inc(a2["decay"], 16)
        for name in ("permpe", "perm", "block", "invf", "relpos", "relneg"):
            act.dma_start(m2[name][:, :], dram["const"][:, CONST[name]]).then_inc(a2["const"], 16)
        split_to(act, U_M2)
        act_root(act, N4)
        act_mix2(act)
        act_mla(act)
        act_out(act, 4, SEQ, True, U_M2 + 23, 1)
        act_norm(act, 5, SEQ, out_s["v_ready"], out_at[4]["v_ready"] + 2, False, "ffn2_norm_2", 0)
        split_to(act, FFNS[3]["u0"])
        act_root(act, N5)
        act_ffn(act, 3)
        act_out(act, 5, SEQ, True, FFNS[3]["u0"] + NU_UP, 3)
        act_root(act, N6)
        act.wait_ge(r_s["recip"], r_at[N6]["recip"] + 1)
        for c in range(CH):
            for j in range(2):
                g = 2 * c + j
                act.wait_ge(fin_s["turned"], g + 1)
                act.activation(fin["otok"][:, c, j * 512:(j + 1) * 512], ps[:, g % 4, :], ACT.Copy,
                               scale=rcol[:, c + 1:c + 2]) \
                   .then_inc(fin_s["kept_act"], 1)

    def zpad(b):
        return m1["E"][:, b * 532:b * 532 + 3 + TOK]

    def cacc(b):
        return m1["E"][:, 1064 + b * TOK:1064 + (b + 1) * TOK]

    def e_tile(h, j, buf=None, w=None):
        o = (h % 2) * sum(EW) + EO[j]
        return (m1["E"] if buf is None else buf)[0:META if j == 0 else P, o:o + (EW[j] if w is None else w)]

    S_PARTS = [(0, EW[0]), (1, EW[1]), (2, sum(EW[2:]))]
    S_PART_OF = [1, 2, 3, 3, 3]

    def v_part(n, c):
        rows, j = (META, 0) if c < 0 else (P, c + 1)
        hi, lo = ((m1["vm_hi"], m1["vm_lo"]) if c < 0 else (m1["v_hi"][:, c], m1["v_lo"][:, c]))
        half = slice(n * 512, (n + 1) * 512)
        return hi[:, half], lo[:, half], ps[0:rows, V_BANK[n][c], :], rcol[0:rows, j:j + 1]

    ga, gb = wa[0:HEADS, 0:TOK], wa[0:HEADS, TOK:2 * TOK]
    gc, go = wb[0:HEADS, 0:TOK], wb[0:HEADS, TOK:2 * TOK]
    V_ORDER = [0, -1, 1, 2, 3]
    V_BANK = [{0: 4, -1: 5, 1: 1, 2: 2, 3: 3}, {0: 0, 1: 6, 2: 7, 3: 4, -1: 5}]
    V_TURN = [(0, -1, 1, 2, 3), (0, 1, 2, 3, -1)]
    V_Z = {0: 6, 1: 7, 2: 8}
    QK_BANK = [4, 5, 6, 7, 2]

    MLA_Q_BANK, MLA_K_BANK = (0, 4), (5, 1)

    def dve_rms(v, i):
        s, at, n = r_s, r_at[i], R_TOK.get(i, SEQ)
        c0 = 0 if n == TOK else 1
        v.wait_ge(s["root"], at["root"] + 1)
        v.reciprocal(rcol[:, c0:], rcol[:, c0:]).then_inc(s["recip"], 1)

    def r_ready(v, i):
        v.wait_ge(r_s["ready"], r_at[i]["ready"] + (2 if i in R_TOK else 1))

    def lo_of_x(v, i, k, n, name, g0):
        v.wait_ge(norm_s["hi_ready"], norm_at[i]["hi_ready"] + k + 1)
        v.scalar_tensor_tensor(out=tile(xlo, k, n), in0=tile(hT, k, n), scalar=gain(name, g0 + k),
                               in1=tile(xhi, k, n).bitcast(F32), op0=ALU.mult, op1=ALU.subtract) \
         .then_inc(norm_s["x_ready"], 1)

    def sum_square(v, i, k, n):
        def add(a, b, *needs):
            for count in needs:
                v.wait_ge(steps["dve"], count)
            step_count["dve"] += 1
            return v.tensor_tensor(tile(sqbuf, a, n), tile(sqbuf, a, n), tile(sqbuf, b, n), ALU.add) \
                    .then_inc(steps["dve"], 1)

        if k % 2 == 1:
            v.wait_ge(norm_s["sq_ready"], norm_at[i]["sq_ready"] + k + 1)
            add(k - 1, k)
        if k % 4 == 3:
            add(k - 3, k - 1, step_count["dve"])
        if k == KD - 1:
            v.wait_ge(steps["dve"], step_count["dve"])
            v.memset(cell[:, 0:1], 0.0).then_inc(norm_s["summed"], 1)

    def dve_norm(v, i, n, name, g0, squares=False):
        for k in range(KD):
            lo_of_x(v, i, k, n, name, g0)
            if squares:
                sum_square(v, i, k, n)

    def dve_ffn(v, i, rms):
        f, s, at, n, u0 = FFNS[i], ffn_s, ffn_at[i], FFNS[i]["n"], FFNS[i]["u0"]
        r_ready(v, rms)
        with v.Fori(0, KF // 2) as r:
            for b in range(2):
                v.wait_ge(unit_done, STARTED + r * 4 + (u0 + 2 * b + 1))
                v.wait_ge(s["banks_free"], at["banks_free"] + r * 2 + (b + 1))
                v.tensor_tensor(tile(wa, b, n), bank(2 * b if n == TOK else b, n), tile(rbc, 0, n), ALU.mult) \
                 .then_inc(s["gate_scaled"], 1)
                v.wait_ge(s["silu_done"], at["silu_done"] + r * 2 + (b + 1))
                v.wait_ge(unit_done, STARTED + r * 4 + (u0 + 2 * b + 2))
                v.wait_ge(s["hid_ready"], at["hid_ready"] + r * 2 + (b + 1))
                v.tensor_tensor(tile(wb, b, n), tile(wa, b, n), bank(4 + 2 * b if n == TOK else 2 + b, n), ALU.mult) \
                 .then_inc(s["banks_free"], 1)
                v.wait_ge(s["banks_free"], at["banks_free"] + r * 2 + (b + 3))
                v.tensor_tensor(tile(wb, b, n), tile(wb, b, n), tile(rbc, 0, n), ALU.mult).then_inc(s["product"], 1)
                v.wait_ge(s["hi_ready"], at["hi_ready"] + r * 2 + (b + 1))
                v.tensor_tensor(tile(hid_lo, r * 2 + b, n), tile(wb, b, n),
                                tile(hid_hi, r * 2 + b, n).bitcast(F32), ALU.subtract).then_inc(s["hid_ready"], 1)

    def free_ffn(v):
        v.memset(cell[:, 0:1], 0.0).then_inc(ffn_s["banks_free"], 2)
        v.memset(cell[:, 1:2], 0.0).then_inc(ffn_s["hid_ready"], 2)

    def free_out(v, i, n):
        v.memset(tile(sq, 1, n), 0.0).then_inc(out_s["acc_done"], 1)
        v.memset(tile(acc, 0, n), 0.0).then_inc(out_s["acc_done"], 1)
        v.memset(cell[:, 2:3], 0.0).then_inc(out_s["v_ready"], 2)

    def dve_out(v, i, n, value, u0, per, gains=None, add=None, norm=None):
        s, at = out_s, out_at[i]
        with v.Fori(0, 2) as r:
            for j in range(4):
                if at["sq_ready"] + j > 0:
                    v.wait_ge(s["sq_ready"], at["sq_ready"] + r * 4 + j)
                v.wait_ge(s["acc_done"], at["acc_done"] + r * 4 + (j + 2))
                v.tensor_tensor(tile(acc, 0, n), tile(acc, 0, n), tile(sq, (j + 1) % 2, n), ALU.add) \
                 .then_inc(s["acc_done"], 1)
                if add is None:
                    v.wait_ge(s["sq_ready"], at["sq_ready"] + r * 4 + (j + 1))
                    g0, factor = gains
                    g = vec[:, bass.ds(r * 4 + (VEC["norm_gains"] + g0 + j), 1)]
                    v.tensor_scalar(tile(value, r * 4 + j, n), out_bank(i, j, n), g, factor, ALU.mult, ALU.mult) \
                     .then_inc(s["v_ready"], 1)
                else:
                    v.wait_ge(unit_done, STARTED + r * (4 * per) + (u0 + per * (j + 1)))
                    v.scalar_tensor_tensor(out=tile(value, r * 4 + j, n), in0=out_bank(i, j, n), scalar=add,
                                           in1=tile(value, r * 4 + j, n), op0=ALU.mult, op1=ALU.add) \
                     .then_inc(s["v_ready"], 1)
                if norm is not None:
                    v.wait_ge(norm_s["hi_ready"], norm_at[norm[0]]["hi_ready"] + r * 4 + (j + 1))
                    v.scalar_tensor_tensor(out=tile(xlo, r * 4 + j, n), in0=tile(value, r * 4 + j, n),
                                           scalar=vec[:, bass.ds(r * 4 + (VEC[norm[1]] + j), 1)],
                                           in1=tile(xhi, r * 4 + j, n).bitcast(F32), op0=ALU.mult, op1=ALU.subtract) \
                     .then_inc(norm_s["x_ready"], 1)

    def dve_res(v, i, n, value, rms, norm, name, g0):
        s, at = res_s, res_at[i]
        if n == TOK:
            r_ready(v, rms)
            r0 = tile(rbc, 0, n)
        else:
            v.wait_ge(r_s["spread"], r_at[rms]["spread"] + 1)
            r0 = ps[:, 6, :]
        v.tensor_tensor(tile(wa, 0, n), tile(value, 0, n), r0, ALU.mult).then_inc(s["t_ready"], 1)
        v.wait_ge(s["t_ready"], at["t_ready"] + 1)
        v.tensor_tensor(tile(hT, 0, n), tile(hT, 0, n), tile(wa, 0, n), ALU.add).then_inc(s["h_ready"], 1)
        if n == SEQ:
            r_ready(v, rms)
        for k in range(1, KD + 2):
            if k < KD:
                if k >= 2:
                    v.wait_ge(s["h_ready"], at["h_ready"] + k - 1)
                v.tensor_tensor(tile(wa, k % 2, n), tile(value, k, n), tile(rbc, 0, n), ALU.mult).then_inc(s["t_ready"], 1)
            if k >= 2:
                lo_of_x(v, norm, k - 2, n, name, g0)

    def dve_mlstm(v):
        s, u0 = a1, U_M1
        v.wait_ge(norm_s["x_ready"], norm_at[1]["x_ready"] + KD)
        v.memset(zpad(0)[:, 0:3], 0.0)
        v.memset(zpad(1)[:, 0:3], 0.0)
        v.memset(go, 1.0).then_inc(s["pad"], 1)
        v.wait_ge(s["pad"], 1)
        r_ready(v, N1)
        for m in range(8):
            b = m % 2
            v.wait_ge(unit_done, STARTED + u0 + m + 1)
            if m >= 2:
                v.wait_ge(s["conv_done"], m - 1)
            v.tensor_tensor(zpad(b)[:, 3:3 + TOK].rearrange("p (a n) -> p a n", a=2), bank(2 * (m % 3), TOK),
                            tile(rbc, 0, TOK), ALU.mult).then_inc(s["z_ready"], 1)
            v.wait_ge(s["z_ready"], m + 1)
            if m >= 2:
                v.wait_ge(s["qk_ready"], m - 1)
            w = [gain("a_conv_w", 8 * j + m) for j in range(CONV)]
            link(v, "dve", v.tensor_scalar(cacc(b), zpad(b)[:, 3:3 + TOK], w[3], gain("a_conv_b", m), ALU.mult, ALU.add))
            for j in (2, 1):
                link(v, "dve", v.scalar_tensor_tensor(out=cacc(b), in0=zpad(b)[:, j:j + TOK], scalar=w[j], in1=cacc(b),
                                                      op0=ALU.mult, op1=ALU.add))
            v.scalar_tensor_tensor(out=cacc(b), in0=zpad(b)[:, 0:TOK], scalar=w[0], in1=cacc(b), op0=ALU.mult,
                                   op1=ALU.add).then_inc(s["conv_done"], 1)
        v.wait_ge(unit_done, STARTED + u0 + 9)
        g2 = [x.rearrange("p (a n) -> p a n", a=2) for x in (ga, gb)]
        rg2 = tile(rbc, 0, TOK)
        link(v, "dve", v.tensor_tensor(g2[0], bank(6, TOK)[0:HEADS], rg2[0:HEADS], ALU.mult))
        f_rows = slice(F_COL, F_COL + HEADS)
        v.tensor_tensor(g2[1], bank(6, TOK)[f_rows], rg2[f_rows], ALU.mult).then_inc(s["gates_read"], 1)
        link(v, "dve", v.tensor_scalar(ga, ga, gateb[:, 0:1], None, ALU.add))
        v.wait_ge(s["gates_read"], 1)
        link(v, "dve", v.tensor_scalar(gb, gb, gateb[:, 1:2], None, ALU.add))
        v.scalar_tensor_tensor(out=gc, in0=gb, scalar=-1.0, in1=gb, op0=ALU.mult, op1=ALU.min).then_inc(s["neg_abs"], 1)
        v.wait_ge(s["softplus"], 1)
        link(v, "dve", v.scalar_tensor_tensor(out=gb, in0=gb, scalar=0.0, in1=gc, op0=ALU.min, op1=ALU.subtract))
        link(v, "dve", v.tensor_tensor_scan(gc, go, gb, 0.0, ALU.mult, ALU.add))
        link(v, "dve", v.tensor_tensor(ga, ga, gc, ALU.subtract))
        link(v, "dve", v.tensor_tensor_scan(gb, ga, ga, 0.0, ALU.max, ALU.max))
        link(v, "dve", v.tensor_tensor(gc, gc, gb, ALU.add))
        v.tensor_scalar(gb, gb, -1.0, None, ALU.mult).then_inc(s["nm_ready"], 1)
        v.memset(m1["acol"][:, :], 0.0).then_inc(s["rden"], 1)
        v.wait_ge(s["rden"], 1)
        for n in range(2):
            for q, c in enumerate(V_ORDER):
                hi, lo, bank_, r = v_part(n, c)
                v.wait_ge(s["v_ready"], 5 * n + q + 1)
                v.scalar_tensor_tensor(out=lo, in0=bank_, scalar=r, in1=hi.bitcast(F32), op0=ALU.mult, op1=ALU.subtract) \
                 .then_inc(s["v_split"], 1)
        v.wait_ge(s["a_turned"], 1)
        link(v, "dve", v.tensor_copy(m1["acol"][0:META, 0:HEADS], ps[0:META, 3, 0:HEADS]))
        v.tensor_copy(m1["acol"][:, HEADS:], ps[:, 3, HEADS:(CH + 1) * HEADS]).then_inc(s["acol_ready"], 1)
        v.tensor_copy(m1["mcol"][:, :], ps[:, 3, (CH + 1) * HEADS:(2 * CH + 1) * HEADS]).then_inc(s["acol_ready"], 1)

        for m in range(8):
            v.wait_ge(unit_done, STARTED + u0 + 17 + m + 1)
            v.tensor_tensor(tile(m1["y"], m, SEQ), ps[:, 1 + m % 2, :], rbc[:, META:TOK], ALU.mult).then_inc(s["og_raw"], 1)

        def keep(h):
            v.wait_ge(s["num_done"], h + 1)
            v.wait_ge(s["og_ready"], h + 1)
            v.tensor_tensor(tile(m1["y"], h, SEQ), ps[:, 1, :], tile(m1["y"], h, SEQ), ALU.mult).then_inc(s["num_kept"], 1)

        def qk_lo(i):
            m = i // 2 + 4 * (i % 2)
            v.wait_ge(s["qk_hi"], i + 2)
            v.tensor_tensor(xlo[:, m * TOK:(m + 1) * TOK], m1["qkT"][:, m * TOK:(m + 1) * TOK],
                            xhi[:, m * TOK:(m + 1) * TOK].bitcast(F32), ALU.subtract).then_inc(s["qk_split"], 1)

        qk_lo(0)
        qk_lo(1)
        v.wait_ge(a1["const"], 32)
        for h in range(HEADS):
            for j in range(CH + 1):
                g = (CH + 1) * h + j
                e = e_tile(h, j)
                v.wait_ge(s["E_ready"], g + 1)
                if j >= 1:
                    link(v, "dve", v.scalar_tensor_tensor(out=e[:, 0:P], in0=e[:, 0:P], scalar=1.0, in1=m1["tri"][:, :],
                                                          op0=ALU.min, op1=ALU.mult))
                v.wait_ge(s["dots"], g + 1)
                v.scalar_tensor_tensor(out=e, in0=ps[0:META if j == 0 else P, QK_BANK[j], 0:EW[j]],
                                       scalar=A_DK ** -0.5, in1=e, op0=ALU.mult, op1=ALU.mult).then_inc(s["S_ready"], 1)
            if h >= 1:
                keep(h - 1)
            else:
                for i in range(2, 8):
                    qk_lo(i)
        keep(HEADS - 1)
        v.wait_ge(s["em_ready"], 1)
        em = gc[:, META:TOK]
        den = ps[0:HEADS, 3, :]
        dn = ga[:, META:TOK]
        link(v, "dve", v.scalar_tensor_tensor(out=dn, in0=den, scalar=-1.0, in1=em, op0=ALU.mult, op1=ALU.max))
        v.tensor_tensor(dn, den, dn, ALU.max).then_inc(s["rden"], 1)
        v.wait_ge(s["d_turned"], 1)
        v.reciprocal(m1["acol"][:, 0:CH * HEADS], ps[:, 3, 0:CH * HEADS]).then_inc(s["rden"], 1)
        free_out(v, 1, SEQ)
        for h in range(HEADS + 1):
            if h < HEADS:
                v.wait_ge(s["rb_done"], h + 1)
                if h >= 2:
                    v.wait_ge(s["y_split"], h - 1)
                v.tensor_tensor(tile(wb, h % 2, SEQ), tile(m1["y"], h, SEQ), ps[:, 4 + h % 4, :], ALU.mult) \
                 .then_inc(s["y_ready"], 1)
            if h >= 1:
                v.wait_ge(s["y_hi"], h)
                v.tensor_tensor(tile(xlo, h - 1, SEQ), tile(wb, (h - 1) % 2, SEQ), tile(xhi, h - 1, SEQ).bitcast(F32),
                                ALU.subtract).then_inc(s["y_split"], 1)

    MAGIC = 12582912.0
    TWO_PI = 6.283185307179586
    PI_1 = 6.25
    PI_2 = float(np.float32(np.round((TWO_PI - PI_1) * 2.0 ** 16) / 2.0 ** 16))
    PI_3 = TWO_PI - PI_1 - PI_2
    PI_SAFE = 3.1415925

    def dve_normed(v, m):
        ob = tile(wa, m % 2, SEQ)
        v.wait_ge(a2["rroot"], m + 1)
        v.tensor_tensor(ob, ob, rbc[:, 0:SEQ], ALU.mult).then_inc(a2["r_ready"], 1)

    def dve_ret_lo(v, m):
        v.wait_ge(a2["r_hi"], m + 1)
        v.tensor_tensor(tile(xlo, 4 + m, SEQ), tile(wa, m % 2, SEQ), tile(xhi, 4 + m, SEQ).bitcast(F32), ALU.subtract) \
         .then_inc(a2["r_split"], 1)

    def mix_bank(e):
        return (0, 1, 4, 5)[e] if e < 4 else e % 2

    def dve_mix2(v):
        s, u0 = a2, U_M2
        v.wait_ge(s["decay"], 32)
        v.scalar_tensor_tensor(out=m2["lgt"][:, :], in0=m2["lg"][:, :], scalar=-1.0, in1=m2["lg"][:, :],
                               op0=ALU.mult, op1=ALU.min).then_inc(s["lg1"], 1)
        v.wait_ge(s["pos"], 16)
        v.wait_ge(s["const"], 96)
        posi, posf = m2["RS"][:, 0, :].bitcast(I32), m2["RS"][:, 1, :]
        turn = m2["RS"][:, 2, :]
        link(v, "dve", v.tensor_copy(posf, posi))

        def angles(j, co, si):
            ang, ab = m2[si][:, :], m2[co][:, :]
            link(v, "dve", v.tensor_scalar(ang, posf, m2["invf"][:, j:j + 1], None, ALU.mult))
            link(v, "dve", v.tensor_scalar(turn, ang, 1.0 / TWO_PI, None, ALU.mult))
            link(v, "dve", v.tensor_scalar(turn, turn, MAGIC, None, ALU.add))
            link(v, "dve", v.tensor_scalar(turn, turn, MAGIC, None, ALU.subtract))
            for part in (PI_1, PI_2, PI_3):
                link(v, "dve", v.scalar_tensor_tensor(out=ang, in0=turn, scalar=-part, in1=ang, op0=ALU.mult, op1=ALU.add))
            v.tensor_scalar(ang, ang, -PI_SAFE, PI_SAFE, ALU.max, ALU.min).then_inc(s["angle"], 1)
            v.wait_ge(s["angle"], 2 * j + 1)
            v.scalar_tensor_tensor(out=ab, in0=ang, scalar=-1.0, in1=ang, op0=ALU.mult, op1=ALU.max) \
             .then_inc(s["angle"], 1)

        def latent(k):
            x = m2["cq"][:, k, :] if k < 2 else m2["ckv"][:, :]
            hi = m2["cq_hi"][:, k, :] if k < 2 else m2["ckv_hi"][:, :]
            lo = m2["cq_lo"][:, k, :] if k < 2 else m2["ckv_lo"][:, :]
            return x, hi, lo

        def rope(r):
            rows = slice(NOPE, QK_DIM) if r == 0 else slice(0, P)
            co, si = ("cosm", "sinm") if r == 0 else ("cosr", "sinr")
            x = (m2["kpe"][rows, :] if r == 0 else (m2["rq"] if r < 5 else m2["rk"])[:, (r - 1) % 4, :])
            tmp = wa[rows, 0:SEQ]
            if r < 2:
                v.wait_ge(s["trig"], 2 * r + 2)
            v.wait_ge(s["swapped"], r + 1)
            v.tensor_tensor(tmp, m2[si][rows, :], ps[rows, 6 + r % 2, :], ALU.mult).then_inc(s["swap_used"], 1)
            link(v, "dve", v.tensor_tensor(x, x, m2[co][rows, :], ALU.mult))
            v.wait_ge(s["swap_used"], r + 1)
            v.tensor_tensor(x, x, tmp, ALU.add).then_inc(s["roped"], 1)

        raws = [m2["cq"][:, 0, :], m2["cq"][:, 1, :], m2["ckv"][:, :], m2["kpe"][NOPE:QK_DIM, :]]
        raws += [m2[x][:, m, :] for x in ("rq", "rk") for m in range(4)] + [None] * 4
        raws += [m2["rg"][:, m, :] for m in range(4)]
        at_unit = list(range(12)) + [16, 17, 18, 19]

        def leave(e):
            rows = ROPE_DIM if e == 3 else P
            v.wait_ge(unit_done, STARTED + u0 + at_unit[e] + 1)
            dst = raws[at_unit[e]]
            v.scalar_tensor_tensor(out=dst, in0=ps[0:rows, mix_bank(e), :], scalar=RET_DIM ** -0.5 if 8 <= e < 12 else 1.0,
                                   in1=rbc[0:rows, META:TOK], op0=ALU.mult, op1=ALU.mult).then_inc(s["raw_ready"], 1)

        def latents(step):
            if step == 0:
                v.wait_ge(s["croot"], 2)
                for k in range(3):
                    x = latent(k)[0]
                    r0 = 0 if k < 2 else TOK
                    v.scalar_tensor_tensor(out=x, in0=x, scalar=gain("q_norm_2", k) if k < 2 else gain("kv_norm_2", 0),
                                           in1=wb[:, r0:r0 + SEQ], op0=ALU.mult, op1=ALU.mult).then_inc(s["cnorm"], 1)
            else:
                for k in range(3):
                    x, hi, lo = latent(k)
                    v.wait_ge(s["chi"], k + 1)
                    v.tensor_tensor(lo, x, hi.bitcast(F32), ALU.subtract).then_inc(s["csplit"], 1)

        r_ready(v, N4)
        for e in range(16):
            leave(e)
            if e == 1:
                angles(0, "cosm", "sinm")
            if e == 2:
                angles(1, "cosr", "sinr")
                v.wait_ge(s["lg2"], 1)
                v.scalar_tensor_tensor(out=m2["lg"][:, :], in0=m2["lg"][:, :], scalar=0.0, in1=m2["lgt"][:, :],
                                       op0=ALU.min, op1=ALU.subtract).then_inc(s["lg_ready"], 1)
            if 5 <= e <= 13:
                rope(e - 5)
                v.wait_ge(s["roped"], e - 4)
            if e == 6:
                latents(0)
            if e == 9:
                latents(1)

        def center(m):
            ob = tile(wa, m % 2, SEQ)
            v.wait_ge(s["mean"], m + 1)
            v.tensor_tensor(ob, ob, ps[:, 6, :], ALU.subtract).then_inc(s["cent"], 1)

        def gate(m):
            ob = tile(wa, m % 2, SEQ)
            v.wait_ge(s["rg_ready"], m + 1)
            v.wait_ge(s["csq2"], m + 1)
            link(v, "dve", v.tensor_tensor(ob, ob, m2["rg"][:, m, :], ALU.mult))

        def normed(m):
            dve_normed(v, m)

        def ret_lo(m):
            dve_ret_lo(v, m)

        after = {}
        for m in range(4):
            after.update({(2 * m + 3, 2): (center, m), (2 * m + 4, 0): (gate, m)})
            if m < 3:
                after.update({(2 * m + 4, 3): (normed, m), (2 * m + 5, 0): (ret_lo, m)})
        for h in range(HEADS + 4):
            if h < HEADS:
                v.wait_ge(s["dec_ready"], h + 1)
            for c in range(CH):
                g = CH * h + c
                if h < HEADS:
                    v.wait_ge(s["dots"], g + 1)
                    if h >= 1:
                        v.wait_ge(s["dec_used"], g - CH + 1)
                    o = (SEQ - P) - P * c
                    v.tensor_tensor(m2["RS"][:, c, :], m2["dec"][:, h % 2, o:o + SEQ], ps[:, 2 + c, :], ALU.mult) \
                     .then_inc(s["RS_ready"], 1)
                if (h, c) in after:
                    step, m = after[h, c]
                    step(m)

    def dve_mla(v):
        s, u0 = a3, U_M2 + 20
        rows = slice(NOPE, QK_DIM)
        for h in range(HEADS):
            x, tmp = m3["qT"][rows, h, :], wb[rows, (h % 2) * TOK:(h % 2) * TOK + SEQ]
            v.wait_ge(s["swapped"], h + 1)
            if h >= 2:
                v.wait_ge(s["q_ready"], h - 1)
            link(v, "dve", v.tensor_tensor(tmp, m3["sinm"][rows, :], ps[rows, 2 + h % 2, :], ALU.mult))
            v.wait_ge(s["cosine"], h + 1)
            v.tensor_tensor(x, x, tmp, ALU.add).then_inc(s["q_ready"], 1)
            v.tensor_copy(m3["kT"][rows, h, :], m3["kpe"][rows, :]).then_inc(s["kpe_ready"], 1)
            if h == 1:
                dve_normed(v, 3)
            if h == 3:
                dve_ret_lo(v, 3)
                free_out(v, 4, SEQ)

        def maximum(h, c):
            g = CH * h + c
            v.wait_ge(s["dots"], g + 1)
            link(v, "dve", v.reduce_max(small[:, 24 + c:25 + c], ps[:, c % 2, :], AX_X))
            if h >= 1:
                v.wait_ge(s["P_exp"], g - CH + 1)
            v.tensor_scalar(small[:, c:c + 1], small[:, 24 + c:25 + c], -MLA_SCALE, None, ALU.mult) \
             .then_inc(s["max_ready"], 1)

        def scale(h, c):
            v.wait_ge(s["P_exp"], CH * h + c + 1)
            link(v, "dve", v.reciprocal(small[:, 16 + c:17 + c], small[:, 8 + c:9 + c]))
            x = m3["PR"][:, h % 2, c * SEQ:(c + 1) * SEQ]
            v.tensor_scalar(x, x, small[:, 16 + c:17 + c], None, ALU.mult).then_inc(s["P_ready"], 1)

        def keep_turned(h, c):
            if h >= 1:
                v.wait_ge(s["o_done"], h)
            v.wait_ge(s["turned"], CH * h + c + 1)
            v.tensor_copy(m3["PT"][:, c * SEQ:(c + 1) * SEQ], ps[:, 2 + c, :]).then_inc(s["PT_dve"], 1)

        def out_lo(m):
            v.wait_ge(s["o_hi"], m + 1)
            v.tensor_tensor(tile(xlo, m, SEQ), ps[:, 6 + m % 2, :], tile(xhi, m, SEQ).bitcast(F32), ALU.subtract) \
             .then_inc(s["o_split"], 1)

        maximum(0, 0)
        for c in range(1, CH):
            maximum(0, c)
            scale(0, c - 1)
        maximum(1, 0)
        scale(0, CH - 1)
        for h in range(HEADS):
            if h + 1 < HEADS:
                maximum(h + 1, 1)
                scale(h + 1, 0)
            keep_turned(h, 1)
            if h % 2 == 0 and h >= 2:
                out_lo(h // 2 - 1)
            if h + 1 < HEADS:
                for c in (2, 3):
                    maximum(h + 1, c)
                    scale(h + 1, c - 1)
                if h + 2 < HEADS:
                    maximum(h + 2, 0)
                scale(h + 1, 3)
        out_lo(HEADS // 2 - 1)

    def prog_vector(v):
        v.memset(eps[:, :], EPS).then_inc(init["eps"], 1)
        v.memset(halfpi[:, :], TWO_PI / 4).then_inc(init["eps"], 1)
        v.wait_ge(init["turned"], 1)
        v.tensor_copy(vec[:, 0:NGAINS], ps[:, 5, 0:NGAINS]).then_inc(init["h_ready"], 1)
        hv = hT[:, :].rearrange("p (k t) -> p k t", k=KD)
        v.wait_ge(init["turned"], 2)
        link(v, "dve", v.tensor_copy(hv[:, :, 0:META], ps[:, 4, 0:KD * META].rearrange("p (k t) -> p k t", k=KD)))
        for k in range(KD):
            v.wait_ge(init["turned"], 3 + k)
            v.tensor_copy(hv[:, k, META:TOK], ps[:, k % 4, :]).then_inc(init["h_ready"], 1)
        v.wait_ge(init["turned"], KD + 3)
        v.tensor_copy(vec[:, NGAINS:], ps[:, 5, NGAINS:NVEC]).then_inc(init["h_ready"], 1)
        free_ffn(v)
        dve_norm(v, 0, TOK, "norm_gains", 0, True)
        dve_rms(v, N0)
        free_out(v, 0, TOK)
        dve_ffn(v, 0, N0)
        dve_out(v, 0, TOK, ybuf, NU_UP, 3, gains=(8, 0.5))
        dve_rms(v, R0)
        dve_res(v, 0, TOK, ybuf, R0, 1, "norm_gains", 16)
        for k in range(1, KD):
            sum_square(v, 1, k, TOK)
        dve_rms(v, N1)
        dve_mlstm(v)
        dve_out(v, 1, SEQ, m1["y"], U_M1 + 25, 1, gains=(24, 1.0))
        dve_rms(v, R1)
        free_ffn(v)
        dve_res(v, 1, SEQ, m1["y"], R1, 2, "norm_gains", 32)
        for k in range(1, KD):
            sum_square(v, 2, k, SEQ)
        dve_rms(v, N2)
        free_out(v, 2, SEQ)
        dve_ffn(v, 1, N2)
        dve_out(v, 2, SEQ, ybuf, FFNS[1]["u0"] + NU_UP, 3, gains=(40, 0.5))
        dve_rms(v, R2)
        free_ffn(v)
        dve_res(v, 2, SEQ, ybuf, R2, 3, "ffn1_norm_2", 0)
        for k in range(1, KD):
            sum_square(v, 3, k, SEQ)
        dve_rms(v, N3)
        free_out(v, 3, SEQ)
        dve_ffn(v, 2, N3)
        dve_out(v, 3, SEQ, hT, FFNS[2]["u0"] + NU_UP, 3, add=0.5, norm=(4, "mix_norm_2"))
        dve_rms(v, N4)
        dve_mix2(v)
        dve_mla(v)
        dve_out(v, 4, SEQ, hT, U_M2 + 23, 1, add=1.0)
        free_ffn(v)
        dve_norm(v, 5, SEQ, "ffn2_norm_2", 0)
        dve_rms(v, N5)
        free_out(v, 5, SEQ)
        dve_ffn(v, 3, N5)
        dve_out(v, 5, SEQ, hT, FFNS[3]["u0"] + NU_UP, 3, add=0.5)
        for k in range(KD):
            v.wait_ge(out_s["v_ready"], out_at[5]["v_ready"] + k + 3)
            v.tensor_scalar(fin["fin"][:, k, :], tile(hT, k, SEQ), gain("final_norm_2", k), None, ALU.mult) \
             .then_inc(fin_s["t_ready"], 1)
        dve_rms(v, N6)


    def out_bank(i, j, n):
        return bank(2 * (j % 2) if n == TOK else j % 2 + (0 if i == 1 else 4), n)

    def product(pe, outs, lhs, rhs, first, last):
        n = 0
        for l, r in ((0, 0), (0, 1), (1, 0)):
            for o, x in zip(outs, rhs):
                ins = pe.matmul(o, lhs[l], x[r], start=first and n == 0, stop=last and n == 2)
            n += 1
        return ins

    def w_tile(u, k, n=P, c0=0, width=P):
        return [w[:, u % SLOTS, k * n + c0:k * n + c0 + width] for w in (whi, wlo)]

    def x_cols(k, o, w):
        return [x[:, k * TOK + o:k * TOK + o + w] for x in (xhi, xlo)]

    def project(pe, b, n, u, norm=None, width=P, wn=P, before_last=None):
        for k in range(KD):
            if before_last is not None and k == KD - 1:
                before_last()
            if norm is not None:
                pe.wait_ge(norm_s["x_ready"], norm_at[norm]["x_ready"] + k + 1)
            p = pieces(b, n)
            ins = product(pe, [o[0:width] for o, _, _ in p], w_tile(u, k, wn, 0, width), [x_cols(k, o, w) for _, o, w in p],
                          k == 0, k == KD - 1)
        return ins

    def column_sums(pe, sources, n):
        chunks = ([(0, 0)] if n == TOK else []) + [(c + 1, META + c * P) for c in range(CH)]
        for c, o in chunks:
            for q, (buf, o0) in enumerate(sources):
                ins = pe.matmul(ps[:, 7, c:c + 1], buf[:, o0 + o:o0 + o + P], ones[:, 0:1], start=q == 0,
                                stop=q == len(sources) - 1, skip_group_check=True)
        ins.then_inc(r_s["sums"], 1)

    def sum_out(pe, i, n):
        pe.wait_ge(out_s["acc_done"], out_at[i]["acc_done"] + KD + 2)
        pe.wait_ge(out_s["sq_ready"], out_at[i]["sq_ready"] + KD)
        column_sums(pe, [(acc, 0), (sq, (KD - 1) % 2 * TOK)], n)

    def sum_norm(pe, i, n):
        pe.wait_ge(norm_s["summed"], norm_at[i]["summed"] + 1)
        column_sums(pe, [(sqbuf, 0), (sqbuf, 4 * TOK)], n)

    def first_tiles(pe, norm, n, banks, units):
        for k in range(KD):
            pe.wait_ge(norm_s["x_ready"], norm_at[norm]["x_ready"] + k + 1)
            for b, u in zip(banks, units):
                if k == 0:
                    pe.wait_ge(lo_done, u + 1)
                p = pieces(b, n)
                ins = product(pe, [o for o, _, _ in p], w_tile(u, k), [x_cols(k, o, w) for _, o, w in p], k == 0, k == KD - 1)
                if k == KD - 1:
                    ins.then_inc(unit_done, 1)

    def spread(pe, rms):
        pe.wait_ge(r_s["recip"], r_at[rms]["recip"] + 1)
        if rms in R_TOK:
            pe.transpose(ps[:, 7, 16:16 + META], rcol[0:META, 0:1].broadcast_to([META, P]), ident[0:META, 0:META])
        for c in range(CH):
            ins = pe.transpose(ps[:, 6, c * P:(c + 1) * P], rcol[:, c + 1:c + 2].broadcast_to([P, P]), ident[:, :])
        ins.then_inc(r_s["spread"], 1)

    def pe_ffn(pe, i, norm, rms, acc_of=None):
        f, s, at, n, u0 = FFNS[i], ffn_s, ffn_at[i], FFNS[i]["n"], FFNS[i]["u0"]

        def unit(r, b, g, between=None):
            u = u0 + 2 * b + g
            pe.wait_ge(lo_done, r * 4 + (u + 1))
            pe.wait_ge(s["banks_free"], at["banks_free"] + r * 2 + (b + 1))
            p = pieces((4 * g + 2 * b) if n == TOK else (2 * g + b), n)
            for k in range(KD):
                if between is not None:
                    between(k)
                ins = product(pe, [o for o, _, _ in p], w_tile(u, k), [x_cols(k, o, w) for _, o, w in p],
                              k == 0, k == KD - 1)
            ins.then_inc(unit_done, 1)

        def operand(k):
            pe.wait_ge(norm_s["x_ready"], norm_at[norm]["x_ready"] + k + 1)

        def sums(k):
            if k == (1 if n == TOK else KD - 2):
                sum_norm(pe, norm, n)
            if n == TOK and k == KD - 3:
                spread(pe, rms)

        def spreading(k):
            if n == SEQ and k == 1:
                spread(pe, rms)

        if acc_of is not None:
            sum_out(pe, acc_of, n)
            unit(0, 0, 0, operand)
            unit(0, 0, 1)
            unit(0, 1, 0, spreading)
        else:
            pe.wait_ge(s["banks_free"], at["banks_free"] + 1)
            first_tiles(pe, norm, n, (0, 4) if n == TOK else (0, 2), (u0, u0 + 1))
            unit(0, 1, 0, sums)
        if n == TOK:
            pe.wait_ge(r_s["ready"], r_at[rms]["ready"] + 2)
        unit(0, 1, 1, spreading if acc_of is None else None)
        with pe.Fori(1, KF // 2) as r:
            for b in range(2):
                for g in range(2):
                    unit(r, b, g)
        if n == TOK:
            pe.wait_ge(s["gate_scaled"], at["gate_scaled"] + KF)
        u0 += NU_UP
        v_at = out_at[[0, 2, 3, 5][i]]["v_ready"]
        with pe.Fori(0, 2) as r:
            for j in range(4):
                pe.wait_ge(out_s["v_ready"], v_at + r * 4 + (j + 1))
                b = 2 * (j % 2) if n == TOK else 4 + j % 2
                p = pieces(b, n)
                for q, (k0, kn) in enumerate(FFN_PIECES):
                    u = u0 + 3 * j + q
                    pe.wait_ge(lo_done, r * 12 + (u + 1))
                    for k in range(k0, k0 + kn):
                        if j == 0:
                            pe.wait_ge(s["hid_ready"], at["hid_ready"] + k + 3)
                        ins = product(pe, [o for o, _, _ in p], w_tile(u, k - k0),
                                      [[x[:, k * TOK + o:k * TOK + o + w] for x in (hid_hi, hid_lo)] for _, o, w in p],
                                      k == 0, k == KF - 1)
                    ins.then_inc(unit_done, 1)

    def pe_out(pe, i, u0, order, ready):
        s, at = out_s, out_at[i]
        with pe.Fori(0, 2) as r:
            for j in range(4):
                pe.wait_ge(s["v_ready"], at["v_ready"] + r * 4 + (j + 1))
                pe.wait_ge(lo_done, r * 4 + (u0 + j + 1))
                for q, k in enumerate(order):
                    if j == 0:
                        sem, count = ready(k)
                        pe.wait_ge(sem, count)
                    ins = product(pe, [ps[:, j % 2 + (0 if i == 1 else 4), :]], w_tile(u0 + j, k), [x_cols(k, META, SEQ)], q == 0, q == KD - 1)
                ins.then_inc(unit_done, 1)

    def pe_mlstm(pe):
        s, u0 = a1, U_M1
        first_tiles(pe, 1, TOK, (0, 2), (u0, u0 + 1))
        for m in range(2, 8):
            pe.wait_ge(lo_done, u0 + m + 1)
            if m == 3:
                spread(pe, N1)
            if m >= 3:
                pe.wait_ge(s["z_ready"], m - 2)
            project(pe, 2 * (m % 3), TOK, u0 + m, None).then_inc(unit_done, 1)
            if m == 2:
                sum_norm(pe, 1, TOK)
        pe.wait_ge(lo_done, u0 + 9)
        pe.wait_ge(r_s["ready"], r_at[N1]["ready"] + 2)
        project(pe, 6, TOK, u0 + 8, width=F_COL + HEADS, wn=GATE_N).then_inc(unit_done, 1)
        for n in range(2):
            if n == 1:
                pe.wait_ge(s["gates_read"], 1)
            for j in range(4):
                u = u0 + 9 + 4 * n + j
                pe.wait_ge(lo_done, u + 1)
                for kk in range(2):
                    k = 2 * j + kk
                    for c in V_TURN[n]:
                        if n == 0 and k == 0 and c in V_Z:
                            pe.wait_ge(s["z_ready"], V_Z[c])
                        if n == 1 and k == 0 and c in (3, -1):
                            pe.wait_ge(s["v_split"], 1 if c == 3 else 2)
                        rows = META if c < 0 else P
                        x = x_cols(k, 0 if c < 0 else META + P * c, rows)
                        ins = product(pe, [ps[0:rows, V_BANK[n][c], :]], x, [w_tile(u, kk, 512, 0, 512)], k == 0, k == KD - 1)
                ins.then_inc(unit_done, 1)
        pe.wait_ge(s["v_split"], 5)
        pe.wait_ge(s["nm_ready"], 1)
        pe.transpose(ps[0:META, 3, 0:HEADS], ga[:, 0:META], ident[0:HEADS, 0:HEADS])
        for c in range(CH):
            pe.transpose(ps[:, 3, (c + 1) * HEADS:(c + 2) * HEADS], ga[:, META + P * c:META + P * (c + 1)],
                         ident[0:HEADS, 0:HEADS])
            ins = pe.transpose(ps[:, 3, (c + CH + 1) * HEADS:(c + CH + 2) * HEADS], gb[:, META + P * c:META + P * (c + 1)],
                               ident[0:HEADS, 0:HEADS])
        ins.then_inc(s["a_turned"], 1)
        for m in range(8):
            pe.wait_ge(lo_done, u0 + 17 + m + 1)
            if m >= 2:
                pe.wait_ge(s["og_raw"], m - 1)
            project(pe, 1 + m % 2, SEQ, u0 + 17 + m, None).then_inc(unit_done, 1)

        def broadcast(h):
            for c in range(CH):
                ins = pe.transpose(ps[:, 0, c * P:(c + 1) * P],
                                   m1["mcol"][:, c * HEADS + h:c * HEADS + h + 1].broadcast_to([P, P]), ident[:, :])
            ins.then_inc(s["bc_done"], 1)

        def dots(h, j):
            rows = slice(64 * (h % 2), 64 * (h % 2) + 64)
            ks, q0 = (0, META) if j == 0 else (META + P * (j - 1), META + P * (j - 1))
            kw = META if j == 0 else P
            kt, qt = (4 + h // 2) * TOK, (h // 2) * TOK
            ks, q0 = kt + ks, qt + q0
            product(pe, [ps[0:kw, QK_BANK[j], 0:EW[j]]], [x[rows, ks:ks + kw] for x in (xhi, xlo)],
                    [[x[rows, q0:q0 + EW[j]] for x in (xhi, xlo)]], True, True).then_inc(s["dots"], 1)

        pe.wait_ge(s["qk_ready"], 8)
        pe.wait_ge(s["const"], 32)
        pe.wait_ge(s["v_split"], 10)
        pe.wait_ge(s["og_raw"], 8)
        pe.wait_ge(s["acol_ready"], 2)
        broadcast(0)
        pe.wait_ge(s["qk_split"], 2)
        for j in range(CH + 1):
            dots(0, j)
        for h in range(HEADS):
            if h + 1 < HEADS:
                pe.wait_ge(s["E_ready"], (CH + 1) * (h + 1))
                broadcast(h + 1)
                pe.wait_ge(s["qk_split"], 2 * ((h + 1) // 2) + 2)
            for j in range(CH + 1):
                pe.wait_ge(s["S_ready"], (CH + 1) * h + j + 1)
                if h + 1 < HEADS:
                    dots(h + 1, j)
            if h >= 1:
                pe.wait_ge(s["num_kept"], h)
            for j in range(CH + 1):
                pe.wait_ge(s["S_split"], 3 * h + S_PART_OF[j])
                t0 = 0 if j == 0 else P * (j - 1)
                rows = META if j == 0 else P
                S = [e_tile(h, j, Shi), e_tile(h, j, m1r["E_r"])]
                vv = [m1["vm_hi"], m1["vm_lo"]] if j == 0 else [m1["v_hi"][:, j - 1], m1["v_lo"][:, j - 1]]
                for q, x in enumerate(S):
                    pe.matmul(ps[0:HEADS, 3, t0:SEQ], m1r["selcol_r"][0:rows, h * HEADS:(h + 1) * HEADS], x,
                              start=h == 0 and j == 0 and q == 0, stop=h == HEADS - 1 and j == CH and q == 1,
                              skip_group_check=True)
                for q, (l, r) in enumerate(((0, 0), (0, 1), (1, 0))):
                    ins = pe.matmul(ps[:, 1, t0:SEQ], vv[l][0:rows, h * P:(h + 1) * P], S[r], start=j == 0 and q == 0,
                                    stop=j == CH and q == 2, skip_group_check=True)
            ins.then_inc(s["num_done"], 1)
        pe.wait_ge(s["rden"], 2)
        for c in range(CH):
            ins = pe.transpose(ps[:, 3, c * HEADS:(c + 1) * HEADS], ga[:, META + P * c:META + P * (c + 1)],
                               ident[0:HEADS, 0:HEADS])
        ins.then_inc(s["d_turned"], 1)
        pe.wait_ge(s["rden"], 3)
        for h in range(HEADS):
            if h >= 4:
                pe.wait_ge(s["y_ready"], h - 3)
            for c in range(CH):
                ins = pe.transpose(ps[:, 4 + h % 4, c * P:(c + 1) * P],
                                   m1["acol"][:, c * HEADS + h:c * HEADS + h + 1].broadcast_to([P, P]), ident[:, :])
            ins.then_inc(s["rb_done"], 1)

    def pe_mix2(pe):
        s, u0 = a2, U_M2

        def swap(r):
            pe.wait_ge(s["raw_ready"], r + 4)
            if r >= 2:
                pe.wait_ge(s["swap_used"], r - 1)
            if r == 0:
                pe.wait_ge(s["const"], 96)
                ins = pe.matmul(ps[0:QK_DIM, 6, :], m2["permpe"][NOPE:QK_DIM, :], m2["kpe"][NOPE:QK_DIM, :], start=True, stop=True)
            else:
                x = (m2["rq"] if r < 5 else m2["rk"])[:, (r - 1) % 4, :]
                ins = pe.matmul(ps[:, 6 + r % 2, :], m2["perm"][:, :], x, start=True, stop=True)
            ins.then_inc(s["swapped"], 1)

        for e in range(12):
            pe.wait_ge(lo_done, u0 + e + 1)
            if e >= 4:
                pe.wait_ge(s["raw_ready"], e - 3 if e < 6 else e - 1)
            ready = 4 if e == 0 else None
            if e == 3:
                ins = project(pe, mix_bank(e), SEQ, u0 + e, None, ROPE_DIM, ROPE_DIM)
            else:
                ins = project(pe, mix_bank(e), SEQ, u0 + e, ready, before_last=(lambda: sum_out(pe, 3, SEQ)) if e == 0 else None)
            ins.then_inc(unit_done, 1)
            if e == 1:
                spread(pe, N4)
            if e == 2:
                for k in range(2):
                    pe.wait_ge(s["csq"], k + 1)
                    ins = pe.matmul(ps[:, 2, :], ones[:, :], sq[:, k * TOK:k * TOK + SEQ], start=k == 0, stop=k == 1)
                ins.then_inc(s["cstat"], 1)
            if e == 3:
                pe.wait_ge(s["csq"], 3)
                pe.matmul(ps[:, 3, :], ones[:, :], sq[:, 0:SEQ], start=True, stop=True).then_inc(s["cstat"], 1)
            if e >= 4:
                swap(e - 4)
        pe.wait_ge(s["croot"], 2)
        for j in range(4):
            pe.wait_ge(lo_done, u0 + 12 + j + 1)
            for kk in range(2):
                k = 2 * j + kk
                for c in range(CH):
                    ins = product(pe, [ps[:, 2 + c, :]], x_cols(k, META + P * c, P), [w_tile(u0 + 12 + j, kk, 512, 0, 512)],
                                  k == 0, k == KD - 1)
            ins.then_inc(unit_done, 1)
            if j == 0:
                swap(8)
        for m in range(4):
            pe.wait_ge(lo_done, u0 + 16 + m + 1)
            pe.wait_ge(s["raw_ready"], 11 + m)
            project(pe, m % 2, SEQ, u0 + 16 + m, None).then_inc(unit_done, 1)

        def dots(h, c):
            rows = slice(64 * (h % 2), 64 * (h % 2) + 64)
            pe.matmul(ps[:, 2 + c, :], m2["rk"][rows, h // 2, c * P:(c + 1) * P], m2["rq"][rows, h // 2, :],
                      start=True, stop=True).then_inc(s["dots"], 1)

        pe.wait_ge(s["rv_ready"], 4)
        pe.wait_ge(s["roped"], 9)
        pe.wait_ge(s["raw_ready"], 16)
        for c in range(CH):
            dots(0, c)
        for h in range(HEADS):
            m = h // 2
            rows = slice(64 * (h % 2), 64 * (h % 2) + 64)
            if h % 2 == 0 and m >= 2:
                pe.wait_ge(s["ob_ready"], m - 1)
            for c in range(CH):
                pe.wait_ge(s["RS_ready"], CH * h + c + 1)
                if h + 1 < HEADS:
                    dots(h + 1, c)
                pe.matmul(ps[rows, m % 2, :], m2["rv"][:, c, h * RET_DIM:(h + 1) * RET_DIM], m2["RS"][:, c, :],
                          start=c == 0, stop=c == CH - 1).then_inc(s["dec_used"], 1)
                if h >= 2 and c == 1:
                    (pe_mean if h % 2 == 0 else pe_variance)(pe, m - 1)
            if h % 2 == 1:
                pe.wait_ge(s["dec_used"], CH * (h + 1))
                pe.transpose(ps[0:2, 6, 0:2], ident[0:2, 0:2], ident[0:2, 0:2]).then_inc(s["o_done"], 1)

    def pe_mean(pe, m):
        pe.wait_ge(a2["ob_ready"], m + 1)
        pe.matmul(ps[:, 6, :], m2["block"][:, :], tile(wa, m % 2, SEQ), start=True, stop=True).then_inc(a2["mean"], 1)

    def pe_variance(pe, m):
        pe.wait_ge(a2["csq2"], m + 1)
        pe.matmul(ps[:, 7, :], m2["block"][:, :], tile(sq, m % 2, SEQ), start=True, stop=True).then_inc(a2["var"], 1)

    def pe_mla(pe):
        s, u0 = a3, U_M2 + 20
        rows = slice(NOPE, QK_DIM)

        def swap(h):
            pe.wait_ge(s["q_raw"], h + 1)
            if h >= 2:
                pe.wait_ge(s["q_ready"], h - 1)
            pe.matmul(ps[0:QK_DIM, 2 + h % 2, :], m3["permpe"][rows, :], m3["qT"][rows, h, :], start=True, stop=True) \
              .then_inc(s["swapped"], 1)

        pe.wait_ge(a2["csplit"], 3)
        for h in range(HEADS):
            u, hh = u0 + h // 4, h % 4
            if hh == 0:
                pe.wait_ge(lo_done, u + 1)
            if h >= 2:
                pe.wait_ge(s["q_raw"], h - 1)
            for k in range(2):
                ins = product(pe, [ps[0:QK_DIM, MLA_Q_BANK[h % 2], :]], w_tile(u, k, 4 * QK_DIM, hh * QK_DIM, QK_DIM),
                              [[m2["cq_hi"][:, k, :], m2["cq_lo"][:, k, :]]], k == 0, k == 1)
            ins.then_inc(unit_done if hh == 3 else s["q_part"], 1)
            if h == 1:
                pe_mean(pe, 3)
            if h == 2:
                pe_variance(pe, 3)
            if h >= 1:
                swap(h - 1)
        swap(HEADS - 1)
        u = u0 + 2
        pe.wait_ge(lo_done, u + 1)
        lat = [m2["ckv_hi"][:, :], m2["ckv_lo"][:, :]]
        for h in range(HEADS):
            if h >= 2:
                pe.wait_ge(s["k_ready"], h - 1)
            product(pe, [ps[0:NOPE, MLA_K_BANK[h % 2], :]], w_tile(u, 0, UNIT, h * P, NOPE), [lat], True, True) \
                .then_inc(s["k_part"], 1)
        wv = [w[:, u % SLOTS, :].rearrange("p (h c) -> p h c", h=HEADS)[:, :, NOPE:NOPE + V_DIM] for w in (whi, wlo)]
        for c in range(CH):
            if c >= 2:
                pe.wait_ge(s["v_ready"], c - 1)
            o = ps[:, 6 + c % 2, :].rearrange("p (h c) -> p h c", h=HEADS)
            product(pe, [o], [x[:, c * P:(c + 1) * P] for x in lat], [wv], True, True) \
                .then_inc(s["v_part"] if c < CH - 1 else unit_done, 1)

        def dots(h, c):
            g = CH * h + c
            if g >= 2:
                pe.wait_ge(s["P_exp"], g - 1)
            pe.matmul(ps[:, c % 2, :], m3["qT"][:, h, c * P:(c + 1) * P], m3["kT"][:, h, :], start=True, stop=True) \
              .then_inc(s["dots"], 1)

        def turn(h, c):
            if h >= 1:
                pe.wait_ge(*((s["PT_dve"], h) if c == 1 else (s["PT_act"], 3 * (h - 1) + max(c, 1))))
            pe.wait_ge(s["P_ready"], CH * h + c + 1)
            for k in range(CH):
                ins = pe.transpose(ps[:, 2 + c, k * P:(k + 1) * P],
                                   m3["PR"][:, h % 2, c * SEQ + k * P:c * SEQ + (k + 1) * P], ident[:, :])
            ins.then_inc(s["turned"], 1)

        pe.wait_ge(s["q_ready"], HEADS)
        pe.wait_ge(s["k_ready"], HEADS)
        pe.wait_ge(s["kpe_ready"], HEADS)
        pe.wait_ge(s["v_ready"], CH)
        for c in range(CH):
            dots(0, c)
        dots(1, 0)
        turned = m3["PT"][:, :].rearrange("p (c k n) -> p c k n", c=CH, k=CH)
        for h in range(HEADS):
            for c in range(CH):
                turn(h, c)
                nh, nc_ = (h + 1, c + 1) if c + 1 < CH else (h + 2, 0)
                if nh < HEADS:
                    dots(nh, nc_)
            m = h // 2
            if h % 2 == 0 and m >= 2:
                pe.wait_ge(s["o_split"], m - 1)
            pe.wait_ge(s["PT_dve"], h + 1)
            pe.wait_ge(s["PT_act"], 3 * h + 3)
            for k in range(CH):
                ins = pe.matmul(ps[64 * (h % 2):64 * (h % 2) + 64, 6 + m % 2, :], m3["vm"][:, k, h * V_DIM:(h + 1) * V_DIM],
                                turned[:, :, k, :], start=k == 0, stop=k == CH - 1)
            ins.then_inc(s["o_done"], 1)

    def prog_tensor(pe):
        pe.wait_ge(init["ident"], 16)
        pe.wait_ge(init["gains"], 16)
        pe.wait_ge(init["eps"], 2)
        pe.transpose(ps[0:16, 6, 0:16], ident[0:16, 0:16], ident[0:16, 0:16]).then_inc(unit_done, STARTED)
        pe.transpose(ps[:, 5, 0:NGAINS], vrows[0:NGAINS, :], ident[0:NGAINS, 0:NGAINS]).then_inc(init["turned"], 1)
        pe.wait_ge(init["meta"], 16)
        for k in range(KD):
            ins = pe.transpose(ps[:, 4, k * META:(k + 1) * META], meta_tok[:, k * P:(k + 1) * P], ident[0:META, 0:META])
        ins.then_inc(init["turned"], 1)
        for c in range(CH):
            pe.wait_ge(init[f"x{c}"], 16)
        for k in range(KD):
            if k >= 4:
                pe.wait_ge(init["h_ready"], k - 2)
            for c in range(CH):
                ins = pe.transpose(ps[:, k % 4, c * P:(c + 1) * P], x_tok[:, c, k * P:(k + 1) * P], ident[:, :])
            ins.then_inc(init["turned"], 1)
        pe.wait_ge(init["vecs"], 16 * (len(VEC_ROWS) - 1))
        pe.transpose(ps[:, 5, 0:NVEC], vrows[:, :], ident[0:NVEC, 0:NVEC]).then_inc(init["turned"], 1)
        pe.wait_ge(init["const"], 32)
        pe_ffn(pe, 0, 0, N0)
        sum_out(pe, 0, TOK)
        spread(pe, R0)
        pe.wait_ge(r_s["ready"], r_at[R0]["ready"] + 2)
        pe_mlstm(pe)
        pe_out(pe, 1, U_M1 + 25, range(KD), lambda k: (a1["y_split"], k + 1))
        sum_out(pe, 1, SEQ)
        spread(pe, R1)
        pe.wait_ge(r_s["ready"], r_at[R1]["ready"] + 1)
        pe_ffn(pe, 1, 2, N2)
        sum_out(pe, 2, SEQ)
        spread(pe, R2)
        pe.wait_ge(r_s["ready"], r_at[R2]["ready"] + 1)
        pe_ffn(pe, 2, 3, N3)
        pe_mix2(pe)
        pe_mla(pe)
        pe_out(pe, 4, U_M2 + 23, [4, 5, 6, 7, 0, 1, 2, 3],
               lambda k: (a3["o_split"], k + 1) if k < 4 else (a2["r_split"], k - 3))
        pe_ffn(pe, 3, 5, N5, 4)
        sum_out(pe, 5, SEQ)
        for c in range(CH):
            for j in range(2):
                g = 2 * c + j
                if g >= 4:
                    pe.wait_ge(fin_s["kept_act"], g - 3)
                for k in range(4):
                    pe.wait_ge(fin_s["t_ready"], 4 * j + k + 1)
                    ins = pe.transpose(ps[:, g % 4, k * P:(k + 1) * P], fin["fin"][:, 4 * j + k, c * P:(c + 1) * P], ident[:, :])
                ins.then_inc(fin_s["turned"], 1)

    with ctx:
        block = ctx.enter_context(nc.Block())

        @block.sync
        def _(sp):
            prog_sync(sp)

        @block.gpsimd
        def _(pool):
            prog_gpsimd(pool)

        @block.scalar
        def _(act):
            prog_scalar(act)

        @block.vector
        def _(v):
            prog_vector(v)

        @block.tensor
        def _(pe):
            prog_tensor(pe)


_UNUSED = {"b_w_in", "b_f_bias", "b_lb_raw", "b_g_norm", "b_w_out"}


def kernel(**inputs):
    import concourse.bacc as _bacc
    from concourse.bass_utils import run_bass_kernel_spmd as _run

    nc = _bacc.Bacc("TRN2", target_bir_lowering=False, num_devices=1)
    arrays, dram = {}, {}
    for name, value in inputs.items():
        a = np.ascontiguousarray(value)
        if name in _UNUSED or a.size == 0:
            continue
        arrays[f"in_{name}"] = a
        dram[name] = nc.dram_tensor(f"in_{name}", a.shape, mybir.dt.from_np(a.dtype), kind="ExternalInput").ap()
    arrays["in_const"] = constants()
    dram["const"] = nc.dram_tensor("in_const", (P, NCONST), F32, kind="ExternalInput").ap()
    out = nc.dram_tensor("out_0", (1, SEQ, D), F32, kind="ExternalOutput").ap()
    program(nc, dram, out)
    r = _run(nc, [arrays], core_ids=[0])
    return r.results[0]["out_0"]
```
